# Optimizing a Trainium2 kernel written in Bass

```python
import math
import jax, jax.numpy as jnp
from jax import lax
import numpy as np

D_MODEL = 1024
BATCH = 1
SEQ = 256
DEPTH = 1

RET_HEADS = 4
RET_DK = 256
RET_DV = 512
RET_CHUNK = 128
RET_QK_W = RET_HEADS * RET_DK
RET_V_W = RET_HEADS * RET_DV
ATT_GROUPS = ((128, 1), (512, 4), (2048, 16))
N_ATT_GROUPS = len(ATT_GROUPS)
ATT_HEADS_PER_GROUP = 4
ATT_HEAD_DIM = 128
ATT_GROUP_W = ATT_HEADS_PER_GROUP * ATT_HEAD_DIM
N_ATT_HEADS = N_ATT_GROUPS * ATT_HEADS_PER_GROUP
REL_BUCKETS = 32
REL_MAX_DIST = 2048
D_FF = 4 * D_MODEL
N_BRANCHES = 2
RMS_EPS = 1e-6
GN_EPS = 1e-5
ROPE_BASE = 10000.0

IN_SIZES = ([RET_QK_W, RET_QK_W, RET_V_W, RET_V_W]
            + [ATT_GROUP_W] * (3 * N_ATT_GROUPS)
            + [D_MODEL] * N_BRANCHES)
IN_COLS = sum(IN_SIZES)
IN_OFFSETS = [sum(IN_SIZES[:i + 1]) for i in range(len(IN_SIZES) - 1)]


def rms_norm(x, g):
    xf = x.astype(jnp.float32)
    y = xf * lax.rsqrt(jnp.mean(xf * xf, axis=-1, keepdims=True) + RMS_EPS)
    return (y * g.astype(jnp.float32)).astype(x.dtype)

def modulate(h, shift, scale):
    return h * (1 + scale[:, None, :]) + shift[:, None, :]

def t5_bucket(dist):
    max_exact = REL_BUCKETS // 2
    d_f = jnp.maximum(dist, 1).astype(jnp.float32)
    large = max_exact + (jnp.log(d_f / max_exact) / math.log(REL_MAX_DIST / max_exact)
                         * (REL_BUCKETS - max_exact)).astype(jnp.int32)
    large = jnp.minimum(large, REL_BUCKETS - 1)
    return jnp.where(dist < max_exact, dist, large)

def rotary(x, pos):
    half = x.shape[-1] // 2
    inv = ROPE_BASE ** (-jnp.arange(half, dtype=jnp.float32) / half)
    ang = pos.astype(jnp.float32)[:, None] * inv[None, :]
    cos, sin = jnp.cos(ang).astype(x.dtype), jnp.sin(ang).astype(x.dtype)
    x1, x2 = x[..., :half], x[..., half:]
    return jnp.concatenate([x1 * cos - x2 * sin, x1 * sin + x2 * cos], axis=-1)

def retention(q, k, v):
    B, H, S, dk = q.shape
    dv = v.shape[-1]
    C = RET_CHUNK
    nc = S // C
    log_g = jnp.log1p(-(2.0 ** (-5.0 - jnp.arange(H, dtype=jnp.float32))))
    idx = jnp.arange(C, dtype=jnp.float32)
    rel = idx[:, None] - idx[None, :]
    inner_decay = jnp.where(rel >= 0, jnp.exp(log_g[:, None, None] * jnp.maximum(rel, 0.0)), 0.0)
    q_decay = jnp.exp(log_g[:, None] * (idx + 1.0))
    k_decay = jnp.exp(log_g[:, None] * (C - 1.0 - idx))
    chunk_decay = jnp.exp(log_g * C)

    def to_chunks(t):
        return jnp.moveaxis(t.astype(jnp.float32).reshape(B, H, nc, C, t.shape[-1]), 2, 0)

    qc, kc, vc = to_chunks(q), to_chunks(k), to_chunks(v)

    def step(state, inp):
        qi, ki, vi = inp
        s = jnp.einsum('bhid,bhjd->bhij', qi, ki) * inner_decay[None]
        o = (jnp.einsum('bhij,bhje->bhie', s, vi)
             + jnp.einsum('bhid,bhde->bhie', qi, state) * q_decay[None, :, :, None])
        state = (state * chunk_decay[None, :, None, None]
                 + jnp.einsum('bhjd,bhje->bhde', ki * k_decay[None, :, :, None], vi))
        return state, o

    state0 = jnp.zeros((B, H, dk, dv), jnp.float32)
    _, o = lax.scan(step, state0, (qc, kc, vc))
    return jnp.moveaxis(o, 0, 2).reshape(B, H, S, dv)

def dilated_group(q, k, v, bias_tab, window, dilation):
    B, H, S, dh = q.shape
    w = window // dilation
    blk = w
    span = dilation * blk
    Sp = -(-S // span) * span
    L = Sp // dilation
    nb = L // blk

    def split(t):
        t = jnp.pad(t, ((0, 0), (0, 0), (0, Sp - S), (0, 0)))
        t = t.reshape(B, H, L, dilation, dh).transpose(0, 1, 3, 2, 4)
        return t.reshape(B, H, dilation, nb, blk, dh)

    qs, ks, vs = split(q), split(k), split(v)

    def with_prev(t):
        prev = jnp.pad(t[:, :, :, :-1], ((0, 0), (0, 0), (0, 0), (1, 0), (0, 0), (0, 0)))
        return jnp.concatenate([prev, t], axis=4)

    kb, vb = with_prev(ks), with_prev(vs)
    qi = jnp.arange(blk)[:, None]
    kj = jnp.arange(2 * blk)[None, :]
    m = blk + qi - kj
    band = (m >= 0) & (m <= w)
    first_ok = kj >= blk
    valid = band[None] & ((jnp.arange(nb)[:, None, None] > 0) | first_ok[None])
    bias = bias_tab[t5_bucket(jnp.clip(m, 0, w) * dilation)]
    bias = jnp.moveaxis(bias, -1, 0).astype(jnp.float32)

    s = (jnp.einsum('bhrnid,bhrnjd->bhrnij', qs, kb).astype(jnp.float32) * (dh ** -0.5)
         + bias[None, :, None, None])
    s = jnp.where(valid[None, None, None], s, -1e30)
    mx = jnp.max(s, axis=-1, keepdims=True)
    e = jnp.exp(s - mx)
    den = jnp.sum(e, axis=-1, keepdims=True)
    p = (e / den).astype(v.dtype)
    lse = (mx + jnp.log(den))[..., 0]
    o = jnp.einsum('bhrnij,bhrnjd->bhrnid', p, vb)

    def merge(t):
        t = t.reshape(B, H, dilation, L, *t.shape[5:])
        t = jnp.swapaxes(t, 2, 3)
        t = t.reshape(B, H, Sp, *t.shape[4:])
        return t[:, :, :S]

    return merge(o), merge(lse)

def token_mixer(h, w_in, rel_bias, gn_g, gn_b, w_ret_out, w_att_out, w_o):
    B, S, _ = h.shape
    proj = h @ w_in
    parts = jnp.split(proj, IN_OFFSETS, axis=-1)

    def heads(t, n):
        return t.reshape(B, S, n, -1).transpose(0, 2, 1, 3)

    pos = jnp.arange(S)
    rq, rk, rv, rg = parts[0], parts[1], parts[2], parts[3]
    rq = rotary(heads(rq, RET_HEADS), pos)
    rk = rotary(heads(rk, RET_HEADS), pos) * (RET_DK ** -0.5)
    ro = retention(rq, rk, heads(rv, RET_HEADS))
    mu = jnp.mean(ro, axis=-1, keepdims=True)
    var = jnp.mean(jnp.square(ro - mu), axis=-1, keepdims=True)
    ro = ((ro - mu) * lax.rsqrt(var + GN_EPS)).transpose(0, 2, 1, 3).reshape(B, S, RET_V_W)
    ro = (ro * gn_g.astype(jnp.float32) + gn_b.astype(jnp.float32)).astype(h.dtype)
    ret_out = (jax.nn.silu(rg) * ro) @ w_ret_out

    outs, lses = [], []
    for gi, (win, dil) in enumerate(ATT_GROUPS):
        aq, ak, av = parts[4 + 3 * gi], parts[5 + 3 * gi], parts[6 + 3 * gi]
        tab = rel_bias[:, gi * ATT_HEADS_PER_GROUP:(gi + 1) * ATT_HEADS_PER_GROUP]
        o, lse = dilated_group(heads(aq, ATT_HEADS_PER_GROUP), heads(ak, ATT_HEADS_PER_GROUP),
                               heads(av, ATT_HEADS_PER_GROUP), tab, win, dil)
        outs.append(o)
        lses.append(lse)
    o_all = jnp.stack(outs, axis=0)
    wts = jax.nn.softmax(jnp.stack(lses, axis=0), axis=0)
    att = jnp.einsum('gbhs,gbhsd->bshd', wts.astype(o_all.dtype), o_all).reshape(B, S, ATT_GROUP_W)
    att_out = att @ w_att_out

    gate_a, gate_b = parts[-2], parts[-1]
    merged = jax.nn.sigmoid(gate_a) * ret_out + jax.nn.sigmoid(gate_b) * att_out
    return merged @ w_o

def squared_relu_mlp(h, w1, w2):
    return jnp.square(jax.nn.relu(h @ w1)) @ w2

def first_inputs(seed: int = 0) -> dict:
    key = jax.random.key(seed)
    ks = jax.random.split(key, 18)
    nrm = jax.random.normal
    f32 = jnp.float32
    return {
        "x": nrm(ks[0], (BATCH, SEQ, D_MODEL), f32),
        "c": nrm(ks[1], (BATCH, D_MODEL), f32),
        "w_ada": nrm(ks[2], (DEPTH, D_MODEL, 6 * D_MODEL), f32) * D_MODEL ** -0.5,
        "b_ada": nrm(ks[3], (DEPTH, 6 * D_MODEL), f32) * 0.02,
        "norm1_g": 1.0 + 0.02 * nrm(ks[4], (DEPTH, D_MODEL), f32),
        "w_in": nrm(ks[5], (DEPTH, D_MODEL, IN_COLS), f32) * D_MODEL ** -0.5,
        "rel_bias": nrm(ks[6], (REL_BUCKETS, N_ATT_HEADS), f32) * 0.5,
        "ret_gn_g": 1.0 + 0.02 * nrm(ks[7], (DEPTH, RET_V_W), f32),
        "ret_gn_b": 0.02 * nrm(ks[8], (DEPTH, RET_V_W), f32),
        "w_ret_out": nrm(ks[9], (DEPTH, RET_V_W, D_MODEL), f32) * RET_V_W ** -0.5,
        "w_att_out": nrm(ks[10], (DEPTH, ATT_GROUP_W, D_MODEL), f32) * ATT_GROUP_W ** -0.5,
        "w_o": nrm(ks[11], (DEPTH, D_MODEL, D_MODEL), f32) * D_MODEL ** -0.5,
        "norm2_g": 1.0 + 0.02 * nrm(ks[12], (DEPTH, D_MODEL), f32),
        "w_ff1": nrm(ks[13], (DEPTH, D_MODEL, D_FF), f32) * D_MODEL ** -0.5,
        "w_ff2": nrm(ks[14], (DEPTH, D_FF, D_MODEL), f32) * D_FF ** -0.5,
        "norm_f_g": 1.0 + 0.02 * nrm(ks[15], (D_MODEL,), f32),
    }

def first_block(x, c, w_ada, b_ada, norm1_g, w_in, rel_bias, ret_gn_g, ret_gn_b,
              w_ret_out, w_att_out, w_o, norm2_g, w_ff1, w_ff2, norm_f_g):
    for l in range(DEPTH):
        mod = jax.nn.silu(c) @ w_ada[l] + b_ada[l]
        sh1, sc1, g1, sh2, sc2, g2 = jnp.split(mod, 6, axis=-1)
        h = modulate(rms_norm(x, norm1_g[l]), sh1, sc1)
        x = x + g1[:, None, :] * token_mixer(h, w_in[l], rel_bias, ret_gn_g[l], ret_gn_b[l],
                                             w_ret_out[l], w_att_out[l], w_o[l])
        h = modulate(rms_norm(x, norm2_g[l]), sh2, sc2)
        x = x + g2[:, None, :] * squared_relu_mlp(h, w_ff1[l], w_ff2[l])
    return rms_norm(x, norm_f_g)


DEPTH_2 = 2

MLA_HEADS = 8
MLA_NOPE = 64
MLA_ROPE = 32
MLA_V = 64
MLA_Q_RANK = 256
MLA_KV_RANK = 128
Q_BLOCK = 128
POS_MAX_OFFSET = 4096

MLSTM_HEADS = 4
MLSTM_DH = 64
MLSTM_CHUNK = 64
M_INIT = -1e30

SSD_HEADS = 4
SSD_HEADDIM = 64
SSD_GROUPS = 2
SSD_HPG = SSD_HEADS // SSD_GROUPS
SSD_STATE = 128
SSD_CONV = 5
SSD_CHUNK = 128

MLA_OUT = MLA_HEADS * MLA_V
MLSTM_W = MLSTM_HEADS * MLSTM_DH
SSD_INNER = SSD_HEADS * SSD_HEADDIM
MIX_WIDTH = MLA_OUT + MLSTM_W + SSD_INNER
SSD_CONV_DIM = SSD_INNER + 2 * SSD_GROUPS * SSD_STATE
IN_SIZES_2 = (MLA_Q_RANK, MLA_KV_RANK, MLA_ROPE,
            MLSTM_W, MLSTM_W, MLSTM_W, MLSTM_W, 4 * MLSTM_HEADS,
            SSD_INNER, SSD_CONV_DIM, 2 * SSD_HEADS)
IN_WIDTH = sum(IN_SIZES_2)

N_GROUPS = 4
EXPERTS_PER_GROUP = 4
N_EXPERTS = N_GROUPS * EXPERTS_PER_GROUP
TOP_K = 2
D_EXPERT = 256

DEEPNORM_ALPHA = (2 * DEPTH_2) ** 0.25
DEEPNORM_BETA = (8 * DEPTH_2) ** -0.25


F32 = jnp.float32

def _split(t, sizes):
    out, off = [], 0
    for s in sizes:
        out.append(t[..., off:off + s])
        off += s
    return out

def _layernorm(x, g, b, eps=1e-5):
    xf = x.astype(F32)
    mu = jnp.mean(xf, -1, keepdims=True)
    var = jnp.mean(jnp.square(xf - mu), -1, keepdims=True)
    return (xf - mu) * lax.rsqrt(var + eps) * g + b

def _rmsnorm(x, g, eps=1e-6):
    xf = x.astype(F32)
    return xf * lax.rsqrt(jnp.mean(xf * xf, -1, keepdims=True) + eps) * g

def _rope_table(positions):
    inv = ROPE_BASE ** (-jnp.arange(0, MLA_ROPE, 2, dtype=F32) / MLA_ROPE)
    ang = positions.astype(F32)[..., None] * inv
    return jnp.cos(ang), jnp.sin(ang)

def _apply_rope(t, cos, sin):
    half = t.shape[-1] // 2
    t1, t2 = t[..., :half].astype(F32), t[..., half:].astype(F32)
    return jnp.concatenate([t1 * cos - t2 * sin, t2 * cos + t1 * sin], -1)

def _mla(c_q, c_kv, k_r, cos, sin, q_norm, kv_norm, w_uq, w_ukv):
    Bsz, S, _ = c_q.shape
    q = (_rmsnorm(c_q, q_norm).astype(c_q.dtype) @ w_uq).reshape(Bsz, S, MLA_HEADS, MLA_NOPE + MLA_ROPE)
    q_nope = q[..., :MLA_NOPE]
    q_rope = _apply_rope(q[..., MLA_NOPE:], cos[:, :, None], sin[:, :, None]).astype(q.dtype)
    kv = (_rmsnorm(c_kv, kv_norm).astype(c_kv.dtype) @ w_ukv).reshape(Bsz, S, MLA_HEADS, MLA_NOPE + MLA_V)
    k_nope, v = kv[..., :MLA_NOPE], kv[..., MLA_NOPE:]
    k_rope = _apply_rope(k_r, cos, sin).astype(k_r.dtype)
    scale = (MLA_NOPE + MLA_ROPE) ** -0.5
    nb = S // Q_BLOCK
    qn = q_nope.reshape(Bsz, nb, Q_BLOCK, MLA_HEADS, MLA_NOPE).transpose(1, 0, 2, 3, 4)
    qr = q_rope.reshape(Bsz, nb, Q_BLOCK, MLA_HEADS, MLA_ROPE).transpose(1, 0, 2, 3, 4)

    def block(args):
        qn_b, qr_b = args
        s = (jnp.einsum('bqhd,bkhd->bhqk', qn_b, k_nope)
             + jnp.einsum('bqhr,bkr->bhqk', qr_b, k_rope)).astype(F32) * scale
        p = jax.nn.softmax(s, axis=-1).astype(v.dtype)
        return jnp.einsum('bhqk,bkhd->bqhd', p, v)

    o = lax.map(block, (qn, qr))
    return o.transpose(1, 0, 2, 3, 4).reshape(Bsz, S, MLA_OUT)

def _mlstm_scan(q, k, v, ig, lf):
    Bsz, S, H, Dh = q.shape
    L = MLSTM_CHUNK
    nc = S // L

    def chunks(t):
        t = t.reshape((Bsz, nc, L, H) + t.shape[3:])
        return jnp.moveaxis(jnp.moveaxis(t, 1, 0), 3, 2)

    mask = jnp.tril(jnp.ones((L, L), bool))

    def step(carry, inp):
        C, n, m = carry
        qc, kc, vc, igc, lfc = inp
        b = jnp.cumsum(lfc, axis=-1)
        a = jnp.where(mask, b[..., :, None] - b[..., None, :] + igc[..., None, :], -jnp.inf)
        g = b + m[..., None]
        m_t = jnp.maximum(g, jnp.max(a, -1))
        w_intra = jnp.exp(a - m_t[..., None])
        w_inter = jnp.exp(g - m_t)
        qk = jnp.einsum('bhtd,bhsd->bhts', qc, kc).astype(F32) * w_intra
        num = (jnp.einsum('bhts,bhsd->bhtd', qk, vc)
               + w_inter[..., None] * jnp.einsum('bhtd,bhde->bhte', qc, C))
        den = jnp.sum(qk, -1) + w_inter * jnp.einsum('bhtd,bhd->bht', qc, n)
        h = num / jnp.maximum(jnp.abs(den), jnp.exp(-m_t))[..., None]
        bL = b[..., -1]
        dec = bL[..., None] - b + igc
        m_new = jnp.maximum(bL + m, jnp.max(dec, -1))
        w_s = jnp.exp(dec - m_new[..., None])
        w_c = jnp.exp(bL + m - m_new)
        C = w_c[..., None, None] * C + jnp.einsum('bhs,bhsd,bhse->bhde', w_s, kc, vc)
        n = w_c[..., None] * n + jnp.einsum('bhs,bhsd->bhd', w_s, kc)
        return (C, n, m_new), h

    init = (jnp.zeros((Bsz, H, Dh, Dh), F32), jnp.zeros((Bsz, H, Dh), F32),
            jnp.full((Bsz, H), M_INIT, F32))
    _, hs = lax.scan(step, init, (chunks(q), chunks(k), chunks(v), chunks(ig), chunks(lf)))
    hs = jnp.moveaxis(jnp.moveaxis(hs, 2, 3), 0, 1)
    return hs.reshape(Bsz, S, H, Dh)

def _mlstm(q, k, v, o, gates, gate_bias, norm_g):
    Bsz, S, _ = q.shape
    shp = (Bsz, S, MLSTM_HEADS, MLSTM_DH)
    q, k, v = q.reshape(shp), k.reshape(shp) * (MLSTM_DH ** -0.5), v.reshape(shp)
    gt = gates.reshape(Bsz, S, 4, MLSTM_HEADS).astype(F32) + gate_bias
    ig_f, lf_f = gt[:, :, 0], jax.nn.log_sigmoid(gt[:, :, 1])
    ig_b, lf_b = gt[:, :, 2], jax.nn.log_sigmoid(gt[:, :, 3])
    flip = lambda t: jnp.flip(t, axis=1)
    h = (_mlstm_scan(q, k, v, ig_f, lf_f)
         + flip(_mlstm_scan(flip(q), flip(k), flip(v), flip(ig_b), flip(lf_b))))
    mu = jnp.mean(h, -1, keepdims=True)
    var = jnp.mean(jnp.square(h - mu), -1, keepdims=True)
    hn = (h - mu) * lax.rsqrt(var + 1e-5) * norm_g.reshape(MLSTM_HEADS, MLSTM_DH)
    y = jax.nn.sigmoid(o.reshape(shp).astype(F32)) * hn
    return y.reshape(Bsz, S, MLSTM_W)

def _ssd_scan(x, dt, A, Bm, Cm):
    Bsz, S, G, E, P = x.shape
    N = Bm.shape[-1]
    L = SSD_CHUNK
    nc = S // L

    def chunks(t):
        return jnp.moveaxis(t.reshape((Bsz, nc, L) + t.shape[2:]), 1, 0)

    mask = jnp.tril(jnp.ones((L, L), bool))[None, :, :, None, None]

    def step(state, inp):
        xc, dtc, Bc, Cc = inp
        cs = jnp.cumsum(dtc * A, axis=1)
        Lm = jnp.exp(jnp.where(mask, cs[:, :, None] - cs[:, None, :], -jnp.inf))
        CB = jnp.einsum('btgn,bsgn->btsg', Cc, Bc)
        xdt = xc * dtc[..., None]
        y = jnp.einsum('btsg,btsge,bsgep->btgep', CB, Lm, xdt)
        y = y + jnp.einsum('btgn,bgepn->btgep', Cc, state) * jnp.exp(cs)[..., None]
        decay_end = jnp.exp(cs[:, -1:] - cs)
        state = (jnp.exp(cs[:, -1])[..., None, None] * state
                 + jnp.einsum('bsgn,bsge,bsgep->bgepn', Bc, decay_end, xdt))
        return state, y

    init = jnp.zeros((Bsz, G, E, P, N), F32)
    _, ys = lax.scan(step, init, (chunks(x), chunks(dt), chunks(Bm), chunks(Cm)))
    return jnp.moveaxis(ys, 0, 1).reshape(Bsz, S, G, E, P)

def _ssd(z, xbc, dt_raw, conv_w, conv_b, dt_bias, a_log, d_skip, norm_g):
    Bsz, S, Cdim = xbc.shape
    pad = SSD_CONV // 2
    xbc = lax.conv_general_dilated(xbc, conv_w[:, None, :], window_strides=(1,),
                                   padding=((pad, pad),), dimension_numbers=('NWC', 'WIO', 'NWC'),
                                   feature_group_count=Cdim) + conv_b
    xbc = jax.nn.silu(xbc)
    xs, Bm, Cm = _split(xbc, (SSD_INNER, SSD_GROUPS * SSD_STATE, SSD_GROUPS * SSD_STATE))
    x = xs.reshape(Bsz, S, SSD_GROUPS, SSD_HPG, SSD_HEADDIM)
    Bm = Bm.reshape(Bsz, S, SSD_GROUPS, SSD_STATE)
    Cm = Cm.reshape(Bsz, S, SSD_GROUPS, SSD_STATE)
    dt = jax.nn.softplus(dt_raw.reshape(Bsz, S, 2, SSD_GROUPS, SSD_HPG).astype(F32)
                         + dt_bias.reshape(2, SSD_GROUPS, SSD_HPG))
    A = -jnp.exp(a_log.astype(F32)).reshape(2, SSD_GROUPS, SSD_HPG)
    flip = lambda t: jnp.flip(t, axis=1)
    y = (_ssd_scan(x, dt[:, :, 0], A[0], Bm, Cm)
         + flip(_ssd_scan(flip(x), flip(dt[:, :, 1]), A[1], flip(Bm), flip(Cm)))
         + x * d_skip.reshape(SSD_GROUPS, SSD_HPG)[..., None])
    y = y.reshape(Bsz, S, SSD_INNER) * jax.nn.silu(z.astype(F32))
    y = _rmsnorm(y.reshape(Bsz, S, SSD_GROUPS, SSD_INNER // SSD_GROUPS),
                 norm_g.reshape(SSD_GROUPS, SSD_INNER // SSD_GROUPS))
    return y.reshape(Bsz, S, SSD_INNER)

def _hier_moe(x, wg, bg, we, be, w_gate, w_up, w_down):
    glog = (jnp.einsum('bsd,dg->bsg', x, wg) + bg).astype(F32)
    gp, gi = lax.top_k(jax.nn.softmax(glog, -1), 1)
    elog = (jnp.einsum('bsd,gde->bsge', x, we) + be).astype(F32)
    elog = jnp.einsum('bsge,bsg->bse', elog, jax.nn.one_hot(gi[..., 0], N_GROUPS, dtype=F32))
    ep, ei = lax.top_k(jax.nn.softmax(elog, -1), TOP_K)
    ep = ep / jnp.sum(ep, -1, keepdims=True)
    eid = gi * EXPERTS_PER_GROUP + ei
    combine = jnp.sum(jax.nn.one_hot(eid, N_EXPERTS, dtype=F32) * (gp * ep)[..., None], axis=2)
    h = jax.nn.silu(jnp.einsum('bsd,edf->bsef', x, w_gate)) * jnp.einsum('bsd,edf->bsef', x, w_up)
    h = h * combine[..., None].astype(h.dtype)
    return jnp.einsum('bsef,efd->bsd', h, w_down)

def second_inputs(seed: int = 0) -> dict:
    key = jax.random.key(seed)
    ks = jax.random.split(key, 32)
    nrm = lambda k, shape, s: jax.random.normal(k, shape, F32) * s
    gain = lambda k, shape: 1.0 + 0.02 * jax.random.normal(k, shape, F32)

    x = jax.random.normal(ks[0], (BATCH, SEQ, D_MODEL), F32)
    positions = (jax.random.randint(ks[1], (BATCH, 1), 0, POS_MAX_OFFSET, dtype=jnp.int32)
                 + jnp.arange(SEQ, dtype=jnp.int32)[None, :])

    w_in = nrm(ks[2], (DEPTH_2, D_MODEL, IN_WIDTH), D_MODEL ** -0.5)
    mla_q_norm = gain(ks[3], (DEPTH_2, MLA_Q_RANK))
    mla_kv_norm = gain(ks[4], (DEPTH_2, MLA_KV_RANK))
    mla_w_uq = nrm(ks[5], (DEPTH_2, MLA_Q_RANK, MLA_HEADS * (MLA_NOPE + MLA_ROPE)), MLA_Q_RANK ** -0.5)
    mla_w_ukv = nrm(ks[6], (DEPTH_2, MLA_KV_RANK, MLA_HEADS * (MLA_NOPE + MLA_V)), MLA_KV_RANK ** -0.5)

    lin = jnp.linspace(3.0, 6.0, MLSTM_HEADS, dtype=F32)
    zer = jnp.zeros((MLSTM_HEADS,), F32)
    mlstm_gate_bias = jnp.stack([zer, lin, zer, lin])[None] + nrm(ks[7], (DEPTH_2, 4, MLSTM_HEADS), 0.1)
    mlstm_norm = gain(ks[8], (DEPTH_2, MLSTM_W))

    ssd_conv_w = nrm(ks[9], (DEPTH_2, SSD_CONV, SSD_CONV_DIM), SSD_CONV ** -0.5)
    ssd_conv_b = nrm(ks[10], (DEPTH_2, SSD_CONV_DIM), 0.01)
    dt0 = jnp.exp(jax.random.uniform(ks[11], (DEPTH_2, 2, SSD_HEADS), F32, math.log(1e-3), math.log(1e-1)))
    ssd_dt_bias = dt0 + jnp.log(-jnp.expm1(-dt0))
    ssd_a_log = jnp.log(jax.random.uniform(ks[12], (DEPTH_2, 2, SSD_HEADS), F32, 1.0, 16.0))
    ssd_d = gain(ks[13], (DEPTH_2, SSD_HEADS))
    ssd_norm = gain(ks[14], (DEPTH_2, SSD_INNER))

    w_out = nrm(ks[15], (DEPTH_2, MIX_WIDTH, D_MODEL), MIX_WIDTH ** -0.5 * DEEPNORM_BETA)
    ln1_g = gain(ks[16], (DEPTH_2, D_MODEL))
    ln1_b = nrm(ks[17], (DEPTH_2, D_MODEL), 0.02)

    router_group_w = nrm(ks[18], (DEPTH_2, D_MODEL, N_GROUPS), D_MODEL ** -0.5)
    router_group_b = nrm(ks[19], (DEPTH_2, N_GROUPS), 0.01)
    router_expert_w = nrm(ks[20], (DEPTH_2, N_GROUPS, D_MODEL, EXPERTS_PER_GROUP), D_MODEL ** -0.5)
    router_expert_b = nrm(ks[21], (DEPTH_2, N_GROUPS, EXPERTS_PER_GROUP), 0.01)
    expert_w_gate = nrm(ks[22], (DEPTH_2, N_EXPERTS, D_MODEL, D_EXPERT), D_MODEL ** -0.5)
    expert_w_up = nrm(ks[23], (DEPTH_2, N_EXPERTS, D_MODEL, D_EXPERT), D_MODEL ** -0.5)
    expert_w_down = nrm(ks[24], (DEPTH_2, N_EXPERTS, D_EXPERT, D_MODEL), D_EXPERT ** -0.5 * DEEPNORM_BETA)
    ln2_g = gain(ks[25], (DEPTH_2, D_MODEL))
    ln2_b = nrm(ks[26], (DEPTH_2, D_MODEL), 0.02)

    return {"x": x, "positions": positions, "w_in": w_in,
            "mla_q_norm": mla_q_norm, "mla_kv_norm": mla_kv_norm,
            "mla_w_uq": mla_w_uq, "mla_w_ukv": mla_w_ukv,
            "mlstm_gate_bias": mlstm_gate_bias, "mlstm_norm": mlstm_norm,
            "ssd_conv_w": ssd_conv_w, "ssd_conv_b": ssd_conv_b, "ssd_dt_bias": ssd_dt_bias,
            "ssd_a_log": ssd_a_log, "ssd_d": ssd_d, "ssd_norm": ssd_norm,
            "w_out": w_out, "ln1_g": ln1_g, "ln1_b": ln1_b,
            "router_group_w": router_group_w, "router_group_b": router_group_b,
            "router_expert_w": router_expert_w, "router_expert_b": router_expert_b,
            "expert_w_gate": expert_w_gate, "expert_w_up": expert_w_up, "expert_w_down": expert_w_down,
            "ln2_g": ln2_g, "ln2_b": ln2_b}

def second_block(x, positions, w_in, mla_q_norm, mla_kv_norm, mla_w_uq, mla_w_ukv,
              mlstm_gate_bias, mlstm_norm, ssd_conv_w, ssd_conv_b, ssd_dt_bias,
              ssd_a_log, ssd_d, ssd_norm, w_out, ln1_g, ln1_b,
              router_group_w, router_group_b, router_expert_w, router_expert_b,
              expert_w_gate, expert_w_up, expert_w_down, ln2_g, ln2_b):
    dtype = x.dtype
    cos, sin = _rope_table(positions)
    for l in range(DEPTH_2):
        p = jnp.einsum('bsd,dc->bsc', x, w_in[l])
        (c_q, c_kv, k_r, m_q, m_k, m_v, m_o, m_g, s_z, s_xbc, s_dt) = _split(p, IN_SIZES_2)
        y_a = _mla(c_q, c_kv, k_r, cos, sin, mla_q_norm[l], mla_kv_norm[l], mla_w_uq[l], mla_w_ukv[l])
        y_b = _mlstm(m_q, m_k, m_v, m_o, m_g, mlstm_gate_bias[l], mlstm_norm[l])
        y_c = _ssd(s_z, s_xbc, s_dt, ssd_conv_w[l], ssd_conv_b[l], ssd_dt_bias[l],
                   ssd_a_log[l], ssd_d[l], ssd_norm[l])
        heads = jnp.concatenate([y_a.astype(dtype), y_b.astype(dtype), y_c.astype(dtype)], -1)
        mix = jnp.einsum('bsc,cd->bsd', heads, w_out[l])
        x = _layernorm(DEEPNORM_ALPHA * x + mix, ln1_g[l], ln1_b[l]).astype(dtype)
        ffn = _hier_moe(x, router_group_w[l], router_group_b[l], router_expert_w[l], router_expert_b[l],
                        expert_w_gate[l], expert_w_up[l], expert_w_down[l]).astype(dtype)
        x = _layernorm(DEEPNORM_ALPHA * x + ffn, ln2_g[l], ln2_b[l]).astype(dtype)
    return x


def setup_inputs(seed=0):
    out = dict(first_inputs(seed))
    for name, value in second_inputs(seed + 1).items():
        if name != "x":
            out[name + "_2"] = value
    return out


def reference(
    x, c, w_ada, b_ada, norm1_g, w_in, rel_bias, ret_gn_g, ret_gn_b, w_ret_out, w_att_out, w_o,
    norm2_g, w_ff1, w_ff2, norm_f_g, positions_2, w_in_2, mla_q_norm_2, mla_kv_norm_2,
    mla_w_uq_2, mla_w_ukv_2, mlstm_gate_bias_2, mlstm_norm_2, ssd_conv_w_2, ssd_conv_b_2,
    ssd_dt_bias_2, ssd_a_log_2, ssd_d_2, ssd_norm_2, w_out_2, ln1_g_2, ln1_b_2,
    router_group_w_2, router_group_b_2, router_expert_w_2, router_expert_b_2, expert_w_gate_2,
    expert_w_up_2, expert_w_down_2, ln2_g_2, ln2_b_2,
):
    x = first_block(
        x, c, w_ada, b_ada, norm1_g, w_in, rel_bias, ret_gn_g, ret_gn_b, w_ret_out, w_att_out,
        w_o, norm2_g, w_ff1, w_ff2, norm_f_g,
    )
    return second_block(
        x, positions_2, w_in_2, mla_q_norm_2, mla_kv_norm_2, mla_w_uq_2, mla_w_ukv_2,
        mlstm_gate_bias_2, mlstm_norm_2, ssd_conv_w_2, ssd_conv_b_2, ssd_dt_bias_2, ssd_a_log_2,
        ssd_d_2, ssd_norm_2, w_out_2, ln1_g_2, ln1_b_2, router_group_w_2, router_group_b_2,
        router_expert_w_2, router_expert_b_2, expert_w_gate_2, expert_w_up_2, expert_w_down_2,
        ln2_g_2, ln2_b_2,
    )


_drawn_inputs = setup_inputs


def setup_inputs(seed=0):
    import zlib

    import numpy as np

    out = dict(_drawn_inputs(seed))
    spreads = {}
    factors = {'norm1_g': 3.435,
     'ret_gn_g': 5.767,
     'ret_gn_b': 5.675,
     'norm2_g': 2.747,
     'mla_q_norm_2': 8.0,
     'mla_kv_norm_2': 8.0,
     'mlstm_norm_2': 8.0,
     'ssd_conv_b_2': 8.0,
     'ssd_d_2': 8.0,
     'ssd_norm_2': 6.902,
     'router_group_b_2': 8.0,
     'router_expert_b_2': 7.161}
    for name, (base, spread) in spreads.items():
        noise = np.random.default_rng([zlib.crc32(name.encode()), seed]).standard_normal(out[name].shape)
        drawn = base * np.exp(spread * noise) if base else spread * noise
        out[name] = __import__('jax').numpy.asarray(drawn.astype(out[name].dtype))
    for name, factor in factors.items():
        out[name] = (out[name] * factor).astype(out[name].dtype)
    return out
```

```python
from contextlib import ExitStack

import concourse.bass as bass
import numpy as np
from concourse import mybir

F32 = mybir.dt.float32
F32R = mybir.dt.float32r
I32 = mybir.dt.int32
ALU = mybir.AluOpType
ACT = mybir.ActivationFunctionType
AX = mybir.AxisListType

P = 128
S = 256
TOK = S // P
D = 1024
KC = D // P
NT = 512
RH, RDK, RDV = 4, 256, 512
GROUPS = ((128, 1), (512, 4), (2048, 16))
AH, ADH = 4, 128
N_AH = len(GROUPS) * AH
BUCKETS, MAX_DIST = 32, 2048
FF_TILES = 4096 // NT
LAYERS = 2
MH, NOPE, ROPE, MV = 8, 64, 32, 64
QD = NOPE + ROPE
LH, LDH = 4, 64
SH, SP_, SG, SN = 4, 64, 2, 128
CONV = 5
XBC = SH * SP_ + 2 * SG * SN
XBC_CH = XBC // P
EXPERTS, EGROUPS, EPG = 16, 4, 4
DE = 256
ALPHA = (2 * LAYERS) ** 0.25
NEG = -1e30

UNIT = 1024
SLOTS = 4
RAW = 8
PIECE = 2
UP = 4
N_ADA = 6 * D // NT
U_ADA = 0
U_RET_IN = U_ADA + N_ADA * UP
N_RET_IN = 12
U_RET_OUT = U_RET_IN + N_RET_IN * UP
U_ATT_IN = U_RET_OUT + RH * 4
N_ATT_IN = 9
U_GATE = U_ATT_IN + N_ATT_IN * UP
N_GATE = 4
U_ATT_OUT = U_GATE + N_GATE * UP
U_WO = U_ATT_OUT + 4
U_MLP = U_WO + 8
U_LAYERS = U_MLP + FF_TILES * 8
L_IN = 0
N_IN2 = 5
L_UQ = L_IN + N_IN2 * UP
L_UKV = L_UQ + 2
L_OUT = L_UKV + 1
L_ROUTER = L_OUT + 8
L_MOE = L_ROUTER + 1
L_UNITS = L_MOE + EXPERTS * 6
UNITS = U_LAYERS + LAYERS * L_UNITS
assert UNITS % RAW == 0 and L_UNITS % RAW == 0 and U_LAYERS % RAW == 0

M_RET_IN = N_ADA
M_ATT_IN = M_RET_IN + N_RET_IN
M_GATE = M_ATT_IN + N_ATT_IN
M_MLP = M_GATE + N_GATE
M_LAYERS = M_MLP
LM_ROUTER = N_IN2
LM = LM_ROUTER + 1
T_H1 = 0
T_RET = T_H1 + 4
T_ATT = T_RET + 2 * RH
T_MERGE = T_ATT + 2
T_H2 = T_MERGE + 4
T_MLP = T_H2 + 4
T_LAYERS = T_MLP + 2 * FF_TILES
LT_X = 0
LT_MLA = LT_X + 4
LT_OUT = LT_MLA + 2
LT_X2 = LT_OUT + 4
LT_MOE = LT_X2 + 4
LT = LT_MOE + 2 * EXPERTS
R_LAYERS = 4
LR = 5
C_LAYERS = 4
LC = 2
G_CREDIT = 2

ROW2 = {}
_at = 0
for _n, _w in (("ln1_g", D), ("ln1_b", D), ("ln2_g", D), ("ln2_b", D), ("q_norm", 256), ("kv_norm", 128),
               ("gate_bias", 24), ("a_log", 8), ("d_skip", 4), ("ssd_norm", 256), ("mlstm_norm", 256),
               ("router_b", 20)):
    ROW2[_n] = (_at, _at + _w)
    _at += _w
ROWS2 = _at

IN2 = {"cq": 0, "ckv": 256, "kr": 384, "mg": 416, "dt": 432, "mq": 512, "mk": 768, "mv": 1024, "mo": 1280,
       "xbc": 1536, "z": 2304}


def program(nc, A):
    ctx = ExitStack()
    with ctx:
        def sb(name, shape, dt=F32):
            return ctx.enter_context(nc.sbuf_tensor(name, shape, dt))

        def pb(name, shape):
            return ctx.enter_context(nc.psum_tensor(name, shape, F32))

        def sem(name):
            return ctx.enter_context(nc.semaphore(name))

        w_raw = sb("w_raw", [P, RAW, UNIT])
        w_hi = sb("w_hi", [P, SLOTS, UNIT], F32R)
        w_lo = sb("w_lo", [P, SLOTS, UNIT], F32R)
        xT_hi = sb("xT_hi", [P, KC, S], F32R)
        xT_lo = sb("xT_lo", [P, KC, S], F32R)
        yT_hi = sb("yT_hi", [P, 4, S], F32R)
        yT_lo = sb("yT_lo", [P, 4, S], F32R)
        zero_r = sb("zero_r", [1, P], F32R)
        x_sb = sb("x_sb", [P, TOK, D])
        mod = sb("mod", [P, 6 * D])
        ident = sb("ident", [P, P])
        arena = sb("arena", [P, 20480])
        scr = sb("scr", [P, 2, 384])
        sm = sb("sm", [P, 896])
        pos_i = sb("pos_i", [P, TOK], I32)
        G = pb("G", [P, 2, NT])
        AC = pb("AC", [P, 4, NT])
        T = pb("T", [P, 2, NT])
        AC_tok = AC[:, :, :].rearrange("p (t c) n -> p t (c n)", t=TOK)

        c_loaded = sem("c_loaded")
        x_loaded = sem("x_loaded")
        bias_in_loaded = sem("bias_in_loaded")
        ada_b_loaded = sem("ada_b_loaded")
        raw_landed = [sem("raw_landed%d" % s) for s in range(RAW // PIECE)]
        cst_loaded = sem("cst_loaded")
        norm1_loaded = sem("norm1_loaded")
        pos_loaded = sem("pos_loaded")
        lo_ready = sem("lo_ready")
        x_ready = sem("x_ready")
        out_stored = sem("out_stored")
        hi_ready = sem("hi_ready")
        unit_used = sem("unit_used")
        t_ready = sem("t_ready")
        t_hi = sem("t_hi")
        var_ready = sem("var_ready")
        std_ready = sem("std_ready")
        sumsq_ready = sem("sumsq_ready")
        act_out = sem("act_out")
        c_hi = sem("c_hi")
        bias_rows_out = sem("bias_rows_out")
        bias_stored = sem("bias_stored")
        h_ready = sem("h_ready")
        gn_g_loaded = sem("gn_g_loaded")
        g_free = sem("g_free")
        rg_gated = sem("rg_gated")
        rqk_ready = sem("rqk_ready")
        rqk_out = sem("rqk_out")
        rope_done = sem("rope_done")
        gn_b_loaded = sem("gn_b_loaded")
        ro_ready = sem("ro_ready")
        ro_out = sem("ro_out")
        y_ready = sem("y_ready")
        rel_loaded = [sem("rel_loaded%d" % g) for g in range(len(GROUPS))]
        ao_ready = sem("ao_ready")
        ao_out = sem("ao_out")
        aqk_ready = sem("aqk_ready")
        aqk_out = sem("aqk_out")
        as_out = sem("as_out")
        aeT_ready = sem("aeT_ready")
        ae_ready = sem("ae_ready")
        lse_diff = sem("lse_diff")
        lse_exp = sem("lse_exp")
        norm2_loaded = sem("norm2_loaded")
        normf_loaded = sem("normf_loaded")
        x1_ready = sem("x1_ready")
        ang_ready = sem("ang_ready")
        trig_ready = sem("trig_ready")
        cst2_loaded = sem("cst2_loaded")
        rows_loaded = sem("rows_loaded")
        mla_sumsq = sem("mla_sumsq")
        sp_in = sem("sp_in")
        sp_exp = sem("sp_exp")
        kv_out = sem("kv_out")
        mqkT_ready = sem("mqkT_ready")
        mqkT_out = sem("mqkT_out")
        mmax_ready = sem("mmax_ready")
        meT_ready = sem("meT_ready")
        me_ready = sem("me_ready")
        rows_T = sem("rows_T")
        rows_out = sem("rows_out")
        lqk_T = sem("lqk_T")
        lqk_out = sem("lqk_out")
        lmax_ready = sem("lmax_ready")
        lexp_ready = sem("lexp_ready")
        lgate = sem("lgate")
        lpT_ready = sem("lpT_ready")
        lnum_ready = sem("lnum_ready")
        lpT_out = sem("lpT_out")
        sx_T = sem("sx_T")
        sx_out = sem("sx_out")
        conv_done = sem("conv_done")
        conv_act = sem("conv_act")
        srow_out = sem("srow_out")
        sexp_ready = sem("sexp_ready")
        gexp_in = sem("gexp_in")
        gexp_out = sem("gexp_out")
        t_lo = sem("t_lo")
        ffn_h = sem("ffn_h")
        tab_wide = sem("tab_wide")
        bias_row = sem("bias_row")
        c_lo = sem("c_lo")
        rs_out = sem("rs_out")
        rs_ready = sem("rs_ready")
        acc_free = sem("acc_free")
        as_ready = sem("as_ready")
        aeT_out = sem("aeT_out")
        att_ready = sem("att_ready")
        merged_ready = sem("merged_ready")
        zero_ready = sem("zero_ready")
        cq_ready = sem("cq_ready")
        cum_in = sem("cum_in")
        cum_ready = sem("cum_ready")
        q_ready = sem("q_ready")
        ms_ready = sem("ms_ready")
        meT_out = sem("meT_out")
        mo_out = sem("mo_out")
        mo_ready = sem("mo_ready")
        rows_w = sem("rows_w")
        lrow_out = sem("lrow_out")
        lrow_ready = sem("lrow_ready")
        lqk_ready = sem("lqk_ready")
        lp_ready = sem("lp_ready")
        sxt_T = sem("sxt_T")
        scb_ready = sem("scb_ready")
        srow_ready = sem("srow_ready")
        sw_ready = sem("sw_ready")
        sy_ready = sem("sy_ready")
        sy_out = sem("sy_out")
        heads_ready = sem("heads_ready")
        x2_ready = sem("x2_ready")
        kv_ready = sem("kv_ready")

        def slot(j, n=1):
            return arena[:, j * 1024:(j + n) * 1024].rearrange("p (j t n) -> p j t n", j=n, t=TOK)

        def tile(j):
            return arena[:, j * 1024:(j + 1) * 1024].rearrange("p (t n) -> p t n", t=TOK)

        qkT = arena[:, 12288:16384].rearrange("p (c s) -> p c s", s=S)
        W = arena[:, 16384:18432]
        decay = arena[:, 18432:19968].rearrange("p (h n) -> p h n", h=RH)
        cosR = arena[:, 19968:20224].rearrange("p (t n) -> p t n", t=TOK)
        sinR = arena[:, 20224:20480].rearrange("p (t n) -> p t n", t=TOK)
        onehot = arena[0:BUCKETS + 1, 0:1536].rearrange("p (g n) -> p g n", g=len(GROUPS))
        tab_bc = arena[0:BUCKETS + 1, 1536:3072].rearrange("p (h n) -> p h n", h=N_AH)
        tab = sm[0:BUCKETS + 1, 480:480 + N_AH]
        bias_vec = arena[:, 6144:12288].rearrange("p (h n) -> p h n", h=N_AH)
        h_sb = arena[:, 3072:5120].rearrange("p (t n) -> p t n", t=TOK)
        ccol, csil = sm[:, 0:8], sm[:, 8:16]
        aqkT = [qkT[:, 8 * b:8 * b + 8, :] for b in range(2)]
        rel = [W[:, 0:1536], mod[:, 0:1536], arena[:, 18432:19968]]
        rel = [r.rearrange("p (h n) -> p h n", h=AH) for r in rel]
        a_e = arena[:, 9 * 1024:9 * 1024 + 768].rearrange("p (b n) -> p b n", b=2)
        a_eT = [W[:, 1536:1920], mod[:, 1536:1920]]
        amx, anm, aden = sm[:, 64:88], sm[:, 88:112], sm[:, 112:136]
        aM, adiff, afac, aD = sm[:, 136:144], sm[:, 144:168], sm[:, 168:192], sm[:, 192:200]

        P2 = arena[:, 0:5120].rearrange("p (t n) -> p t n", t=TOK)
        HB = arena[:, 5120:7168].rearrange("p (t n) -> p t n", t=TOK)
        WK = 7168
        tri_f, tri_b, ones = arena[:, 17024:17152], arena[:, 17152:17280], arena[:, 17280:17408]
        mask_f = arena[:, 17408:17920].rearrange("p (t n) -> p t n", t=TOK)
        mask_b = arena[:, 17920:18432].rearrange("p (t n) -> p t n", t=TOK)
        sel = arena[0:16, 18432:20480].rearrange("p (c n) -> p c n", c=16)
        row2 = {n: mod[:, a:b] for n, (a, b) in ROW2.items()}
        V2 = mod[:, ROWS2 + 8:ROWS2 + 8 + 1024].rearrange("p (t n) -> p t n", t=TOK)
        cvw = sm[:, 400:436]
        cv_w, cv_b = cvw[:, 0:30].rearrange("p (c k) -> p c k", k=CONV), cvw[:, 30:36]
        inv_row = sm[:, 436:452]
        cosM = sm[:, 368:400].rearrange("p (t n) -> p t n", t=TOK)
        sinM = sm[:, 860:892].rearrange("p (t n) -> p t n", t=TOK)

        Q = arena[:, WK:WK + 1536].rearrange("p (t n) -> p t n", t=TOK)
        KF = arena[:, WK + 1536:WK + 3072].rearrange("p (t n) -> p t n", t=TOK)
        mqT = arena[:, WK + 3072:WK + 5120].rearrange("p (h s) -> p h s", s=S)
        mkT = arena[:, WK + 5120:WK + 7168].rearrange("p (h s) -> p h s", s=S)
        me = arena[:, WK + 7168:WK + 8192].rearrange("p (b t s) -> p b t s", b=2, t=TOK)
        meT = arena[:, WK + 8192:WK + 9216].rearrange("p (b n) -> p b n", b=2)
        mmax, mnm, mden, mrden = sm[:, 64:80], sm[:, 80:96], sm[:, 96:112], sm[:, 112:128]
        lw = arena[:, WK:WK + 4096].rearrange("p (j t s) -> p j t s", j=2 * LH, t=TOK)
        lqkT = arena[:, WK + 4096:WK + 5120].rearrange("p (c s) -> p c s", s=S)
        lpT = arena[:, WK + 5120:WK + 6144].rearrange("p (b n) -> p b n", b=2)
        cen = arena[:, WK + 6400:WK + 6912]
        csq = arena[:, WK + 6912:WK + 7424]
        rowT = arena[0:16, WK + 9240:WK + 9496]
        lMx, lnm, lfloor, lden = sm[:, 128:144], sm[:, 144:160], sm[:, 160:176], sm[:, 176:192]
        xpad = arena[:, WK:WK + 1560].rearrange("p (c s) -> p c s", c=XBC_CH)
        xc = arena[:, WK + 1560:WK + 3096].rearrange("p (c s) -> p c s", c=XBC_CH)
        XT = arena[:, WK + 3096:WK + 3608].rearrange("p (t n) -> p t n", t=TOK)
        xdt = arena[:, WK + 3608:WK + 4632].rearrange("p (t d n) -> p t d n", t=TOK, d=2)
        sw = arena[:, WK + 4632:WK + 8728].rearrange("p (j t s) -> p j t s", j=2 * SH, t=TOK)
        ys = arena[:, WK:WK + 512].rearrange("p (t n) -> p t n", t=TOK)
        ysq = arena[:, WK + 512:WK + 1024].rearrange("p (t n) -> p t n", t=TOK)
        ffn_a = arena[:, WK:WK + 512].rearrange("p (t n) -> p t n", t=TOK)
        moe_h = arena[:, WK + 512:WK + 1024].rearrange("p (t n) -> p t n", t=TOK)
        bst = sm[:, 208:304].rearrange("p (k n) -> p k n", n=6)
        mv = sm[:, 304:336].rearrange("p (k n) -> p k n", n=2)
        comb = sm[:, 336:368]
        lsum = sm[:, 72:80]
        wt4 = sm[:, 496:500]
        GT = sm[:, 500:548].rearrange("p (t n) -> p t n", t=TOK)
        SI = sm[:, 548:580].rearrange("p (t n) -> p t n", t=TOK)
        sp_e = sm[:, 580:612].rearrange("p (t n) -> p t n", t=TOK)
        z_sp = sm[:, 612:644].rearrange("p (t n) -> p t n", t=TOK)
        w_sp = sm[:, 644:676].rearrange("p (t n) -> p t n", t=TOK)
        q_sp = sm[:, 676:708].rearrange("p (t n) -> p t n", t=TOK)
        SP = sm[:, 708:740].rearrange("p (t n) -> p t n", t=TOK)
        ea = sm[:, 740:748]
        cu = sm[:, 748:780].rearrange("p (t n) -> p t n", t=TOK)
        cs = sm[:, 780:812].rearrange("p (t n) -> p t n", t=TOK)
        rw = sm[:, 812:844].rearrange("p (t n) -> p t n", t=TOK)
        ncs = sm[:, 844:860]
        rt_e = sm[:, 64:74].rearrange("p (t n) -> p t n", t=TOK)
        rlog = sm[:, 612:652].rearrange("p (t n) -> p t n", t=TOK)
        r_m = sm[:, 652:656].rearrange("p (t n) -> p t n", t=TOK)
        r_g, r_1, r_2 = [sm[:, a:a + 8].rearrange("p (t n) -> p t n", t=TOK) for a in (656, 664, 672)]
        r_el = sm[:, 680:688].rearrange("p (t n) -> p t n", t=TOK)
        r_pr = sm[:, 688:720].rearrange("p (t g e) -> p t g e", t=TOK, g=EGROUPS)
        r_w = sm[:, 720:728].rearrange("p (t n) -> p t n", t=TOK)
        r_el2 = sm[:, 728:736].rearrange("p (t n) -> p t n", t=TOK)

        block = ctx.enter_context(nc.Block())

        def done(n):
            return n + SLOTS

        @block.sync
        def _(sp):
            sp.dma_start(ccol, A["c_col"]).then_inc(c_loaded, 16)
            sp.dma_start(x_sb[:, :, :], A["x"].rearrange("b (t p) d -> p (b t) d", p=P)).then_inc(x_loaded, 16)
            sp.dma_start(onehot, A["onehot"]).then_inc(bias_in_loaded, 16)
            sp.dma_start(tab[0:BUCKETS, :], A["rel_bias"]).then_inc(bias_in_loaded, 16)
            sp.dma_start(mod[:, :], A["b_ada"].partition_broadcast(P)).then_inc(ada_b_loaded, 16)

            def piece(src, s):
                sp.dma_start(w_raw[:, s * PIECE:(s + 1) * PIECE, :].rearrange("p u n -> p (u n)"), src)\
                  .then_inc(raw_landed[s], 16)

            n_ring = RAW // PIECE
            stream = A["w_stream"]
            for s in range(n_ring):
                piece(stream[s], s)
            sp.dma_start(ident[:, :], A["identity"]).then_inc(cst_loaded, 16)
            sp.dma_start(arena[:, 18432:20480], A["const1"]).then_inc(cst_loaded, 16)
            sp.dma_start(W[:, 0:D], A["norm1_g"].partition_broadcast(P)).then_inc(norm1_loaded, 16)
            sp.dma_start(inv_row, A["inv_freq"].partition_broadcast(P)).then_inc(pos_loaded, 16)
            sp.dma_start(pos_i[:, :], A["pos_col"]).then_inc(pos_loaded, 16)
            with sp.Fori(1, UNITS // RAW) as i:
                for s in range(n_ring):
                    sp.wait_ge(lo_ready, i * RAW + PIECE * (s + 1) - RAW)
                    piece(stream[bass.ds(i * n_ring + s, 1), :, :].rearrange("o p n -> p (o n)"), s)
            sp.wait_ge(x_ready, 1 + LAYERS)
            sp.dma_start(A["out"].rearrange("b (t p) d -> p (b t) d", p=P), x_sb[:, :, :]).then_inc(out_stored, 16)
            sp.wait_ge(out_stored, 16)

        @block.gpsimd
        def _(pool):
            with pool.Fori(0, UNITS // RAW) as i:
                for s in range(RAW):
                    pool.wait_ge(hi_ready, i * RAW + s + 1)
                    pool.tensor_tensor(w_lo[:, s % SLOTS, :], w_raw[:, s, :],
                                       w_hi[:, s % SLOTS, :].bitcast(F32), ALU.subtract).then_inc(lo_ready, 1)
        @block.scalar
        def _(act):
            def hi(n, k):
                act.wait_ge(raw_landed[k % RAW // PIECE], n * (16 // RAW) + (k // RAW + 1) * 16)
                act.wait_ge(unit_used, n + k + 1)
                act.activation(w_hi[:, k % SLOTS, :], w_raw[:, k % RAW, :], ACT.Copy).then_inc(hi_ready, 1)

            def his(a, b, n=0):
                for k in range(a, b):
                    hi(n, k)

            def turn_hi(n, dst, c0, nch, free=None):
                for t in range(TOK):
                    act.wait_ge(t_ready, n + t + 1)
                    if free is not None and t == 0:
                        act.wait_ge(unit_used, free)
                    act.activation(dst[:, c0:c0 + nch, t * P:(t + 1) * P],
                                   T[:, t, 0:nch * P].rearrange("p (c n) -> p c n", n=P), ACT.Copy).then_inc(t_hi, 1)

            def root(n, ap):
                act.wait_ge(var_ready, n + 1)
                act.activation(ap, ap, ACT.Sqrt).then_inc(std_ready, 1)

            def sumsq(n):
                for t in range(TOK):
                    i = act.activation(h_sb[:, t, :], x_sb[:, t, :], ACT.Square, accum_out=sm[:, 16 + t:17 + t])
                i.then_inc(sumsq_ready, 1)

            def activate(kind, n_done, t=None):
                act.wait_ge(unit_used, n_done)
                if kind == "mlp":
                    act.activation(tile(0), G[:, :, :], ACT.Relu).then_inc(act_out, 1)
                else:
                    act.activation(ffn_a, G[:, :, 0:DE], ACT.Silu).then_inc(act_out, 1)

            def ffn_step(kind, e, last, n, k, t, ndown):
                turn_hi(t, yT_hi, 0, ndown)
                if e == last:
                    return
                ahead = ndown + UP if e < last - 1 else 2 * ndown
                for j in range(ahead):
                    if j == UP:
                        activate(kind, done(n + k))
                    hi(n, k + j)
                if ahead <= UP:
                    activate(kind, done(n + k))

            act.wait_ge(c_loaded, 16)
            act.activation(csil, ccol, ACT.Silu)
            act.drain()
            act.activation(xT_hi[:, :, 0:P], csil.unsqueeze(2).to_broadcast([P, KC, P]), ACT.Copy).then_inc(c_hi, 1)
            his(0, RAW)
            act.wait_ge(x_loaded, 16)
            act.wait_ge(bias_rows_out, N_AH)
            act.dma_start(A["rel_scratch"][:, 0:P, :].rearrange("h p n -> p h n"), bias_vec).then_inc(bias_stored, 16)
            sumsq(0)
            with act.Fori(1, U_RET_IN // RAW) as i:
                his(0, RAW, i * RAW)
            his(U_RET_IN, U_RET_IN + SLOTS)
            root(0, sm[:, 16:18])
            turn_hi(T_H1, xT_hi, 0, 4)
            turn_hi(T_H1 + 2, xT_hi, 4, 4)
            his(U_RET_IN + SLOTS, U_RET_IN + RAW)
            with act.Fori(U_RET_IN // RAW + 1, U_RET_OUT // RAW) as i:
                his(0, RAW, i * RAW)
            his(U_RET_OUT, U_RET_OUT + SLOTS)
            act.wait_ge(h_ready, 1)
            act.dma_start(mod[:, 0:2048], A["gn_g"].partition_broadcast(P)).then_inc(gn_g_loaded, 16)
            act.wait_ge(g_free, G_CREDIT + M_ATT_IN)
            act.activation(arena[:, 8192:12288], arena[:, 8192:12288], ACT.Silu).then_inc(rg_gated, 1)
            for n in range(8):
                tk, s4 = n // 4, n % 4
                act.wait_ge(rqk_ready, n + 1)
                act.activation(qkT[:, 4 * s4:4 * s4 + 4, tk * P:(tk + 1) * P],
                               T[:, n % 2, :].rearrange("p (c n) -> p c n", n=P), ACT.Copy).then_inc(rqk_out, 1)
            act.wait_ge(rope_done, TOK)
            act.dma_start(W, A["gn_b"].partition_broadcast(P)).then_inc(gn_b_loaded, 16)
            for h in range(RH):
                act.wait_ge(ro_ready, h + 1)
                act.activation(tile(h), (G if h % 2 == 0 else AC)[:, 0:2, :], ACT.Copy).then_inc(ro_out, 1)
            root(1, sm[:, 32:40])
            for h in range(RH):
                turn_hi(T_RET + 2 * h, yT_hi, 0, 4, done(U_RET_OUT + 4 * h))
                his(U_RET_OUT + 4 * h + SLOTS, U_RET_OUT + 4 * h + SLOTS + 4)
            act.wait_ge(y_ready, RH)
            act.wait_ge(bias_stored, 16)
            for g in range(len(GROUPS)):
                flat = A["rel_scratch"].rearrange("h p n -> h (p n)")[g * AH:(g + 1) * AH, :]
                for t, (c0, n) in enumerate(((0, P), (P, S))):
                    a = S - 1 - t * P
                    src = flat[:, a:a + P * (2 * S - 1)].rearrange("h (p n) -> p h n", n=2 * S - 1)[:, :, 0:n]
                    act.dma_start(rel[g][:, :, c0:c0 + n], src).then_inc(rel_loaded[g], 16)
            his(U_ATT_IN + SLOTS, U_ATT_IN + RAW)
            with act.Fori(U_ATT_IN // RAW + 1, U_ATT_IN // RAW + 4) as i:
                his(0, RAW, i * RAW)
            his(U_ATT_IN + 32, U_GATE + SLOTS)
            def att_out(k):
                g, h = k // AH, k % AH
                act.wait_ge(ao_ready, k + 1)
                act.activation(tile(3 * g)[:, :, h * ADH:(h + 1) * ADH],
                               AC[:, k % 2, 0:256].rearrange("p (t n) -> p t n", t=TOK), ACT.Copy).then_inc(ao_out, 1)

            for k in range(N_AH):
                if k % AH == 0:
                    for n in range(4):
                        tk, qk = n // 2, n % 2
                        act.wait_ge(aqk_ready, k + n + 1)
                        act.activation(aqkT[k // AH % 2][:, 4 * qk:4 * qk + 4, tk * P:(tk + 1) * P],
                                       T[:, n % 2, :].rearrange("p (c n) -> p c n", n=P), ACT.Copy).then_inc(aqk_out, 1)
                act.wait_ge(as_out, k + 1)
                if k >= 2:
                    act.wait_ge(aeT_ready, k - 1)
                act.activation(a_e[:, k % 2, 0:P], scr[:, k % 2, 0:P], ACT.Exp, bias=anm[:, 2 * k:2 * k + 1],
                               accum_out=aden[:, 2 * k:2 * k + 1])
                act.activation(a_e[:, k % 2, P:384], scr[:, k % 2, P:384], ACT.Exp, bias=anm[:, 2 * k + 1:2 * k + 2],
                               accum_out=aden[:, 2 * k + 1:2 * k + 2]).then_inc(ae_ready, 1)
                if k >= 2:
                    att_out(k - 2)
            att_out(N_AH - 2)
            att_out(N_AH - 1)
            act.wait_ge(lse_diff, 1)
            act.activation(afac, adiff, ACT.Exp).then_inc(lse_exp, 1)
            for j, s in enumerate((1, 2, 4, 5)):
                his(U_GATE + 4 * j + SLOTS, U_GATE + 4 * j + 4 + SLOTS)
                act.wait_ge(unit_used, done(U_GATE + 4 * j + 4))
                act.activation(tile(s), (G if j % 2 == 0 else AC)[:, 0:2, :], ACT.Sigmoid).then_inc(g_free, 1)
            turn_hi(T_ATT, yT_hi, 0, 4)
            his(U_WO, U_WO + 4)
            for n in range(2):
                turn_hi(T_MERGE + 2 * n, yT_hi, 0, 4, done(U_WO + 4 * n))
                his(U_WO + 4 * n + 4, U_WO + 4 * n + 8)
            act.dma_start(W[:, 0:D], A["norm2_g"].partition_broadcast(P)).then_inc(norm2_loaded, 16)
            act.dma_start(W[:, D:2 * D], A["norm_f_g"].partition_broadcast(P)).then_inc(normf_loaded, 16)
            act.wait_ge(x1_ready, 1)
            sumsq(1)
            root(2, sm[:, 16:18])
            turn_hi(T_H2, xT_hi, 0, 4)
            turn_hi(T_H2 + 2, xT_hi, 4, 4)
            activate("mlp", done(U_MLP + UP))
            his(U_MLP + 4, U_MLP + 8)
            with act.Fori(0, FF_TILES - 2) as e:
                ffn_step("mlp", 0, FF_TILES - 1, e * 8 + U_MLP, 8, e * 2 + T_MLP, 4)
            for e in (FF_TILES - 2, FF_TILES - 1):
                ffn_step("mlp", e, FF_TILES - 1, U_MLP, 8 + 8 * e, T_MLP + 2 * e, 4)
            act.wait_ge(x1_ready, 2)
            sumsq(2)
            root(3, sm[:, 16:18])
            act.wait_ge(ang_ready, 1)
            act.activation(sinM, sm[:, 64:96].rearrange("p (t n) -> p t n", t=TOK), ACT.Sin)
            act.activation(cosM, sm[:, 96:128].rearrange("p (t n) -> p t n", t=TOK), ACT.Sin).then_inc(trig_ready, 1)
            act.wait_ge(x_ready, 1)
            act.dma_start(arena[:, 17024:18432], A["const2"]).then_inc(cst2_loaded, 16)
            act.dma_start(arena[0:16, 18432:20480], A["row_select"]).then_inc(cst2_loaded, 16)

            with act.Fori(0, LAYERS) as l:
                n = l * L_UNITS + U_LAYERS
                t = l * LT + T_LAYERS
                r = l * LR + R_LAYERS
                act.wait_ge(x_ready, l + 1)
                act.dma_start(mod[:, 0:ROWS2], A["rows2"][bass.ds(l, 1), :].rearrange("o n -> (o n)").partition_broadcast(P))\
                   .then_inc(rows_loaded, 16)
                act.dma_start(cvw, A["conv_col"][bass.ds(l, 1), :, :].rearrange("o p n -> p (o n)")).then_inc(rows_loaded, 16)
                his(0, SLOTS, n)
                turn_hi(t + LT_X, xT_hi, 0, 4)
                turn_hi(t + LT_X + 2, xT_hi, 4, 4)
                his(SLOTS, 12, n)
                act.wait_ge(g_free, l * LM + (G_CREDIT + M_LAYERS + 1))
                for tk in range(TOK):
                    act.activation(HB[:, tk, 0:256], P2[:, tk, 0:256], ACT.Square, accum_out=sm[:, 200 + tk:201 + tk])
                    i = act.activation(HB[:, tk, 256:384], P2[:, tk, 256:384], ACT.Square, accum_out=sm[:, 202 + tk:203 + tk])
                i.then_inc(mla_sumsq, 1)
                his(12, 16, n)
                root(r, sm[:, 200:204])
                act.wait_ge(sp_in, l + 1)
                act.wait_ge(rows_loaded, l * 32 + 32)
                act.activation(sp_e, sp_e, ACT.Exp)
                act.activation(ea, row2["a_log"], ACT.Exp).then_inc(sp_exp, 1)
                his(16, 20, n)
                turn_hi(t + LT_MLA, yT_hi, 0, 3)
                his(20, L_OUT, n)
                for tk in range(TOK):
                    act.wait_ge(unit_used, done(n + L_OUT))
                    kv = (G if tk == 0 else T)[:, :, :].rearrange("p c (h d) -> p (c h) d", d=NOPE + MV)
                    act.activation(KF[:, tk, :].rearrange("p (h d) -> p h d", d=QD)[:, :, 0:NOPE], kv[:, :, 0:NOPE], ACT.Copy)
                    act.activation(V2[:, tk, :].rearrange("p (h d) -> p h d", d=MV), kv[:, :, NOPE:], ACT.Copy).then_inc(kv_out, 1)
                his(L_OUT, L_OUT + SLOTS, n)
                for m in range(8):
                    qk, tk, hg = m // 4, m // 2 % 2, m % 2
                    act.wait_ge(mqkT_ready, l * 8 + m + 1)
                    act.activation((mqT, mkT)[qk][0:QD, 4 * hg:4 * hg + 4, tk * P:(tk + 1) * P],
                                   T[0:QD, m % 2, :].rearrange("p (c n) -> p c n", n=P), ACT.Copy).then_inc(mqkT_out, 1)
                for h in range(MH):
                    act.wait_ge(mmax_ready, l * MH + h + 1)
                    if h >= 2:
                        act.wait_ge(meT_ready, l * MH + h - 1)
                    for tk in range(TOK):
                        i = act.activation(me[:, h % 2, tk, :], G[:, h % 2, tk * S:(tk + 1) * S], ACT.Exp, scale=QD ** -0.5,
                                           bias=mnm[:, 2 * h + tk:2 * h + tk + 1], accum_out=mden[:, 2 * h + tk:2 * h + tk + 1])
                    i.then_inc(me_ready, 1)
                act.wait_ge(rows_T, l + 1)
                act.activation(rowT[0:16, :], T[0:16, 0, 0:S], ACT.Copy).then_inc(rows_out, 1)
                for tk in range(TOK):
                    act.wait_ge(lqk_T, l * TOK + tk + 1)
                    act.activation(lqkT[:, :, tk * P:(tk + 1) * P], AC[:, tk, :].rearrange("p (c n) -> p c n", n=P), ACT.Copy)\
                       .then_inc(lqk_out, 1)
                act.wait_ge(lmax_ready, l + 1)
                act.activation(lfloor, lfloor, ACT.Exp, scale=-1.0)
                for j in range(2 * LH):
                    c = j % 2 * LH + j // 2
                    for tk in range(TOK):
                        i = act.activation(lw[:, j, tk, :], lw[:, j, tk, :], ACT.Exp, bias=lnm[:, tk * 8 + c:tk * 8 + c + 1])
                    i.then_inc(lexp_ready, 1)
                act.activation(P2[:, :, IN2["mo"]:IN2["mo"] + 256], P2[:, :, IN2["mo"]:IN2["mo"] + 256], ACT.Sigmoid).then_inc(lgate, 1)
                for h in range(LH):
                    act.wait_ge(lpT_ready, l * LH + h + 1)
                    if h >= 2:
                        act.wait_ge(lnum_ready, l * LH + h - 1)
                    act.activation(lpT[:, h % 2, :], T[:, h % 2, :], ACT.Copy).then_inc(lpT_out, 1)
                root(r + 1, sm[:, 64:72])
                for m in range(3):
                    act.wait_ge(sx_T, l * 3 + m + 1)
                    if m < 2:
                        i = act.activation(xpad[:, 0:4, 2 + m * P:2 + (m + 1) * P], AC[:, m, :].rearrange("p (c n) -> p c n", n=P), ACT.Copy)
                    else:
                        i = act.activation(xpad[:, 4:6, 2:2 + S], AC[:, 2, :].rearrange("p (c n) -> p c n", n=S), ACT.Copy)
                    i.then_inc(sx_out, 1)
                act.wait_ge(conv_done, l + 1)
                for c in range(XBC_CH):
                    i = act.activation(xc[:, c, :], xc[:, c, :], ACT.Silu, bias=cv_b[:, c:c + 1])
                act.activation(P2[:, :, IN2["z"]:IN2["z"] + 256], P2[:, :, IN2["z"]:IN2["z"] + 256], ACT.Silu).then_inc(conv_act, 1)
                for j in range(2 * SH):
                    c = j % 2 * SH + j // 2
                    act.wait_ge(srow_out, l * 8 + j + 1)
                    for st in range(TOK):
                        i = act.activation(sw[:, j, st, :], sw[:, j, st, :], ACT.Exp, bias=ncs[:, st * 8 + c:st * 8 + c + 1])
                    i.then_inc(sexp_ready, 1)
                root(r + 2, sm[:, 64:68])
                turn_hi(t + LT_OUT, yT_hi, 0, 4)
                his(L_OUT + 4, L_OUT + 8, n)
                turn_hi(t + LT_OUT + 2, yT_hi, 0, 4, done(n + L_OUT + 4))
                his(L_ROUTER, L_MOE + 3, n)
                root(r + 3, sm[:, 16:18])
                turn_hi(t + LT_X2, xT_hi, 0, 4)
                turn_hi(t + LT_X2 + 2, xT_hi, 4, 4)
                his(L_MOE + 3, L_MOE + 4, n)
                act.wait_ge(gexp_in, l + 1)
                act.activation(rt_e, rt_e, ACT.Exp).then_inc(gexp_out, 1)
                activate("moe", done(n + L_MOE + UP))
                his(L_MOE + 4, L_MOE + 8, n)
                with act.Fori(0, 3) as e4:
                    for q in range(4):
                        ffn_step("moe", 0, EXPERTS - 1, e4 * 24 + n, L_MOE + 8 + 6 * q, t + LT_MOE + e4 * 8 + 2 * q, 2)
                for e in range(12, EXPERTS):
                    ffn_step("moe", e, EXPERTS - 1, n, L_MOE + 8 + 6 * e, t + LT_MOE + 2 * e, 2)
                root(r + 4, sm[:, 16:18])
        @block.tensor
        def _(pe):
            def mm3(out, xh, xl, wh, wl, start, stop):
                pe.matmul(out, xh, wh, start=start, stop=False)
                pe.matmul(out, xh, wl, start=False, stop=False)
                return pe.matmul(out, xl, wh, start=False, stop=stop)

            def up(n, k, banks):
                for u in range(UP):
                    pe.wait_ge(lo_ready, n + (k + u + 1))
                    s = (k + u) % SLOTS
                    for t in range(TOK):
                        for j in range(2):
                            c, w = 2 * u + j, slice(j * NT, (j + 1) * NT)
                            i = mm3(banks[:, t, :], xT_hi[:, c, t * P:(t + 1) * P], xT_lo[:, c, t * P:(t + 1) * P],
                                    w_hi[:, s, w], w_lo[:, s, w], c == 0, c == KC - 1)
                    i.then_inc(unit_used, 1)

            def down(n, k, nch, first, last):
                for c in range(nch):
                    pe.wait_ge(lo_ready, n + (k + c + 1))
                    s = (k + c) % SLOTS
                    for t in range(TOK):
                        for j in range(2):
                            w = slice(j * NT, (j + 1) * NT)
                            i = mm3(AC[:, 2 * t + j, :], yT_hi[:, c, t * P:(t + 1) * P], yT_lo[:, c, t * P:(t + 1) * P],
                                    w_hi[:, s, w], w_lo[:, s, w], first and c == 0, last and c == nch - 1)
                    i.then_inc(unit_used, 1)

            def turn(n, src, nch):
                for t in range(TOK):
                    if not (isinstance(n, int) and n < TOK):
                        pe.wait_ge(t_lo, n + t - 1)
                    for c in range(nch):
                        i = pe.transpose(T[:, t, c * P:(c + 1) * P], src[:, t, c * P:(c + 1) * P], ident[:, :])
                    i.then_inc(t_ready, 1)

            def clear_acc():
                for b in range(4):
                    pe.matmul(AC[:, b, :], zero_r[0:1, :], xT_hi[0:1, 0:2, :].rearrange("p c n -> p (c n)"),
                              start=True, stop=False)

            def ffn_step(e, last, n, k, t, h, h_src, ndown):
                pe.wait_ge(ffn_h, h + 1)
                turn(t, h_src, ndown)
                if e < last:
                    up(n, k, G)
                pe.wait_ge(t_lo, t + TOK)
                down(n, k + UP if e < last else k, ndown, False, e == last)

            pe.wait_ge(tab_wide, 1)
            pe.wait_ge(bias_in_loaded, 32)
            for h in range(N_AH):
                if h >= 2:
                    pe.wait_ge(bias_rows_out, h - 1)
                pe.matmul(T[:, h % 2, :], tab_bc[:, h, :], onehot[:, h // AH, :], start=True, stop=True).then_inc(bias_row, 1)
            pe.wait_ge(c_lo, 1)
            with pe.Fori(0, N_ADA // 2) as i2:
                for b in range(2):
                    pe.wait_ge(g_free, i2 * 2 + (G_CREDIT + b - 1))
                    for u in range(UP):
                        pe.wait_ge(lo_ready, i2 * (2 * UP) + (b * UP + u + 1))
                        for j in range(2):
                            c, w = 2 * u + j, slice(j * NT, (j + 1) * NT)
                            i = mm3(G[:, b, :], xT_hi[:, c, 0:P], xT_lo[:, c, 0:P], w_hi[:, u, w], w_lo[:, u, w], c == 0, c == KC - 1)
                        i.then_inc(unit_used, 1)
            pe.wait_ge(h_ready, 1)
            pe.wait_ge(cst_loaded, 32)
            turn(T_H1, h_sb[:, :, 0:NT], 4)
            turn(T_H1 + 2, h_sb[:, :, NT:D], 4)
            pe.wait_ge(t_lo, T_H1 + 4)
            with pe.Fori(0, N_RET_IN // 2) as i2:
                for b in range(2):
                    pe.wait_ge(g_free, i2 * 2 + (G_CREDIT + M_RET_IN + b - 1))
                    up(i2 * (2 * UP) + U_RET_IN, b * UP, (G, AC)[b])
            for n in range(8):
                tk, s4 = n // 4, n % 4
                pe.wait_ge(rope_done, tk + 1)
                if n >= 2:
                    pe.wait_ge(rqk_out, n - 1)
                for c in range(4):
                    i = pe.transpose(T[:, n % 2, c * P:(c + 1) * P], tile(s4)[:, tk, c * P:(c + 1) * P], ident[:, :])
                i.then_inc(rqk_ready, 1)

            def ret_scores(h):
                if h >= 2:
                    pe.wait_ge(rs_out, h - 1)
                b = h % 2
                for c in range(2):
                    pe.matmul(T[:, b, 0:S], qkT[:, 8 + 2 * h + c, 0:P], qkT[:, 2 * h + c, :], start=c == 0, stop=c == 1)
                for c in range(2):
                    i = pe.matmul(T[:, b, S:S + P], qkT[:, 8 + 2 * h + c, P:S], qkT[:, 2 * h + c, P:S], start=c == 0, stop=c == 1)
                i.then_inc(rs_ready, 1)

            def ret_out(h):
                b, o = h % 2, (G if h % 2 == 0 else AC)
                pe.wait_ge(rs_out, h + 1)
                if h >= 2:
                    pe.wait_ge(ro_out, h - 1)
                v = tile(4 + h)
                pe.matmul(o[:, 0, :], scr[:, b, 0:P], v[:, 0, :], start=True, stop=True)
                pe.matmul(o[:, 1, :], scr[:, b, P:S], v[:, 0, :], start=True, stop=False)
                pe.matmul(o[:, 1, :], scr[:, b, S:S + P], v[:, 1, :], start=False, stop=True).then_inc(ro_ready, 1)

            pe.wait_ge(rqk_out, 8)
            ret_scores(0)
            for h in range(RH):
                if h + 1 < RH:
                    ret_scores(h + 1)
                ret_out(h)
            for h in range(RH):
                pe.wait_ge(y_ready, h + 1)
                turn(T_RET + 2 * h, tile(8 + h), 4)
                pe.wait_ge(t_lo, T_RET + 2 * h + TOK)
                down(0, U_RET_OUT + 4 * h, 4, h == 0, h == RH - 1)
            pe.wait_ge(acc_free, 1)
            with pe.Fori(0, 4) as i2:
                for b in range(2):
                    pe.wait_ge(g_free, i2 * 2 + (G_CREDIT + M_ATT_IN + b - 1))
                    up(i2 * (2 * UP) + U_ATT_IN, b * UP, (G, AC)[b])
            pe.wait_ge(g_free, G_CREDIT + M_ATT_IN + 7)
            up(U_ATT_IN, 8 * UP, G)

            def att_scores(k):
                b, h, qk = k % 2, k % AH, aqkT[k // AH % 2]
                if k >= 2:
                    pe.wait_ge(as_out, k - 1)
                pe.matmul(G[:, b, 0:P], qk[:, h, 0:P], qk[:, AH + h, 0:P], start=True, stop=True)
                pe.matmul(G[:, b, P:384], qk[:, h, P:S], qk[:, AH + h, :], start=True, stop=True).then_inc(as_ready, 1)

            def att_turn(k):
                b = k % 2
                pe.wait_ge(ae_ready, k + 1)
                if k >= 2:
                    pe.wait_ge(aeT_out, k - 1)
                for c in range(3):
                    i = pe.transpose(T[:, b, c * P:(c + 1) * P], a_e[:, b, c * P:(c + 1) * P], ident[:, :])
                i.then_inc(aeT_ready, 1)

            def att_values(k):
                b, v = k % 2, tile(3 * (k // AH) + 2)[:, :, k % AH * ADH:(k % AH + 1) * ADH]
                pe.wait_ge(aeT_out, k + 1)
                if k >= 2:
                    pe.wait_ge(ao_out, k - 1)
                pe.matmul(AC[:, b, 0:P], a_eT[b][:, 0:P], v[:, 0, :], start=True, stop=True)
                pe.matmul(AC[:, b, P:S], a_eT[b][:, P:S], v[:, 0, :], start=True, stop=False)
                pe.matmul(AC[:, b, P:S], a_eT[b][:, S:384], v[:, 1, :], start=False, stop=True).then_inc(ao_ready, 1)

            pe.wait_ge(g_free, G_CREDIT + M_GATE)
            for k in range(N_AH + 2):
                if k < N_AH:
                    if k % AH == 0:
                        if k:
                            att_turn(k - 1)
                            pe.wait_ge(aeT_out, k)
                        for n in range(4):
                            tk, qk = n // 2, n % 2
                            if k + n >= 2:
                                pe.wait_ge(aqk_out, k + n - 1)
                            for c in range(AH):
                                i = pe.transpose(T[:, n % 2, c * P:(c + 1) * P],
                                                 tile(3 * (k // AH) + qk)[:, tk, c * P:(c + 1) * P], ident[:, :])
                            i.then_inc(aqk_ready, 1)
                        pe.wait_ge(aqk_out, k + 4)
                    att_scores(k)
                if 1 <= k <= N_AH and (k % AH or k == N_AH):
                    att_turn(k - 1)
                if k >= 2:
                    att_values(k - 2)
            for j in range(N_GATE):
                if j < 2:
                    pe.wait_ge((as_out, ao_out)[j], N_AH)
                else:
                    pe.wait_ge(g_free, G_CREDIT + M_GATE + j - 1)
                up(0, U_GATE + j * UP, (G, AC)[j % 2])
            pe.wait_ge(att_ready, 1)
            turn(T_ATT, tile(0), 4)
            pe.wait_ge(t_lo, T_ATT + TOK)
            pe.wait_ge(g_free, G_CREDIT + M_MLP)
            down(0, U_ATT_OUT, 4, True, True)
            for n in range(2):
                pe.wait_ge(merged_ready, n + 1)
                turn(T_MERGE + 2 * n, tile(10 + n), 4)
                pe.wait_ge(t_lo, T_MERGE + 2 * n + TOK)
                pe.wait_ge(acc_free, 2)
                down(0, U_WO + 4 * n, 4, n == 0, n == 1)
            pe.wait_ge(h_ready, 2)
            turn(T_H2, h_sb[:, :, 0:NT], 4)
            turn(T_H2 + 2, h_sb[:, :, NT:D], 4)
            pe.wait_ge(t_lo, T_H2 + 4)
            pe.wait_ge(acc_free, 3)
            pe.wait_ge(zero_ready, 1)
            clear_acc()
            up(0, U_MLP, G)
            with pe.Fori(0, FF_TILES - 2) as e:
                ffn_step(0, FF_TILES - 1, e * 8 + U_MLP, UP, e * 2 + T_MLP, e, tile(1), 4)
            for e in (FF_TILES - 2, FF_TILES - 1):
                ffn_step(e, FF_TILES - 1, U_MLP, UP + 8 * e, T_MLP + 2 * e, e, tile(1), 4)

            pe.wait_ge(cst2_loaded, 32)
            with pe.Fori(0, LAYERS) as l:
                n = l * L_UNITS + U_LAYERS
                tb = l * LT + T_LAYERS
                m = l * LM + (M_LAYERS + G_CREDIT)
                pe.wait_ge(x_ready, l + 1)
                turn(tb + LT_X, x_sb[:, :, 0:NT], 4)
                turn(tb + (LT_X + 2), x_sb[:, :, NT:D], 4)
                pe.wait_ge(t_lo, tb + (LT_X + 4))
                for j in range(N_IN2):
                    pe.wait_ge(g_free, m + (j - 1))
                    up(n, L_IN + j * UP, (G, AC)[j % 2])
                pe.wait_ge(cq_ready, l + 1)
                turn(tb + LT_MLA, P2, 3)
                pe.wait_ge(t_lo, tb + (LT_MLA + TOK))
                pe.wait_ge(g_free, m + N_IN2)
                for c in range(2):
                    pe.wait_ge(lo_ready, n + (L_UQ + c + 1))
                    s = (L_UQ + c) % SLOTS
                    for t in range(TOK):
                        for b, (w0, w1) in enumerate(((0, NT), (NT, MH * QD))):
                            i = mm3(AC[:, 2 * t + b, 0:w1 - w0], yT_hi[:, c, t * P:(t + 1) * P], yT_lo[:, c, t * P:(t + 1) * P],
                                    w_hi[:, s, w0:w1], w_lo[:, s, w0:w1], c == 0, c == 1)
                    i.then_inc(unit_used, 1)
                pe.wait_ge(lo_ready, n + (L_UKV + 1))
                s = L_UKV % SLOTS
                for t in range(TOK):
                    for b in range(2):
                        w = slice(b * NT, (b + 1) * NT)
                        i = mm3((G, T)[t][:, b, :], yT_hi[:, 2, t * P:(t + 1) * P], yT_lo[:, 2, t * P:(t + 1) * P],
                                w_hi[:, s, w], w_lo[:, s, w], True, True)
                i.then_inc(unit_used, 1)
                pe.wait_ge(cum_in, l + 1)
                pe.wait_ge(kv_out, l * TOK + TOK)
                cum = G[:, 0, 0:64].rearrange("p (k n) -> p k n", n=16)
                pe.matmul(cum[:, 0, :], tri_f, cu[:, 0, :], start=True, stop=True)
                pe.matmul(cum[:, 1, :], ones, cu[:, 0, :], start=True, stop=False)
                pe.matmul(cum[:, 1, :], tri_f, cu[:, 1, :], start=False, stop=True)
                pe.matmul(cum[:, 2, :], tri_b, cu[:, 0, :], start=True, stop=False)
                pe.matmul(cum[:, 2, :], ones, cu[:, 1, :], start=False, stop=True)
                pe.matmul(cum[:, 3, :], tri_b, cu[:, 1, :], start=True, stop=True).then_inc(cum_ready, 1)
                for k in range(8):
                    qk, tk, hg = k // 4, k // 2 % 2, k % 2
                    pe.wait_ge((q_ready, kv_ready)[qk], l + 1)
                    if k >= 2:
                        pe.wait_ge(mqkT_out, l * 8 + (k - 1))
                    for c in range(4):
                        h = 4 * hg + c
                        i = pe.transpose(T[0:QD, k % 2, c * P:(c + 1) * P], (Q, KF)[qk][:, tk, h * QD:(h + 1) * QD], ident[:, :])
                    i.then_inc(mqkT_ready, 1)

                def mla_scores(h):
                    if h >= 2:
                        pe.wait_ge(me_ready, l * MH + (h - 1))
                    for t in range(TOK):
                        i = pe.matmul(G[:, h % 2, t * S:(t + 1) * S], mqT[0:QD, h, t * P:(t + 1) * P], mkT[0:QD, h, :], start=True, stop=True)
                    i.then_inc(ms_ready, 1)

                def mla_turn(h):
                    pe.wait_ge(me_ready, l * MH + (h + 1))
                    if h >= 2:
                        pe.wait_ge(meT_out, l * MH + (h - 1))
                    for kt in range(TOK):
                        for t in range(TOK):
                            c = kt * TOK + t
                            i = pe.transpose(T[:, h % 2, c * P:(c + 1) * P], me[:, h % 2, t, kt * P:(kt + 1) * P], ident[:, :])
                    i.then_inc(meT_ready, 1)

                def mla_values(h):
                    pe.wait_ge(meT_out, l * MH + (h + 1))
                    if h >= 2:
                        pe.wait_ge(mo_out, l * MH + (h - 1))
                    for t in range(TOK):
                        for kt in range(TOK):
                            c = kt * TOK + t
                            i = pe.matmul(AC[:, h % 2, t * MV:(t + 1) * MV], meT[:, h % 2, c * P:(c + 1) * P],
                                          V2[:, kt, h * MV:(h + 1) * MV], start=kt == 0, stop=kt == TOK - 1)
                    i.then_inc(mo_ready, 1)

                pe.wait_ge(mqkT_out, l * 8 + 8)
                pe.wait_ge(rows_w, l + 1)
                for h in range(MH + 2):
                    if h < MH:
                        mla_scores(h)
                    if 1 <= h <= MH:
                        mla_turn(h - 1)
                    if h >= 2:
                        mla_values(h - 2)
                pe.wait_ge(meT_out, l * MH + MH)
                for t in range(TOK):
                    i = pe.transpose(T[0:16, 0, t * P:(t + 1) * P], rw[:, t, :], ident[:, :])
                i.then_inc(rows_T, 1)
                pe.wait_ge(mo_out, l * MH + MH)
                for t in range(TOK):
                    for c in range(4):
                        a = IN2["mq"] + c * P
                        i = pe.transpose(AC[:, t, c * P:(c + 1) * P], P2[:, t, a:a + P], ident[:, :])
                    i.then_inc(lqk_T, 1)
                pe.wait_ge(rows_out, l + 1)

                def row(out, c):
                    return pe.matmul(out, sel[0:16, c, :], rowT[0:16, :], start=True, stop=True)

                for j in range(2 * LH):
                    if j >= 2:
                        pe.wait_ge(lrow_out, l * 8 + (j - 1))
                    row(G[:, j % 2, 0:S], j % 2 * LH + j // 2).then_inc(lrow_ready, 1)
                pe.wait_ge(lqk_out, l * TOK + TOK)
                for h in range(LH):
                    a = h % 2 * LDH
                    for t in range(TOK):
                        i = pe.matmul(AC[:, h, t * S:(t + 1) * S], lqkT[a:a + LDH, h // 2, t * P:(t + 1) * P],
                                      lqkT[a:a + LDH, 2 + h // 2, :], start=True, stop=True)
                    i.then_inc(lqk_ready, 1)
                pe.wait_ge(lrow_out, l * 8 + 8)

                def lstm_turn(h):
                    pe.wait_ge(lp_ready, l * LH + (h + 1))
                    if h >= 2:
                        pe.wait_ge(lpT_out, l * LH + (h - 1))
                    for st in range(TOK):
                        for t in range(TOK):
                            c = st * TOK + t
                            i = pe.transpose(T[:, h % 2, c * P:(c + 1) * P], lw[:, 2 * h, t, st * P:(st + 1) * P], ident[:, :])
                    i.then_inc(lpT_ready, 1)

                def lstm_values(h):
                    pe.wait_ge(lpT_out, l * LH + (h + 1))
                    a = IN2["mv"] + h * LDH
                    for t in range(TOK):
                        for st in range(TOK):
                            c = st * TOK + t
                            i = pe.matmul(G[:, 0, t * S + h * LDH:t * S + (h + 1) * LDH], lpT[:, h % 2, c * P:(c + 1) * P],
                                          P2[:, st, a:a + LDH], start=st == 0, stop=st == TOK - 1)
                    i.then_inc(lnum_ready, 1)

                for h in range(LH + 1):
                    if h < LH:
                        lstm_turn(h)
                    if h >= 1:
                        lstm_values(h - 1)
                for k in range(3):
                    for c in range(4):
                        t, ch = (k, c) if k < 2 else (c % 2, 4 + c // 2)
                        a = IN2["xbc"] + ch * P
                        i = pe.transpose(AC[:, k, c * P:(c + 1) * P], P2[:, t, a:a + P], ident[:, :])
                    i.then_inc(sx_T, 1)
                pe.wait_ge(conv_act, l + 1)
                for t in range(TOK):
                    for c in range(2):
                        a = (t * 2 + c) * P
                        i = pe.transpose(T[:, 0, a:a + P], xc[:, c, t * P:(t + 1) * P], ident[:, :])
                i.then_inc(sxt_T, 1)
                for g in range(SG):
                    for st in range(TOK):
                        i = pe.matmul(AC[:, g, st * S:(st + 1) * S], xc[:, 2 + g, st * P:(st + 1) * P], xc[:, 4 + g, :], start=True, stop=True)
                    i.then_inc(scb_ready, 1)
                for j in range(2 * SH):
                    if j >= 2:
                        pe.wait_ge(srow_out, l * 8 + (j - 1))
                    row(AC[:, 2 + j % 2, 0:S], 8 + j % 2 * SH + j // 2).then_inc(srow_ready, 1)
                for h in range(SH):
                    pe.wait_ge(sw_ready, l * 8 + (2 * h + 2))
                    for t, pairs in enumerate((((0, 0), (1, 0), (1, 1)), ((0, 0), (0, 1), (1, 1)))):
                        for k, (d, st) in enumerate(pairs):
                            i = pe.matmul(T[:, 1, t * S + h * SP_:t * S + (h + 1) * SP_], sw[:, 2 * h + d, st, t * P:(t + 1) * P],
                                          xdt[:, st, d, h * SP_:(h + 1) * SP_], start=k == 0, stop=k == 2)
                    i.then_inc(sy_ready, 1)
                pe.wait_ge(sy_out, l + 1)
                turn(tb + LT_OUT, HB[:, :, 0:NT], 4)
                pe.wait_ge(t_lo, tb + (LT_OUT + TOK))
                down(n, L_OUT, 4, True, False)
                pe.wait_ge(heads_ready, l + 1)
                turn(tb + (LT_OUT + 2), HB[:, :, NT:D], 4)
                pe.wait_ge(t_lo, tb + (LT_OUT + 2 + TOK))
                down(n, L_OUT + 4, 4, False, True)
                pe.wait_ge(x2_ready, l + 1)
                turn(tb + LT_X2, x_sb[:, :, 0:NT], 4)
                turn(tb + (LT_X2 + 2), x_sb[:, :, NT:D], 4)
                pe.wait_ge(t_lo, tb + (LT_X2 + 4))
                pe.wait_ge(lo_ready, n + (L_ROUTER + 1))
                s, nr = L_ROUTER % SLOTS, EGROUPS + EXPERTS
                for t in range(TOK):
                    for c in range(KC):
                        w = slice(c * nr, (c + 1) * nr)
                        i = mm3(G[:, t, 0:nr], xT_hi[:, c, t * P:(t + 1) * P], xT_lo[:, c, t * P:(t + 1) * P],
                                w_hi[:, s, w], w_lo[:, s, w], c == 0, c == KC - 1)
                i.then_inc(unit_used, 1)
                pe.wait_ge(acc_free, l * LC + (C_LAYERS + 1))
                clear_acc()
                pe.wait_ge(g_free, m + LM)
                up(n, L_MOE, G)
                with pe.Fori(0, 3) as e4:
                    for q in range(4):
                        ffn_step(0, EXPERTS - 1, e4 * 24 + n, L_MOE + UP + 6 * q, e4 * 8 + (tb + (LT_MOE + 2 * q)),
                                 l * EXPERTS + e4 * 4 + (FF_TILES + q), moe_h, 2)
                for e in range(12, EXPERTS):
                    ffn_step(e, EXPERTS - 1, n, L_MOE + UP + 6 * e, tb + (LT_MOE + 2 * e), l * EXPERTS + (FF_TILES + e), moe_h, 2)
        @block.vector
        def _(dve):
            dep = dve.drain

            def lo(n, dst_hi, dst_lo, c0, nch):
                for t in range(TOK):
                    dve.wait_ge(t_hi, n + t + 1)
                    s = slice(t * P, (t + 1) * P)
                    dve.tensor_tensor(dst_lo[:, c0:c0 + nch, s], T[:, t, 0:nch * P].rearrange("p (c n) -> p c n", n=P),
                                      dst_hi[:, c0:c0 + nch, s].bitcast(F32), ALU.subtract).then_inc(t_lo, 1)

            def rstd(n, ap, scale, eps):
                dep()
                dve.tensor_scalar(ap, ap, scale, eps, ALU.mult, ALU.add).then_inc(var_ready, 1)
                dve.wait_ge(std_ready, n + 1)
                dve.reciprocal(ap, ap)
                dep()

            def wide(row, t=TOK):
                return row.unsqueeze(1).to_broadcast([P, t, row.shape[1]])

            def read_tile(dst, banks, n_done):
                dve.wait_ge(unit_used, n_done)
                dve.tensor_copy(dst, banks[:, 0:2, :]).then_inc(g_free, 1)

            def modulated(n, sc, sh, g_loaded, n_h):
                A1 = W[:, 0:D]
                dve.wait_ge(sumsq_ready, n)
                dve.wait_ge(g_loaded, 16)
                dve.scalar_tensor_tensor(A1, mod[:, sc * D:(sc + 1) * D], 1.0, A1, ALU.add, ALU.mult)
                rstd((0, 2)[n - 1], sm[:, 16:18], 1.0 / D, 1e-6)
                for t in range(TOK):
                    dve.scalar_tensor_tensor(h_sb[:, t, :], x_sb[:, t, :], sm[:, 16 + t:17 + t], A1, ALU.mult, ALU.mult)
                dep()
                dve.tensor_tensor(h_sb, h_sb, wide(mod[:, sh * D:(sh + 1) * D]), ALU.add).then_inc(h_ready, 1)

            dve.memset(sm[:, 892:893], 0.0).then_inc(unit_used, SLOTS)
            dve.memset(sm[:, 893:894], 0.0).then_inc(g_free, G_CREDIT)
            dve.memset(zero_r[:, :].bitcast(F32), 0.0).then_inc(zero_ready, 1)
            for k in range(4):
                dve.memset(wt4[:, k:k + 1], 4.0 - k)
            dve.memset(tab[BUCKETS:BUCKETS + 1, :], NEG)
            dep()
            dve.wait_ge(bias_in_loaded, 32)
            dve.tensor_copy(tab_bc, tab.unsqueeze(2).to_broadcast([BUCKETS + 1, N_AH, P])).then_inc(tab_wide, 1)
            dve.wait_ge(c_hi, 1)
            dve.tensor_tensor(xT_lo[:, :, 0:P], csil.unsqueeze(2).to_broadcast([P, KC, P]), xT_hi[:, :, 0:P].bitcast(F32),
                              ALU.subtract).then_inc(c_lo, 1)
            for h in range(N_AH):
                dve.wait_ge(bias_row, h + 1)
                dve.tensor_copy(bias_vec[:, h, :], T[:, h % 2, :]).then_inc(bias_rows_out, 1)
            dve.wait_ge(ada_b_loaded, 16)
            with dve.Fori(0, N_ADA // 2) as i2:
                for b in range(2):
                    m = mod[:, bass.ds(i2 * (2 * NT) + b * NT, NT)]
                    dve.wait_ge(unit_used, i2 * (2 * UP) + done(U_ADA + (b + 1) * UP))
                    dve.tensor_tensor(m, m, G[:, b, :], ALU.add).then_inc(g_free, 1)
            dep()
            modulated(1, 1, 0, norm1_loaded, 1)
            lo(T_H1, xT_hi, xT_lo, 0, 4)
            lo(T_H1 + 2, xT_hi, xT_lo, 4, 4)
            dve.wait_ge(bias_stored, 16)
            with dve.Fori(0, N_RET_IN // 2) as i2:
                for b in range(2):
                    dst = arena[:, bass.ds(i2 * 2048 + b * 1024, 1024)].rearrange("p (t n) -> p t n", t=TOK)
                    read_tile(dst, (G, AC)[b], i2 * (2 * UP) + done(U_RET_IN + (b + 1) * UP))
            dep()
            dve.wait_ge(cst_loaded, 32)
            halves = slot(0, 4).rearrange("p j t (h x n) -> p j t h x n", h=2, x=2)
            for t in range(TOK):
                x1, x2 = halves[:, :, t, :, 0, :], halves[:, :, t, :, 1, :]
                t1, t2 = [W[:, a * 1024:(a + 1) * 1024].rearrange("p (j h n) -> p j h n", j=4, h=2) for a in range(2)]
                c, s = [r[:, t, :].unsqueeze(1).unsqueeze(1).to_broadcast([P, 4, 2, P]) for r in (cosR, sinR)]
                dve.tensor_tensor(t1, x1, s, ALU.mult)
                dve.tensor_tensor(t2, x2, s, ALU.mult)
                dep()
                dve.tensor_tensor(x1, x1, c, ALU.mult)
                dve.tensor_tensor(x2, x2, c, ALU.mult)
                dep()
                dve.tensor_tensor(x1, x1, t2, ALU.subtract)
                dve.tensor_tensor(x2, x2, t1, ALU.add).then_inc(rope_done, 1)
                dep()
            for h in range(RH):
                dve.wait_ge(rs_ready, h + 1)
                if h >= 2:
                    dve.wait_ge(ro_ready, h - 1)
                dve.tensor_tensor(scr[:, h % 2, :], T[:, h % 2, 0:384], decay[:, h, :], ALU.mult).then_inc(rs_out, 1)
            for h in range(RH):
                dve.wait_ge(ro_out, h + 1)
                for t in range(TOK):
                    dve.bn_stats(bst[:, 2 * h + t, :], tile(h)[:, t, :])
            dep()
            for k in range(2 * RH):
                dve.bn_aggr(mv[:, k, :], bst[:, k, :])
            dep()
            dve.tensor_copy(sm[:, 32:40], mv[:, 0:8, 1])
            rstd(1, sm[:, 32:40], 1.0, 1e-5)
            dve.wait_ge(gn_g_loaded, 16)
            dve.wait_ge(gn_b_loaded, 16)
            dve.wait_ge(rg_gated, 1)
            for h in range(RH):
                o, cols = tile(h), slice(h * RDV, (h + 1) * RDV)
                for t in range(TOK):
                    k = 2 * h + t
                    dve.tensor_scalar(o[:, t, :], o[:, t, :], mv[:, k, 0:1], sm[:, 32 + k:33 + k], ALU.subtract, ALU.mult)
                dep()
                dve.tensor_tensor(o, o, wide(mod[:, cols]), ALU.mult)
                dep()
                dve.tensor_tensor(o, o, wide(W[:, cols]), ALU.add)
                dep()
                dve.tensor_tensor(tile(8 + h), tile(8 + h), o, ALU.mult).then_inc(y_ready, 1)
                if h >= 1:
                    lo(T_RET + 2 * (h - 1), yT_hi, yT_lo, 0, 4)
            lo(T_RET + 2 * (RH - 1), yT_hi, yT_lo, 0, 4)
            acc_ct = AC[:, :, :].rearrange("p (t c) n -> p t c n", t=TOK)
            dve.wait_ge(unit_used, done(U_RET_OUT + 4 * RH))
            dve.tensor_copy(tile(10), acc_ct[:, :, 0, :])
            dve.tensor_copy(tile(11), acc_ct[:, :, 1, :]).then_inc(acc_free, 1)
            with dve.Fori(0, 4) as i2:
                for b in range(2):
                    dst = arena[:, bass.ds(i2 * 2048 + b * 1024, 1024)].rearrange("p (t n) -> p t n", t=TOK)
                    read_tile(dst, (G, AC)[b], i2 * (2 * UP) + done(U_ATT_IN + (b + 1) * UP))
            read_tile(tile(8), G, done(U_GATE))
            def att_eT(k):
                dve.wait_ge(aeT_ready, k + 1)
                if k >= 2:
                    dve.wait_ge(ao_ready, k - 1)
                dve.tensor_copy(a_eT[k % 2], T[:, k % 2, 0:384]).then_inc(aeT_out, 1)

            for k in range(N_AH):
                g, h = k // AH, k % AH
                s = scr[:, k % 2, :]
                if h == 0:
                    dve.wait_ge(rel_loaded[g], 32)
                    if k:
                        att_eT(k - 1)
                dve.wait_ge(as_ready, k + 1)
                if k >= 2:
                    dve.wait_ge(ae_ready, k - 1)
                dve.scalar_tensor_tensor(s, G[:, k % 2, 0:384], ADH ** -0.5, rel[g][:, h, :], ALU.mult, ALU.add)
                dep()
                dve.tensor_reduce(amx[:, 2 * k:2 * k + 1], s[:, 0:P], AX.X, ALU.max)
                dve.tensor_reduce(amx[:, 2 * k + 1:2 * k + 2], s[:, P:384], AX.X, ALU.max)
                dep()
                dve.tensor_scalar(anm[:, 2 * k:2 * k + 2], amx[:, 2 * k:2 * k + 2], -1.0, None, ALU.mult).then_inc(as_out, 1)
                if h >= 1:
                    att_eT(k - 1)
            att_eT(N_AH - 1)
            dve.tensor_tensor(aM, amx[:, 0:8], amx[:, 8:16], ALU.max)
            dep()
            dve.tensor_tensor(aM, aM, amx[:, 16:24], ALU.max)
            dep()
            dve.tensor_tensor(adiff.rearrange("p (g n) -> p g n", g=3), amx.rearrange("p (g n) -> p g n", g=3),
                              aM.unsqueeze(1).to_broadcast([P, 3, 8]), ALU.subtract).then_inc(lse_diff, 1)
            dve.wait_ge(lse_exp, 1)
            dve.tensor_tensor(aden, aden, afac, ALU.mult)
            dep()
            dve.tensor_reduce(aD, aden.rearrange("p (g n) -> p n g", g=3), AX.X, ALU.add)
            dep()
            dve.reciprocal(aD, aD)
            dep()
            dve.tensor_tensor(afac.rearrange("p (g n) -> p g n", g=3), afac.rearrange("p (g n) -> p g n", g=3),
                              aD.unsqueeze(1).to_broadcast([P, 3, 8]), ALU.mult)
            dep()
            dve.wait_ge(ao_out, N_AH)
            for g in range(3):
                for h in range(AH):
                    for t in range(TOK):
                        k = (g * AH + h) * 2 + t
                        o, a = tile(3 * g)[:, t, h * ADH:(h + 1) * ADH], tile(0)[:, t, h * ADH:(h + 1) * ADH]
                        if g == 0:
                            dve.tensor_scalar(o, o, afac[:, k:k + 1], None, ALU.mult)
                        else:
                            i = dve.scalar_tensor_tensor(a, o, afac[:, k:k + 1], a, ALU.mult, ALU.add)
                if g < 2:
                    dep()
            i.then_inc(att_ready, 1)
            lo(T_ATT, yT_hi, yT_lo, 0, 4)
            dve.wait_ge(g_free, G_CREDIT + M_MLP)
            dve.wait_ge(unit_used, done(U_WO))
            for n in range(2):
                i = dve.tensor_tensor(tile(4 + n), tile(4 + n), acc_ct[:, :, n, :], ALU.mult)
                if n == 1:
                    i.then_inc(acc_free, 1)
                dve.tensor_tensor(tile(10 + n), tile(10 + n), tile(1 + n), ALU.mult)
            dep()
            for n in range(2):
                dve.tensor_tensor(tile(10 + n), tile(10 + n), tile(4 + n), ALU.add).then_inc(merged_ready, 1)
            lo(T_MERGE, yT_hi, yT_lo, 0, 4)
            lo(T_MERGE + 2, yT_hi, yT_lo, 0, 4)
            def gated_residual(g, n_done):
                dve.wait_ge(unit_used, n_done)
                tmp = arena[:, 10240:12288].rearrange("p (t n) -> p t n", t=TOK)
                dve.tensor_tensor(tmp, AC_tok, wide(mod[:, g * D:(g + 1) * D]), ALU.mult).then_inc(acc_free, 1)
                dep()
                dve.tensor_tensor(x_sb[:, :, :], x_sb[:, :, :], tmp, ALU.add).then_inc(x1_ready, 1)

            gated_residual(2, done(U_MLP))
            modulated(2, 4, 3, norm2_loaded, 2)
            lo(T_H2, xT_hi, xT_lo, 0, 4)
            lo(T_H2 + 2, xT_hi, xT_lo, 4, 4)
            def mlp_hidden(e):
                dve.wait_ge(act_out, e + 1)
                dve.tensor_tensor(tile(1), tile(0), tile(0), ALU.mult).then_inc(ffn_h, 1)

            mlp_hidden(0)
            with dve.Fori(0, FF_TILES - 1) as e:
                lo(e * 2 + T_MLP, yT_hi, yT_lo, 0, 4)
                mlp_hidden(e + 1)
            lo(T_MLP + 2 * (FF_TILES - 1), yT_hi, yT_lo, 0, 4)
            gated_residual(5, done(U_LAYERS))
            dve.wait_ge(sumsq_ready, 3)
            dve.wait_ge(normf_loaded, 16)
            rstd(3, sm[:, 16:18], 1.0 / D, 1e-6)
            for t in range(TOK):
                dve.scalar_tensor_tensor(x_sb[:, t, :], x_sb[:, t, :], sm[:, 16 + t:17 + t], W[:, D:2 * D], ALU.mult, ALU.mult)
            dve.wait_ge(pos_loaded, 32)
            pos, ang, turns = sm[:, 18:20], sm[:, 128:160], sm[:, 160:192]
            dve.tensor_copy(pos, pos_i[:, :])
            dep()
            for t in range(TOK):
                dve.tensor_scalar(ang[:, t * 16:(t + 1) * 16], inv_row, pos[:, t:t + 1], None, ALU.mult)
            dep()
            big = 1.5 * 2.0 ** 23
            c2 = float(np.float32(2 * np.pi - 6.28125))
            c3 = 2 * np.pi - 6.28125 - c2
            for quarter, dst in ((0.0, sm[:, 64:96]), (0.25, sm[:, 96:128])):
                dve.tensor_scalar(turns, ang, 1 / (2 * np.pi), quarter, ALU.mult, ALU.add)
                dep()
                dve.tensor_scalar(turns, turns, big, None, ALU.add)
                dep()
                dve.tensor_scalar(turns, turns, big, None, ALU.subtract)
                dep()
                dve.scalar_tensor_tensor(dst, turns, -6.28125, ang, ALU.mult, ALU.add)
                dep()
                dve.scalar_tensor_tensor(dst, turns, -c2, dst, ALU.mult, ALU.add)
                dep()
                dve.scalar_tensor_tensor(dst, turns, -c3, dst, ALU.mult, ALU.add)
                dep()
                dve.tensor_scalar(dst, dst, quarter * 2 * np.pi, 3.1415925, ALU.add, ALU.min)
                dep()
                i = dve.tensor_scalar(dst, dst, -3.1415925, None, ALU.max)
                if quarter == 0.0:
                    dep()
            i.then_inc(ang_ready, 1)
            dve.wait_ge(trig_ready, 1)
            dve.memset(sm[:, 893:894], 0.0).then_inc(x_ready, 1)

            def layer_norm(n, g, b, out_sem):
                dep()
                xh = x_sb[:, :, :].rearrange("p t (c n) -> p t c n", n=NT)
                for t in range(TOK):
                    for c in range(2):
                        dve.bn_stats(bst[:, 2 * t + c, :], xh[:, t, c, :])
                dep()
                for t in range(TOK):
                    dve.bn_aggr(mv[:, t, :], bst[:, 2 * t:2 * t + 2, :])
                dep()
                dve.tensor_copy(sm[:, 16:18], mv[:, 0:2, 1])
                rstd(n, sm[:, 16:18], 1.0, 1e-5)
                for t in range(TOK):
                    dve.tensor_scalar(x_sb[:, t, :], x_sb[:, t, :], mv[:, t, 0:1], sm[:, 16 + t:17 + t], ALU.subtract, ALU.mult)
                dep()
                dve.tensor_tensor(x_sb[:, :, :], x_sb[:, :, :], wide(row2[g]), ALU.mult)
                dep()
                dve.tensor_tensor(x_sb[:, :, :], x_sb[:, :, :], wide(row2[b]), ALU.add).then_inc(out_sem, 1)

            def rope(x1, x2, t1, t2, c, s):
                dve.tensor_tensor(t1, x1, s, ALU.mult)
                dve.tensor_tensor(t2, x2, s, ALU.mult)
                dep()
                dve.tensor_tensor(x1, x1, c, ALU.mult)
                dve.tensor_tensor(x2, x2, c, ALU.mult)
                dep()
                dve.tensor_tensor(x1, x1, t2, ALU.subtract)
                return dve.tensor_tensor(x2, x2, t1, ALU.add)

            def first_max(v, m, hot):
                dve.tensor_reduce(m, v, AX.X, ALU.max)
                dep()
                dve.tensor_tensor(hot, v, m.to_broadcast([P, TOK, 4]), ALU.is_ge)
                dep()
                dve.tensor_tensor(hot, hot, wide(wt4), ALU.mult)
                dep()
                dve.tensor_reduce(r_w[:, :, 0:1], hot, AX.X, ALU.max)
                dep()
                dve.tensor_tensor(hot, hot, r_w[:, :, 0:1].to_broadcast([P, TOK, 4]), ALU.is_equal)
                dep()

            with dve.Fori(0, LAYERS) as l:
                n = l * L_UNITS + U_LAYERS
                tb = l * LT + T_LAYERS
                r = l * LR + R_LAYERS
                lo(tb + LT_X, xT_hi, xT_lo, 0, 4)
                lo(tb + (LT_X + 2), xT_hi, xT_lo, 4, 4)

                def in_tile(j):
                    read_tile(P2[:, :, j * NT:(j + 1) * NT], (G, AC)[j % 2], n + done(L_IN + (j + 1) * UP))

                in_tile(0)
                dep()
                dve.wait_ge(rows_loaded, l * 32 + 32)
                dve.tensor_tensor(GT, P2[:, :, IN2["mg"]:IN2["mg"] + 24], wide(row2["gate_bias"]), ALU.add)
                dep()
                dve.tensor_scalar(SI[:, :, 0:4], GT[:, :, 4:8], -1.0, None, ALU.mult)
                dve.tensor_scalar(SI[:, :, 4:8], GT[:, :, 12:16], -1.0, None, ALU.mult)
                dve.tensor_copy(SI[:, :, 8:16], GT[:, :, 16:24])
                dep()
                dve.scalar_tensor_tensor(sp_e, SI, -1.0, SI, ALU.mult, ALU.min).then_inc(sp_in, 1)
                dve.wait_ge(mla_sumsq, l + 1)
                dve.tensor_scalar(sm[:, 200:202], sm[:, 200:202], 1.0 / 256, 1e-6, ALU.mult, ALU.add)
                rstd(r, sm[:, 202:204], 1.0 / 128, 1e-6)
                dve.reciprocal(sm[:, 200:202], sm[:, 200:202])
                in_tile(1)
                dep()
                for t in range(TOK):
                    dve.scalar_tensor_tensor(P2[:, t, 0:256], P2[:, t, 0:256], sm[:, 200 + t:201 + t], row2["q_norm"], ALU.mult, ALU.mult)
                    i = dve.scalar_tensor_tensor(P2[:, t, 256:384], P2[:, t, 256:384], sm[:, 202 + t:203 + t], row2["kv_norm"], ALU.mult, ALU.mult)
                i.then_inc(cq_ready, 1)
                for j in range(2, N_IN2):
                    in_tile(j)
                dve.wait_ge(sp_exp, l + 1)
                dve.tensor_scalar(w_sp, sp_e, 2.0, None, ALU.add)
                dep()
                dve.reciprocal(w_sp, w_sp)
                dep()
                dve.tensor_tensor(z_sp, sp_e, w_sp, ALU.mult)
                dep()
                dve.tensor_tensor(w_sp, z_sp, z_sp, ALU.mult)
                dep()
                dve.tensor_scalar(q_sp, w_sp, 1.0 / 17, 1.0 / 15, ALU.mult, ALU.add)
                dep()
                for k in (13, 11, 9, 7, 5, 3, 1):
                    dve.tensor_tensor(q_sp, q_sp, w_sp, ALU.mult)
                    dep()
                    dve.tensor_scalar(q_sp, q_sp, 1.0 / k, None, ALU.add)
                    dep()
                dve.scalar_tensor_tensor(q_sp, q_sp, 2.0, z_sp, ALU.mult, ALU.mult)
                dep()
                dve.scalar_tensor_tensor(SP, SI, 0.0, q_sp, ALU.max, ALU.add)
                dep()
                dve.tensor_scalar(cu[:, :, 0:8], SP[:, :, 0:8], -1.0, None, ALU.mult)
                dve.scalar_tensor_tensor(cu[:, :, 8:16], SP[:, :, 8:16], -1.0, wide(ea), ALU.mult, ALU.mult).then_inc(cum_in, 1)
                lo(tb + LT_MLA, yT_hi, yT_lo, 0, 3)
                dve.wait_ge(unit_used, n + done(L_UKV))
                for t in range(TOK):
                    dve.tensor_copy(Q[:, t, :], AC_tok[:, t, 0:MH * QD])
                dep()
                qh = Q.rearrange("p t (h d) -> p t h d", d=QD)
                t1, t2 = [scr[:, b, 0:256].rearrange("p (t h n) -> p t h n", t=TOK, h=MH) for b in range(2)]
                hr = ROPE // 2
                rope(qh[:, :, :, NOPE:NOPE + hr], qh[:, :, :, NOPE + hr:QD], t1, t2,
                     *[v.unsqueeze(2).to_broadcast([P, TOK, MH, hr]) for v in (cosM, sinM)]).then_inc(q_ready, 1)
                dep()
                kr = P2[:, :, IN2["kr"]:IN2["kr"] + ROPE]
                rope(kr[:, :, 0:hr], kr[:, :, hr:ROPE], scr[:, 0, 0:32].rearrange("p (t n) -> p t n", t=TOK),
                     scr[:, 1, 0:32].rearrange("p (t n) -> p t n", t=TOK), cosM, sinM)
                dep()
                dve.wait_ge(kv_out, l * TOK + TOK)
                dve.tensor_copy(KF.rearrange("p t (h d) -> p t h d", d=QD)[:, :, :, NOPE:QD],
                                kr.unsqueeze(2).to_broadcast([P, TOK, MH, ROPE])).then_inc(kv_ready, 1)
                dve.wait_ge(cum_ready, l + 1)
                for d in range(2):
                    dve.tensor_copy(cs.rearrange("p t (k d h) -> p t k d h", k=2, d=2)[:, :, :, d, :],
                                    G[:, 0, 32 * d:32 * d + 32].rearrange("p (t k d h) -> p t k d h", t=TOK, k=2, d=2)[:, :, :, d, :])
                dep()
                for d in range(2):
                    dve.tensor_tensor(rw[:, :, 4 * d:4 * d + 4], GT[:, :, 8 * d:8 * d + 4], cs[:, :, 4 * d:4 * d + 4], ALU.subtract)
                dve.tensor_copy(rw[:, :, 8:16], cs[:, :, 8:16])
                dve.tensor_scalar(ncs.rearrange("p (t c) -> p t c", t=TOK), cs[:, :, 8:16], -1.0, None, ALU.mult).then_inc(rows_w, 1)

                def mla_eT(h):
                    dve.wait_ge(meT_ready, l * MH + (h + 1))
                    if h >= 2:
                        dve.wait_ge(mo_ready, l * MH + (h - 1))
                    dve.tensor_copy(meT[:, h % 2, :], T[:, h % 2, :]).then_inc(meT_out, 1)

                def mla_out(h):
                    dve.wait_ge(mo_ready, l * MH + (h + 1))
                    dve.reciprocal(mrden[:, 2 * h:2 * h + 2], mden[:, 2 * h:2 * h + 2])
                    dep()
                    dve.tensor_tensor(HB[:, :, h * MV:(h + 1) * MV], AC[:, h % 2, 0:2 * MV].rearrange("p (t n) -> p t n", t=TOK),
                                      mrden[:, 2 * h:2 * h + 2].unsqueeze(2).to_broadcast([P, TOK, MV]), ALU.mult).then_inc(mo_out, 1)

                for h in range(MH):
                    dve.wait_ge(ms_ready, l * MH + (h + 1))
                    dve.tensor_reduce(mmax[:, 2 * h:2 * h + 2], G[:, h % 2, :].rearrange("p (t n) -> p t n", t=TOK), AX.X, ALU.max)
                    dep()
                    dve.tensor_scalar(mnm[:, 2 * h:2 * h + 2], mmax[:, 2 * h:2 * h + 2], -QD ** -0.5, None, ALU.mult).then_inc(mmax_ready, 1)
                    if h >= 1:
                        mla_eT(h - 1)
                    if h >= 2:
                        mla_out(h - 2)
                mla_eT(MH - 1)
                mla_out(MH - 2)
                mla_out(MH - 1)
                by_c = [v.rearrange("p (t c) -> p t c", t=TOK) for v in (lMx, lfloor, lden)]
                dve.wait_ge(meT_out, l * MH + MH)
                for j in range(2 * LH):
                    dve.wait_ge(lrow_ready, l * 8 + (j + 1))
                    dve.tensor_tensor(lw[:, j, :, :], wide(G[:, j % 2, 0:S]), (mask_f, mask_b)[j % 2], ALU.add).then_inc(lrow_out, 1)
                dep()
                for j in range(2 * LH):
                    c = j % 2 * LH + j // 2
                    dve.tensor_reduce(by_c[0][:, :, c:c + 1], lw[:, j, :, :], AX.X, ALU.max)
                dep()
                dve.tensor_scalar(lnm, lMx, -1.0, None, ALU.mult)
                dve.tensor_tensor(by_c[1], by_c[0], cs[:, :, 0:8], ALU.add).then_inc(lmax_ready, 1)
                for j in range(2 * LH):
                    c, h = j % 2 * LH + j // 2, j // 2
                    dve.wait_ge(lexp_ready, l * 8 + (j + 1))
                    dve.wait_ge(lqk_ready, l * LH + (h + 1))
                    for t in range(TOK):
                        dve.scalar_tensor_tensor(lw[:, j, t, :], AC[:, h, t * S:(t + 1) * S], LDH ** -0.5, lw[:, j, t, :],
                                                 ALU.mult, ALU.mult, accum_out=lden[:, t * 8 + c:t * 8 + c + 1])
                dep()
                dve.scalar_tensor_tensor(lden, lden, -1.0, lden, ALU.mult, ALU.max)
                dep()
                dve.tensor_tensor(lden, lden, lfloor, ALU.max)
                dep()
                dve.reciprocal(lden, lden)
                dep()
                for h in range(LH):
                    for t in range(TOK):
                        kb = t * 8 + LH + h
                        dve.tensor_scalar(lw[:, 2 * h + 1, t, :], lw[:, 2 * h + 1, t, :], lden[:, kb:kb + 1], None, ALU.mult)
                    dep()
                    for t in range(TOK):
                        kf = t * 8 + h
                        i = dve.scalar_tensor_tensor(lw[:, 2 * h, t, :], lw[:, 2 * h, t, :], lden[:, kf:kf + 1], lw[:, 2 * h + 1, t, :], ALU.mult, ALU.add)
                    i.then_inc(lp_ready, 1)
                dve.wait_ge(lnum_ready, l * LH + LH)
                num = G[:, 0, :].rearrange("p (k n) -> p k n", n=LDH)
                cen8, csq8 = [v.rearrange("p (k n) -> p k n", n=LDH) for v in (cen, csq)]
                dve.tensor_reduce(lsum, num, AX.X, ALU.add)
                dep()
                dve.tensor_scalar(lsum, lsum, -1.0 / LDH, None, ALU.mult)
                dep()
                dve.tensor_tensor(cen8, num, lsum.unsqueeze(2).to_broadcast([P, 8, LDH]), ALU.add)
                dep()
                dve.tensor_tensor(csq, cen, cen, ALU.mult)
                dep()
                dve.tensor_reduce(sm[:, 64:72], csq8, AX.X, ALU.add)
                rstd(r + 1, sm[:, 64:72], 1.0 / LDH, 1e-5)
                dve.tensor_tensor(cen8, cen8, sm[:, 64:72].unsqueeze(2).to_broadcast([P, 8, LDH]), ALU.mult)
                dep()
                cen2 = cen.rearrange("p (t n) -> p t n", t=TOK)
                dve.tensor_tensor(cen2, cen2, wide(row2["mlstm_norm"]), ALU.mult)
                dep()
                dve.wait_ge(lgate, l + 1)
                dve.tensor_tensor(HB[:, :, 512:768], cen2, P2[:, :, IN2["mo"]:IN2["mo"] + 256], ALU.mult)
                dve.memset(xpad[:, :, 0:2], 0.0)
                dve.memset(xpad[:, :, S + 2:S + 4], 0.0)
                dep()
                dve.wait_ge(sx_out, l * 3 + 3)
                for k in range(CONV):
                    for c in range(XBC_CH):
                        src = xpad[:, c, k:k + S]
                        if k == 0:
                            dve.tensor_scalar(xc[:, c, :], src, cv_w[:, c, 0:1], None, ALU.mult)
                        else:
                            i = dve.scalar_tensor_tensor(xc[:, c, :], src, cv_w[:, c, k:k + 1], xc[:, c, :], ALU.mult, ALU.add)
                    if k < CONV - 1:
                        dep()
                i.then_inc(conv_done, 1)
                for j in range(2 * SH):
                    dve.wait_ge(srow_ready, l * 8 + (j + 1))
                    dve.tensor_tensor(sw[:, j, :, :], wide(AC[:, 2 + j % 2, 0:S]), (mask_b, mask_f)[j % 2], ALU.add).then_inc(srow_out, 1)
                    if j == 0:
                        dve.wait_ge(sxt_T, l + 1)
                        dve.tensor_copy(XT, T[:, 0, :].rearrange("p (t n) -> p t n", t=TOK))
                dep()
                xh = XT.rearrange("p t (h n) -> p t h n", h=SH)
                for d in range(2):
                    dve.tensor_tensor(xdt[:, :, d, :].rearrange("p t (h n) -> p t h n", h=SH), xh,
                                      SP[:, :, 8 + 4 * d:12 + 4 * d].unsqueeze(3).to_broadcast([P, TOK, SH, SP_]), ALU.mult)
                dep()
                dve.wait_ge(scb_ready, l * SG + SG)
                for j in range(2 * SH):
                    dve.wait_ge(sexp_ready, l * 8 + (j + 1))
                    dve.tensor_tensor(sw[:, j, :, :], sw[:, j, :, :], AC[:, j // 4, :].rearrange("p (t n) -> p t n", t=TOK), ALU.mult)\
                       .then_inc(sw_ready, 1)
                dve.wait_ge(conv_act, l + 1)
                ysh = ys.rearrange("p t (h n) -> p t h n", h=SH)
                dve.tensor_tensor(ysh, xh, row2["d_skip"].unsqueeze(1).unsqueeze(3).to_broadcast([P, TOK, SH, SP_]), ALU.mult)
                dep()
                dve.wait_ge(sy_ready, l * SH + SH)
                dve.tensor_tensor(ys, ys, T[:, 1, :].rearrange("p (t n) -> p t n", t=TOK), ALU.add).then_inc(sy_out, 1)
                dep()
                dve.tensor_tensor(ys, ys, P2[:, :, IN2["z"]:IN2["z"] + 256], ALU.mult)
                dep()
                dve.tensor_tensor(ysq, ys, ys, ALU.mult)
                dep()
                dve.tensor_reduce(sm[:, 64:68], ysq.rearrange("p t (g n) -> p (t g) n", g=SG), AX.X, ALU.add)
                rstd(r + 2, sm[:, 64:68], 1.0 / P, 1e-6)
                ysg = ys.rearrange("p t (g n) -> p (t g) n", g=SG)
                dve.tensor_tensor(ysg, ysg, sm[:, 64:68].unsqueeze(2).to_broadcast([P, 4, P]), ALU.mult)
                dep()
                dve.tensor_tensor(HB[:, :, 768:1024], ys, wide(row2["ssd_norm"]), ALU.mult).then_inc(heads_ready, 1)
                lo(tb + LT_OUT, yT_hi, yT_lo, 0, 4)
                lo(tb + (LT_OUT + 2), yT_hi, yT_lo, 0, 4)
                dve.wait_ge(unit_used, n + done(L_ROUTER))
                dve.scalar_tensor_tensor(x_sb[:, :, :], x_sb[:, :, :], ALPHA, AC_tok, ALU.mult, ALU.add).then_inc(acc_free, 1)
                layer_norm(r + 3, "ln1_g", "ln1_b", x2_ready)
                lo(tb + LT_X2, xT_hi, xT_lo, 0, 4)
                lo(tb + (LT_X2 + 2), xT_hi, xT_lo, 4, 4)
                dve.wait_ge(unit_used, n + done(L_MOE))
                dve.tensor_tensor(rlog, G[:, :, 0:EGROUPS + EXPERTS], wide(row2["router_b"]), ALU.add).then_inc(g_free, 1)
                dep()
                first_max(rlog[:, :, 0:4], r_m[:, :, 0:1], r_g)
                dve.tensor_tensor(rt_e[:, :, 0:4], rlog[:, :, 0:4], r_m[:, :, 0:1].to_broadcast([P, TOK, 4]), ALU.subtract)
                dve.tensor_tensor(r_pr, rlog[:, :, 4:20].rearrange("p t (g e) -> p t g e", g=EGROUPS),
                                  r_g.unsqueeze(3).to_broadcast([P, TOK, EGROUPS, EPG]), ALU.mult)
                dep()
                dve.tensor_reduce(r_el, r_pr.rearrange("p t g e -> p t e g"), AX.X, ALU.add)
                dep()
                first_max(r_el, r_m[:, :, 0:1], r_1)
                dve.scalar_tensor_tensor(r_el2, r_1, NEG, r_el, ALU.mult, ALU.add)
                dep()
                first_max(r_el2, r_m[:, :, 1:2], r_2)
                dve.tensor_tensor(rt_e[:, :, 4:5], r_m[:, :, 1:2], r_m[:, :, 0:1], ALU.subtract).then_inc(gexp_in, 1)
                dve.wait_ge(gexp_out, l + 1)
                dve.tensor_reduce(r_w[:, :, 0:1], rt_e[:, :, 0:4], AX.X, ALU.add)
                dve.tensor_scalar(r_w[:, :, 1:2], rt_e[:, :, 4:5], 1.0, None, ALU.add)
                dep()
                dve.tensor_tensor(r_w[:, :, 2:3], r_w[:, :, 0:1], r_w[:, :, 1:2], ALU.mult)
                dep()
                dve.reciprocal(r_w[:, :, 2:3], r_w[:, :, 2:3])
                dve.tensor_tensor(r_2, r_2, rt_e[:, :, 4:5].to_broadcast([P, TOK, 4]), ALU.mult)
                dep()
                dve.tensor_tensor(r_1, r_1, r_2, ALU.add)
                dep()
                dve.tensor_tensor(r_1, r_1, r_w[:, :, 2:3].to_broadcast([P, TOK, 4]), ALU.mult)
                dep()
                dve.tensor_tensor(comb.rearrange("p (t g e) -> p t g e", t=TOK, g=EGROUPS),
                                  r_g.unsqueeze(3).to_broadcast([P, TOK, EGROUPS, EPG]),
                                  r_1.unsqueeze(2).to_broadcast([P, TOK, EGROUPS, EPG]), ALU.mult)
                dep()

                def moe_hidden(e0, e):
                    dve.wait_ge(act_out, l * EXPERTS + e0 + (FF_TILES + e + 1))
                    for t in range(TOK):
                        i = dve.scalar_tensor_tensor(moe_h[:, t, :], ffn_a[:, t, :], comb[:, bass.ds(e0 + (t * EXPERTS + e), 1)],
                                                     G[:, t, DE:2 * DE], ALU.mult, ALU.mult)
                    i.then_inc(ffn_h, 1)

                moe_hidden(0, 0)
                with dve.Fori(0, 3) as e4:
                    for q in range(4):
                        lo(e4 * 8 + (tb + (LT_MOE + 2 * q)), yT_hi, yT_lo, 0, 2)
                        moe_hidden(e4 * 4, q + 1)
                for e in range(12, EXPERTS):
                    lo(tb + (LT_MOE + 2 * e), yT_hi, yT_lo, 0, 2)
                    if e + 1 < EXPERTS:
                        moe_hidden(0, e + 1)
                dve.wait_ge(unit_used, n + done(L_UNITS))
                dve.scalar_tensor_tensor(x_sb[:, :, :], x_sb[:, :, :], ALPHA, AC_tok, ALU.mult, ALU.add).then_inc(acc_free, 1)
                layer_norm(r + 4, "ln2_g", "ln2_b", x_ready)


def up_units(w):
    n = w.shape[1] // NT
    return w.reshape(UP, 2, P, n, NT).transpose(3, 0, 2, 1, 4).reshape(n * UP, P, UNIT)


def down_units(w):
    return w.reshape(-1, P, UNIT)


def padded(w, cols):
    return np.concatenate([w, np.zeros(w.shape[:-1] + (cols - w.shape[-1],), np.float32)], axis=-1)


def ffn_units(ups, downs):
    parts = [ups[0]]
    for e in range(len(ups)):
        if e + 1 < len(ups):
            parts.append(ups[e + 1])
        parts.append(downs[e])
    return parts


def weight_stream(a):
    w_in = a["w_in"][0]
    cols = np.split(w_in, [N_RET_IN * NT, (N_RET_IN + N_ATT_IN) * NT], axis=1)
    parts = [up_units(a["w_ada"][0]), up_units(cols[0]), down_units(a["w_ret_out"][0]), up_units(cols[1]),
             up_units(cols[2]), down_units(a["w_att_out"][0]), down_units(a["w_o"][0])]
    ff1 = up_units(a["w_ff1"][0]).reshape(FF_TILES, UP, P, UNIT)
    ff2 = down_units(a["w_ff2"][0]).reshape(FF_TILES, 4, P, UNIT)
    parts += ffn_units(ff1, ff2)
    for l in range(LAYERS):
        w = a["w_in_2"][l]
        at, sizes = {}, (("cq", 256), ("ckv", 128), ("kr", 32), ("mq", 256), ("mk", 256), ("mv", 256), ("mo", 256),
                         ("mg", 16), ("z", 256), ("xbc", XBC), ("dt", 8))
        c = 0
        for name, n in sizes:
            at[name] = w[:, c:c + n]
            c += n
        first = padded(np.concatenate([at[k] for k in ("cq", "ckv", "kr", "mg", "dt")], axis=1), NT)
        rest = np.concatenate([at[k] for k in ("mq", "mk", "mv", "mo", "xbc", "z")], axis=1)
        parts.append(up_units(np.concatenate([first, rest], axis=1)))
        parts.append(padded(a["mla_w_uq_2"][l].reshape(2, P, MH * QD), UNIT))
        parts.append(a["mla_w_ukv_2"][l].reshape(1, P, UNIT))
        parts.append(down_units(a["w_out_2"][l]))
        we = a["router_expert_w_2"][l].transpose(1, 0, 2).reshape(D, EXPERTS)
        router = np.concatenate([a["router_group_w_2"][l], we], axis=1)
        parts.append(padded(router.reshape(KC, P, -1).transpose(1, 0, 2).reshape(1, P, -1), UNIT))
        both = np.concatenate([a["expert_w_gate_2"][l], a["expert_w_up_2"][l]], axis=2)
        parts += ffn_units([up_units(w) for w in both], [down_units(w) for w in a["expert_w_down_2"][l]])
    units = np.concatenate(parts, axis=0)
    return np.ascontiguousarray(units.reshape(UNITS // PIECE, PIECE, P, UNIT).transpose(0, 2, 1, 3)).reshape(-1, P, PIECE * UNIT)


def bucket_of(dist):
    exact = BUCKETS // 2
    d = np.maximum(dist, 1).astype(np.float32)
    scale = np.float32(np.log(MAX_DIST / exact))
    large = exact + (np.log(d / np.float32(exact)) / scale * np.float32(BUCKETS - exact)).astype(np.int32)
    return np.where(dist < exact, dist, np.minimum(large, BUCKETS - 1))


def shape_constants():
    f = np.float32
    idx = np.arange(P, dtype=f)
    log_g = np.log1p(-(2.0 ** (-5.0 - np.arange(RH))))
    s, t = np.arange(P)[:, None], np.arange(S)[None, :]
    dec = np.where(t >= s, np.exp(log_g[:, None, None] * np.maximum(t - s, 0)), 0.0) * RDK ** -0.5
    decay = np.concatenate([dec, dec[:, :, 0:P]], axis=2).transpose(1, 0, 2).reshape(P, -1).astype(f)
    half = RDK // 2
    inv = f(10000.0) ** (-np.arange(half, dtype=f) / f(half))
    ang = np.arange(S, dtype=f)[:, None] * inv[None, :]
    by_p = lambda v: v.reshape(TOK, P, half).transpose(1, 0, 2).reshape(P, -1).astype(f)
    const1 = np.concatenate([decay, by_p(np.cos(ang)), by_p(np.sin(ang))], axis=1)
    onehot = np.zeros((BUCKETS + 1, len(GROUPS), NT), f)
    for g, (win, dil) in enumerate(GROUPS):
        for c in range(NT):
            d = S - 1 - c
            ok = 0 <= d <= win and d % dil == 0
            onehot[bucket_of(np.array([d]))[0] if ok else BUCKETS, g, c] = 1.0
    u, v = np.arange(P)[:, None], np.arange(P)[None, :]
    tri_f, tri_b = (u <= v).astype(f), (u >= v).astype(f)
    first, second = np.arange(S)[:, None], np.arange(S)[None, :]
    tiles = lambda m: m.reshape(TOK, P, S).transpose(1, 0, 2).reshape(P, -1)
    mask_f = tiles(np.where(second <= first, 0.0, NEG).astype(f))
    mask_b = tiles(np.where(second >= first, 0.0, NEG).astype(f))
    const2 = np.concatenate([tri_f, tri_b, np.ones((P, P), f), mask_f, mask_b], axis=1)
    select = np.zeros((16, 16, P), f)
    for c in range(16):
        select[c, c, :] = 1.0
    hr = ROPE // 2
    inv_freq = f(10000.0) ** (-np.arange(0, ROPE, 2, dtype=f) / f(ROPE))
    return {"identity": np.eye(P, dtype=f), "const1": const1, "onehot": onehot.reshape(BUCKETS + 1, -1), "const2": const2,
            "row_select": select.reshape(16, -1), "inv_freq": inv_freq.astype(f).reshape(hr)}


def kernel(**inputs):
    import concourse.bacc as bacc
    from concourse.bass_utils import run_bass_kernel_spmd

    a = {k: np.asarray(v) for k, v in inputs.items()}
    arrays = shape_constants()
    arrays["w_stream"] = weight_stream(a)
    arrays["c_col"] = a["c"].reshape(KC, P).T
    arrays["x"] = a["x"]
    arrays["rel_bias"] = a["rel_bias"]
    arrays["b_ada"] = a["b_ada"].reshape(-1)
    for name, src in (("norm1_g", "norm1_g"), ("norm2_g", "norm2_g"), ("norm_f_g", "norm_f_g"), ("gn_g", "ret_gn_g"), ("gn_b", "ret_gn_b")):
        arrays[name] = a[src].reshape(-1)
    arrays["pos_col"] = a["positions_2"].reshape(TOK, P).T
    rows = [np.concatenate([a[n][l].reshape(-1) for n in
                            ("ln1_g_2", "ln1_b_2", "ln2_g_2", "ln2_b_2", "mla_q_norm_2", "mla_kv_norm_2", "mlstm_gate_bias_2",
                             "ssd_dt_bias_2", "ssd_a_log_2", "ssd_d_2", "ssd_norm_2", "mlstm_norm_2", "router_group_b_2",
                             "router_expert_b_2")]) for l in range(LAYERS)]
    arrays["rows2"] = np.stack(rows)
    conv = [np.concatenate([a["ssd_conv_w_2"][l].T.reshape(XBC_CH, P, CONV).transpose(1, 0, 2).reshape(P, -1),
                            a["ssd_conv_b_2"][l].reshape(XBC_CH, P).T], axis=1) for l in range(LAYERS)]
    arrays["conv_col"] = np.stack(conv)
    arrays = {n: np.ascontiguousarray(v) for n, v in arrays.items()}

    nc = bacc.Bacc("TRN2", target_bir_lowering=False, num_devices=1)
    A = {n: nc.dram_tensor(n, v.shape, mybir.dt.from_np(v.dtype), kind="ExternalInput").ap() for n, v in arrays.items()}
    A["rel_scratch"] = nc.dram_tensor("rel_scratch", (N_AH, P + 1, NT), F32, kind="Internal").ap()
    A["out"] = nc.dram_tensor("out", a["x"].shape, F32, kind="ExternalOutput").ap()
    program(nc, A)
    r = run_bass_kernel_spmd(nc, [arrays], core_ids=[0])
    return r.results[0]["out"]
```

```python
from contextlib import ExitStack

import concourse.bass as bass
import numpy as np
from concourse import mybir

F32 = mybir.dt.float32
F32R = mybir.dt.float32r
I32 = mybir.dt.int32
ALU = mybir.AluOpType
ACT = mybir.ActivationFunctionType
AX = mybir.AxisListType

P = 128
S = 256
TOK = S // P
D = 1024
KC = D // P
NT = 512
RH, RDK, RDV = 4, 256, 512
GROUPS = ((128, 1), (512, 4), (2048, 16))
AH, ADH = 4, 128
N_AH = len(GROUPS) * AH
BUCKETS, MAX_DIST = 32, 2048
FF_TILES = 4096 // NT
LAYERS = 2
MH, NOPE, ROPE, MV = 8, 64, 32, 64
QD = NOPE + ROPE
LH, LDH = 4, 64
SH, SP_, SG, SN = 4, 64, 2, 128
CONV = 5
XBC = SH * SP_ + 2 * SG * SN
XBC_CH = XBC // P
EXPERTS, EGROUPS, EPG = 16, 4, 4
DE = 256
ALPHA = (2 * LAYERS) ** 0.25
NEG = -1e30

UNIT = 1024
SLOTS = 4
RAW = 8
PIECE = 2
UP = 4
N_RET_IN = 12
N_ATT_IN = 9
N_GATE = 4
U_RET_IN = 0
U_ATT_FIRST = U_RET_IN + N_RET_IN * UP
U_RET_OUT = U_ATT_FIRST + UP
U_ATT_IN = U_RET_OUT + RH * 4
U_GATE = U_ATT_IN + (N_ATT_IN - 1) * UP
U_ATT_OUT = U_GATE + N_GATE * UP
U_WO = U_ATT_OUT + 4
U_MLP = U_WO + 8
U_LAYERS = U_MLP + FF_TILES * 8
ADA_BEFORE = (0, 0, 1, 3, 5, 8)
N_ADA = len(ADA_BEFORE)
assert KC == RAW
L_IN = 0
N_IN2 = 5
L_UQ = L_IN + N_IN2 * UP
L_UKV = L_UQ + 2
L_OUT = L_UKV + 1
L_ROUTER = L_OUT + 8
L_MOE = L_ROUTER + 1
L_UNITS = L_MOE + EXPERTS * 6
UNITS = U_LAYERS + LAYERS * L_UNITS
assert UNITS % RAW == 0 and L_UNITS % RAW == 0 and U_LAYERS % RAW == 0

M_ATT_IN = 8
M_LAYERS = M_ATT_IN + N_ATT_IN
LM_ROUTER = N_IN2
LM = LM_ROUTER + 1
T_H1 = 0
T_RET = T_H1 + 4
T_ATT = T_RET + 4 * RH
T_MERGE = T_ATT + 4
T_H2 = T_MERGE + 8
T_MLP = T_H2 + 4
T_LAYERS = T_MLP + 2 * FF_TILES
LT_X = 0
LT_MLA = LT_X + 4
LT_OUT = LT_MLA + 2
LT_X2 = LT_OUT + 8
LT_MOE = LT_X2 + 4
LT = LT_MOE + 2 * EXPERTS
R_GN = 1
R_NORM2 = R_GN + RH
R_FINAL = R_NORM2 + 1
R_LAYERS = R_FINAL + 1
LR = 5
C_LAYERS = 4
LC = 2
G_CREDIT = 2

ROW2 = {}
_at = 0
for _n, _w in (("ln1_g", D), ("ln1_b", D), ("ln2_g", D), ("ln2_b", D), ("q_norm", 256), ("kv_norm", 128),
               ("gate_bias", 24), ("a_log", 8), ("d_skip", 4), ("ssd_norm", 256), ("mlstm_norm", 256),
               ("router_b", 20)):
    ROW2[_n] = (_at, _at + _w)
    _at += _w
ROWS2 = _at

IN2 = {"cq": 0, "ckv": 256, "kr": 384, "mg": 416, "dt": 432, "mq": 512, "mk": 768, "mv": 1024, "mo": 1280,
       "xbc": 1536, "z": 2304}


POS0 = U_ATT_IN + 2 * UP
N_POS = U_ATT_OUT - POS0
PER_GROUP = 3 * UP


def head_at(p, after):
    q = p - after
    g, h = q // PER_GROUP, q % PER_GROUP // 2
    return g * AH + h if q >= 0 and q % 2 == 0 and g < len(GROUPS) and h < AH else None


def turn_at(p):
    g, n = (p + UP) // PER_GROUP, (p + UP) % PER_GROUP
    return (g, n) if n < 4 and g < len(GROUPS) else None


def ring_round(r):
    return r + sum(b <= r for b in ADA_BEFORE)


def ada_round(i):
    return i + ADA_BEFORE[i]


def program(nc, A):
    ctx = ExitStack()
    with ctx:
        def sb(name, shape, dt=F32):
            return ctx.enter_context(nc.sbuf_tensor(name, shape, dt))

        def pb(name, shape):
            return ctx.enter_context(nc.psum_tensor(name, shape, F32))

        def sem(name):
            return ctx.enter_context(nc.semaphore(name))

        w_raw = sb("w_raw", [P, RAW, UNIT])
        w_hi = sb("w_hi", [P, SLOTS, UNIT], F32R)
        w_lo = sb("w_lo", [P, SLOTS, UNIT], F32R)
        xT_hi = sb("xT_hi", [P, KC, S], F32R)
        xT_lo = sb("xT_lo", [P, KC, S], F32R)
        yT_hi = sb("yT_hi", [P, 4, S], F32R)
        yT_lo = sb("yT_lo", [P, 4, S], F32R)
        zero_r = sb("zero_r", [1, P], F32R)
        x_sb = sb("x_sb", [P, TOK, D])
        mod = sb("mod", [P, 6 * D])
        ident = sb("ident", [P, P])
        arena = sb("arena", [P, 20480])
        scr = sb("scr", [P, 2, 384])
        sm = sb("sm", [P, 896])
        pos_i = sb("pos_i", [P, TOK], I32)
        G = pb("G", [P, 2, NT])
        AC = pb("AC", [P, 4, NT])
        T = pb("T", [P, 2, NT])
        AC_tok = AC[:, :, :].rearrange("p (t c) n -> p t (c n)", t=TOK)

        raw_landed = [sem("raw_landed%d" % s) for s in range(RAW // PIECE)]
        c_loaded = sem("c_loaded")
        x_loaded = sem("x_loaded")
        norm1_loaded = sem("norm1_loaded")
        ada_used = sem("ada_used")
        cst_loaded = sem("cst_loaded")
        pos_loaded = sem("pos_loaded")
        lo_ready = sem("lo_ready")
        x_ready = sem("x_ready")
        out_stored = sem("out_stored")
        mod_cleared_b = sem("mod_cleared_b")
        hi_ready = sem("hi_ready")
        unit_used = sem("unit_used")
        t_ready = sem("t_ready")
        t_hi = sem("t_hi")
        var_ready = sem("var_ready")
        std_ready = sem("std_ready")
        sumsq_ready = sem("sumsq_ready")
        act_out = sem("act_out")
        mod_sum = sem("mod_sum")
        mod_out = sem("mod_out")
        bias_in_loaded = sem("bias_in_loaded")
        mod_cleared_a = sem("mod_cleared_a")
        ada_b_loaded = sem("ada_b_loaded")
        ada_b2_loaded = sem("ada_b2_loaded")
        c_ready = sem("c_ready")
        bias_row = sem("bias_row")
        bias_rows_out = sem("bias_rows_out")
        bias_stored = sem("bias_stored")
        h_ready = sem("h_ready")
        gn_g_loaded = sem("gn_g_loaded")
        gn_b_loaded = sem("gn_b_loaded")
        rqk_ready = sem("rqk_ready")
        rqk_out = sem("rqk_out")
        ro_ready = sem("ro_ready")
        ro_out = sem("ro_out")
        rg_gated = sem("rg_gated")
        y_ready = sem("y_ready")
        rel_loaded = [sem("rel_loaded%d" % g) for g in range(len(GROUPS))]
        aqk_ready = sem("aqk_ready")
        aqk_out = sem("aqk_out")
        as_out = sem("as_out")
        aeT_ready = sem("aeT_ready")
        ae_ready = sem("ae_ready")
        ao_ready = sem("ao_ready")
        ao_out = sem("ao_out")
        lse_diff = sem("lse_diff")
        lse_exp = sem("lse_exp")
        gate_read = sem("gate_read")
        norm2_loaded = sem("norm2_loaded")
        normf_loaded = sem("normf_loaded")
        x1_ready = sem("x1_ready")
        ang_ready = sem("ang_ready")
        trig_ready = sem("trig_ready")
        cst2_loaded = sem("cst2_loaded")
        rows_loaded = sem("rows_loaded")
        g_free = sem("g_free")
        mla_sumsq = sem("mla_sumsq")
        sp_in = sem("sp_in")
        sp_exp = sem("sp_exp")
        kv_out = sem("kv_out")
        mqkT_ready = sem("mqkT_ready")
        mqkT_out = sem("mqkT_out")
        mmax_ready = sem("mmax_ready")
        meT_ready = sem("meT_ready")
        me_ready = sem("me_ready")
        rows_T = sem("rows_T")
        rows_out = sem("rows_out")
        lqk_T = sem("lqk_T")
        lqk_out = sem("lqk_out")
        lmax_ready = sem("lmax_ready")
        lexp_ready = sem("lexp_ready")
        lgate = sem("lgate")
        lpT_ready = sem("lpT_ready")
        lnum_ready = sem("lnum_ready")
        lpT_out = sem("lpT_out")
        sx_T = sem("sx_T")
        sx_out = sem("sx_out")
        conv_done = sem("conv_done")
        conv_act = sem("conv_act")
        srow_out = sem("srow_out")
        sexp_ready = sem("sexp_ready")
        gexp_in = sem("gexp_in")
        gexp_out = sem("gexp_out")
        t_lo = sem("t_lo")
        ffn_h = sem("ffn_h")
        tab_wide = sem("tab_wide")
        ada_summed = sem("ada_summed")
        rope_done = sem("rope_done")
        rs_out = sem("rs_out")
        rs_ready = sem("rs_ready")
        acc_free = sem("acc_free")
        aeT_out = sem("aeT_out")
        as_ready = sem("as_ready")
        att_ready = sem("att_ready")
        merged_ready = sem("merged_ready")
        zero_ready = sem("zero_ready")
        cq_ready = sem("cq_ready")
        cum_in = sem("cum_in")
        cum_ready = sem("cum_ready")
        q_ready = sem("q_ready")
        ms_ready = sem("ms_ready")
        meT_out = sem("meT_out")
        mo_out = sem("mo_out")
        mo_ready = sem("mo_ready")
        rows_w = sem("rows_w")
        lrow_out = sem("lrow_out")
        lrow_ready = sem("lrow_ready")
        lqk_ready = sem("lqk_ready")
        lp_ready = sem("lp_ready")
        sxt_T = sem("sxt_T")
        scb_ready = sem("scb_ready")
        srow_ready = sem("srow_ready")
        sw_ready = sem("sw_ready")
        sy_ready = sem("sy_ready")
        sy_out = sem("sy_out")
        heads_ready = sem("heads_ready")
        x2_ready = sem("x2_ready")
        kv_ready = sem("kv_ready")

        def slot(j, n=1):
            return arena[:, j * 1024:(j + n) * 1024].rearrange("p (j t n) -> p j t n", j=n, t=TOK)

        def tile(j):
            return arena[:, j * 1024:(j + 1) * 1024].rearrange("p (t n) -> p t n", t=TOK)

        qkT = arena[:, 12288:16384].rearrange("p (c s) -> p c s", s=S)
        W = arena[:, 16384:18432]
        decay = arena[:, 18432:19968].rearrange("p (h n) -> p h n", h=RH)
        cosR = arena[:, 19968:20224].rearrange("p (t n) -> p t n", t=TOK)
        sinR = arena[:, 20224:20480].rearrange("p (t n) -> p t n", t=TOK)
        onehot = arena[0:BUCKETS + 1, 0:1536].rearrange("p (g n) -> p g n", g=len(GROUPS))
        tab_bc = arena[0:BUCKETS + 1, 1536:3072].rearrange("p (h n) -> p h n", h=N_AH)
        tab = sm[0:BUCKETS + 1, 480:480 + N_AH]
        bias_vec = arena[:, 6144:12288].rearrange("p (h n) -> p h n", h=N_AH)
        h_sb = arena[:, 3072:5120].rearrange("p (t n) -> p t n", t=TOK)
        ones_a, ones_b = scr[:, 0, 0:P], arena[:, 9 * 1024 + 768:9 * 1024 + 896]
        ccol, csil = sm[:, 0:8], sm[:, 8:16]
        aqkT = [qkT[:, 8 * b:8 * b + 8, :] for b in range(2)]
        rel = [W[:, 0:1536], mod[:, 0:1536], arena[:, 18432:19968]]
        rel = [r.rearrange("p (h n) -> p h n", h=AH) for r in rel]
        a_e = arena[:, 9 * 1024:9 * 1024 + 768].rearrange("p (b n) -> p b n", b=2)
        a_eT = [W[:, 1536:1920], mod[:, 1536:1920]]
        amx, anm, aden = sm[:, 64:88], sm[:, 88:112], sm[:, 112:136]
        aM, adiff, afac, aD = sm[:, 136:144], sm[:, 144:168], sm[:, 168:192], sm[:, 192:200]

        P2 = arena[:, 0:5120].rearrange("p (t n) -> p t n", t=TOK)
        HB = arena[:, 5120:7168].rearrange("p (t n) -> p t n", t=TOK)
        WK = 7168
        tri_f, tri_b, ones = arena[:, 17024:17152], arena[:, 17152:17280], arena[:, 17280:17408]
        mask_f = arena[:, 17408:17920].rearrange("p (t n) -> p t n", t=TOK)
        mask_b = arena[:, 17920:18432].rearrange("p (t n) -> p t n", t=TOK)
        sel = arena[0:16, 18432:20480].rearrange("p (c n) -> p c n", c=16)
        row2 = {n: mod[:, a:b] for n, (a, b) in ROW2.items()}
        V2 = mod[:, ROWS2 + 8:ROWS2 + 8 + 1024].rearrange("p (t n) -> p t n", t=TOK)
        cvw = sm[:, 400:436]
        cv_w, cv_b = cvw[:, 0:30].rearrange("p (c k) -> p c k", k=CONV), cvw[:, 30:36]
        inv_row = sm[:, 436:452]
        cosM = sm[:, 368:400].rearrange("p (t n) -> p t n", t=TOK)
        sinM = sm[:, 860:892].rearrange("p (t n) -> p t n", t=TOK)

        Q = arena[:, WK:WK + 1536].rearrange("p (t n) -> p t n", t=TOK)
        KF = arena[:, WK + 1536:WK + 3072].rearrange("p (t n) -> p t n", t=TOK)
        mqT = arena[:, WK + 3072:WK + 5120].rearrange("p (h s) -> p h s", s=S)
        mkT = arena[:, WK + 5120:WK + 7168].rearrange("p (h s) -> p h s", s=S)
        me = arena[:, WK + 7168:WK + 8192].rearrange("p (b t s) -> p b t s", b=2, t=TOK)
        meT = arena[:, WK + 8192:WK + 9216].rearrange("p (b n) -> p b n", b=2)
        mmax, mnm, mden, mrden = sm[:, 64:80], sm[:, 80:96], sm[:, 96:112], sm[:, 112:128]
        lw = arena[:, WK:WK + 4096].rearrange("p (j t s) -> p j t s", j=2 * LH, t=TOK)
        lqkT = arena[:, WK + 4096:WK + 5120].rearrange("p (c s) -> p c s", s=S)
        lpT = arena[:, WK + 5120:WK + 6144].rearrange("p (b n) -> p b n", b=2)
        cen = arena[:, WK + 6400:WK + 6912]
        csq = arena[:, WK + 6912:WK + 7424]
        rowT = arena[0:16, WK + 9240:WK + 9496]
        lMx, lnm, lfloor, lden = sm[:, 128:144], sm[:, 144:160], sm[:, 160:176], sm[:, 176:192]
        xpad = arena[:, WK:WK + 1560].rearrange("p (c s) -> p c s", c=XBC_CH)
        xc = arena[:, WK + 1560:WK + 3096].rearrange("p (c s) -> p c s", c=XBC_CH)
        XT = arena[:, WK + 3096:WK + 3608].rearrange("p (t n) -> p t n", t=TOK)
        xdt = arena[:, WK + 3608:WK + 4632].rearrange("p (t d n) -> p t d n", t=TOK, d=2)
        sw = arena[:, WK + 4632:WK + 8728].rearrange("p (j t s) -> p j t s", j=2 * SH, t=TOK)
        ys = arena[:, WK:WK + 512].rearrange("p (t n) -> p t n", t=TOK)
        ysq = arena[:, WK + 512:WK + 1024].rearrange("p (t n) -> p t n", t=TOK)
        ffn_a = arena[:, WK:WK + 512].rearrange("p (t n) -> p t n", t=TOK)
        moe_h = arena[:, WK + 512:WK + 1024].rearrange("p (t n) -> p t n", t=TOK)
        bst = sm[:, 208:304].rearrange("p (k n) -> p k n", n=6)
        mv = sm[:, 304:336].rearrange("p (k n) -> p k n", n=2)
        comb = sm[:, 336:368]
        lsum = sm[:, 72:80]
        wt4 = sm[:, 496:500]
        GT = sm[:, 500:548].rearrange("p (t n) -> p t n", t=TOK)
        SI = sm[:, 548:580].rearrange("p (t n) -> p t n", t=TOK)
        sp_e = sm[:, 580:612].rearrange("p (t n) -> p t n", t=TOK)
        z_sp = sm[:, 612:644].rearrange("p (t n) -> p t n", t=TOK)
        w_sp = sm[:, 644:676].rearrange("p (t n) -> p t n", t=TOK)
        q_sp = sm[:, 676:708].rearrange("p (t n) -> p t n", t=TOK)
        SP = sm[:, 708:740].rearrange("p (t n) -> p t n", t=TOK)
        ea = sm[:, 740:748]
        cu = sm[:, 748:780].rearrange("p (t n) -> p t n", t=TOK)
        cs = sm[:, 780:812].rearrange("p (t n) -> p t n", t=TOK)
        rw = sm[:, 812:844].rearrange("p (t n) -> p t n", t=TOK)
        ncs = sm[:, 844:860]
        rt_e = sm[:, 64:74].rearrange("p (t n) -> p t n", t=TOK)
        rlog = sm[:, 612:652].rearrange("p (t n) -> p t n", t=TOK)
        r_m = sm[:, 652:656].rearrange("p (t n) -> p t n", t=TOK)
        r_g, r_1, r_2 = [sm[:, a:a + 8].rearrange("p (t n) -> p t n", t=TOK) for a in (656, 664, 672)]
        r_el = sm[:, 680:688].rearrange("p (t n) -> p t n", t=TOK)
        r_pr = sm[:, 688:720].rearrange("p (t g e) -> p t g e", t=TOK, g=EGROUPS)
        r_w = sm[:, 720:728].rearrange("p (t n) -> p t n", t=TOK)
        r_el2 = sm[:, 728:736].rearrange("p (t n) -> p t n", t=TOK)

        block = ctx.enter_context(nc.Block())

        def done(n):
            return n + SLOTS

        @block.sync
        def _(sp):
            def piece(at, s):
                src = A["w_stream"][at] if isinstance(at, int) else A["w_stream"][bass.ds(at, 1), :, :].rearrange("o p n -> p (o n)")
                sp.dma_start(w_raw[:, s * PIECE:(s + 1) * PIECE, :].rearrange("p u n -> p (u n)"), src).then_inc(raw_landed[s], 16)

            n_ring = RAW // PIECE
            sp.dma_start(ccol, A["c_col"]).then_inc(c_loaded, 16)
            for s in range(n_ring):
                piece(s, s)
            sp.dma_start(x_sb[:, :, :], A["x"].rearrange("b (t p) d -> p (b t) d", p=P)).then_inc(x_loaded, 16)
            sp.dma_start(W[:, 0:D], A["norm1_g"].partition_broadcast(P)).then_inc(norm1_loaded, 16)
            rounds = sorted([(ada_round(i), "ada", i) for i in range(N_ADA)]
                            + [(ring_round(r), "unit", r) for r in range(ADA_BEFORE[-1] + 1)])
            for (_, kind, k), (at, _, _) in zip(rounds, rounds[1:]):
                for s in range(n_ring):
                    used = k * RAW + PIECE * (s + 1)
                    sp.wait_ge(ada_used if kind == "ada" else lo_ready, used)
                    piece(at * n_ring + s, s)
                if at == 2:
                    sp.dma_start(ident[:, :], A["identity"]).then_inc(cst_loaded, 16)
                    sp.dma_start(arena[:, 18432:20480], A["const1"]).then_inc(cst_loaded, 16)
                    sp.dma_start(inv_row, A["inv_freq"].partition_broadcast(P)).then_inc(pos_loaded, 16)
                    sp.dma_start(pos_i[:, :], A["pos_col"]).then_inc(pos_loaded, 16)
            with sp.Fori(ADA_BEFORE[-1] + 1, UNITS // RAW) as i:
                for s in range(n_ring):
                    sp.wait_ge(lo_ready, i * RAW + PIECE * (s + 1) - RAW)
                    piece(i * n_ring + (N_ADA * n_ring + s), s)
            sp.wait_ge(x_ready, 1 + LAYERS)
            sp.dma_start(A["out"].rearrange("b (t p) d -> p (b t) d", p=P), x_sb[:, :, :]).then_inc(out_stored, 16)
            sp.wait_ge(out_stored, 16)

        @block.gpsimd
        def _(pool):
            pool.memset(mod[:, 2 * D:], 0.0).then_inc(mod_cleared_b, 1)
            with pool.Fori(0, UNITS // RAW) as i:
                for s in range(RAW):
                    pool.wait_ge(hi_ready, i * RAW + s + 1)
                    pool.tensor_tensor(w_lo[:, s % SLOTS, :], w_raw[:, s, :],
                                       w_hi[:, s % SLOTS, :].bitcast(F32), ALU.subtract).then_inc(lo_ready, 1)
        @block.scalar
        def _(act):
            def hi(n, k):
                if isinstance(n, int):
                    landed = (ring_round((n + k) // RAW) + 1) * 16
                else:
                    landed = n * (16 // RAW) + (k // RAW + N_ADA + 1) * 16
                act.wait_ge(raw_landed[k % RAW // PIECE], landed)
                act.wait_ge(unit_used, n + k + 1)
                act.activation(w_hi[:, k % SLOTS, :], w_raw[:, k % RAW, :], ACT.Copy).then_inc(hi_ready, 1)

            def his(a, b, n=0):
                for k in range(a, b):
                    hi(n, k)

            def turn_hi(n, dst, c0, nch, free=None):
                for t in range(TOK):
                    act.wait_ge(t_ready, n + t + 1)
                    if free is not None and t == 0:
                        act.wait_ge(unit_used, free)
                    act.activation(dst[:, c0:c0 + nch, t * P:(t + 1) * P],
                                   T[:, t, 0:nch * P].rearrange("p (c n) -> p c n", n=P), ACT.Copy).then_inc(t_hi, 1)

            def down_his(n, k, t, pairs):
                for q in range(pairs + 1):
                    if q < pairs:
                        turn_hi(t + 2 * q, yT_hi, 2 * (q % 2), 2, done(n + (k + 2 * q - 2)) if q >= 2 else None)
                    if q >= 1:
                        his(k + 2 * (q - 1) + SLOTS, k + 2 * q + SLOTS, n)

            def root(n, ap):
                act.wait_ge(var_ready, n + 1)
                act.activation(ap, ap, ACT.Sqrt).then_inc(std_ready, 1)

            def sumsq(n):
                for t in range(TOK):
                    i = act.activation(h_sb[:, t, :], x_sb[:, t, :], ACT.Square, accum_out=sm[:, 16 + t:17 + t])
                i.then_inc(sumsq_ready, 1)

            def activate(kind, n_done, t=None):
                act.wait_ge(unit_used, n_done)
                if kind == "mlp":
                    act.activation(tile(0), G[:, :, :], ACT.Relu).then_inc(act_out, 1)
                else:
                    act.activation(ffn_a, G[:, :, 0:DE], ACT.Silu).then_inc(act_out, 1)

            def ffn_step(kind, e, last, n, k, t, ndown):
                turn_hi(t, yT_hi, 0, ndown)
                if e == last:
                    return
                ahead = ndown + UP if e < last - 1 else 2 * ndown
                for j in range(ahead):
                    if j == UP:
                        activate(kind, done(n + k))
                    hi(n, k + j)
                if ahead <= UP:
                    activate(kind, done(n + k))

            def mod_rows(i):
                act.wait_ge(mod_sum, i + 1)
                act.activation(mod[:, i * D:(i + 1) * D].rearrange("p (b n) -> p b n", b=2), G[:, :, :], ACT.Copy).then_inc(mod_out, 1)

            act.dma_start(onehot, A["onehot"]).then_inc(bias_in_loaded, 16)
            act.dma_start(tab[0:BUCKETS, :], A["rel_bias"]).then_inc(bias_in_loaded, 16)
            act.wait_ge(mod_cleared_a, 1)
            act.dma_start(mod[0:1, 0:2 * D], A["b_ada"][:, 0:2 * D]).then_inc(ada_b_loaded, 16)
            act.wait_ge(mod_cleared_b, 1)
            act.dma_start(mod[0:1, 2 * D:], A["b_ada"][:, 2 * D:]).then_inc(ada_b2_loaded, 16)
            act.wait_ge(c_loaded, 16)
            act.activation(csil, ccol, ACT.Silu).then_inc(c_ready, 1)
            for h in range(N_AH):
                act.wait_ge(bias_row, h + 1)
                act.activation(bias_vec[:, h, :], T[:, h % 2, :], ACT.Copy).then_inc(bias_rows_out, 1)
            act.wait_ge(bias_rows_out, N_AH)
            act.dma_start(A["rel_scratch"][:, 0:P, :].rearrange("h p n -> p h n"), bias_vec).then_inc(bias_stored, 16)
            act.wait_ge(x_loaded, 16)
            sumsq(0)
            mod_rows(0)
            root(0, sm[:, 16:18])
            his(U_RET_IN, U_RET_IN + 2)
            mod_rows(1)
            his(U_RET_IN + 2, U_RET_IN + SLOTS)
            turn_hi(T_H1, xT_hi, 0, 4)
            turn_hi(T_H1 + 2, xT_hi, 4, 4)
            act.wait_ge(h_ready, 1)
            act.dma_start(mod[:, 0:2048], A["gn_g"].partition_broadcast(P)).then_inc(gn_g_loaded, 16)
            act.dma_start(W, A["gn_b"].partition_broadcast(P)).then_inc(gn_b_loaded, 16)
            for j in range(N_RET_IN + 1):
                his(U_RET_IN + UP * (j + 1), U_RET_IN + UP * (j + 2))
                if 1 <= j <= 4:
                    for tk in range(TOK):
                        act.wait_ge(rqk_ready, 2 * (j - 1) + tk + 1)
                        act.activation(qkT[:, 4 * (j - 1):4 * j, tk * P:(tk + 1) * P],
                                       T[:, tk, :].rearrange("p (c n) -> p c n", n=P), ACT.Copy).then_inc(rqk_out, 1)
                if 6 <= j < 6 + RH:
                    h = j - 6
                    act.wait_ge(ro_ready, h + 1)
                    act.activation(tile(h), AC[:, 2:4, :], ACT.Copy).then_inc(ro_out, 1)
                    root(R_GN + h, sm[:, 32 + 2 * h:34 + 2 * h])
                if 8 <= j < N_RET_IN:
                    act.wait_ge(unit_used, done(U_RET_IN + UP * (j + 1)))
                    act.activation(tile(j), (G, AC)[j % 2][:, 0:2, :], ACT.Silu).then_inc(rg_gated, 1)
            act.wait_ge(y_ready, RH)
            act.wait_ge(bias_stored, 16)
            for g in range(len(GROUPS)):
                flat = A["rel_scratch"].rearrange("h p n -> h (p n)")[g * AH:(g + 1) * AH, :]
                for t, (c0, n) in enumerate(((0, P), (P, S))):
                    a = S - 1 - t * P
                    src = flat[:, a:a + P * (2 * S - 1)].rearrange("h (p n) -> p h n", n=2 * S - 1)[:, :, 0:n]
                    act.dma_start(rel[g][:, :, c0:c0 + n], src).then_inc(rel_loaded[g], 16)
            down_his(0, U_RET_OUT, T_RET, 2 * RH)
            his(U_ATT_IN + SLOTS, POS0 - UP + SLOTS)
            n_turned = 0
            for p in range(-UP, N_POS):
                his(POS0 + p + SLOTS, POS0 + p + SLOTS + 1)
                if turn_at(p):
                    g, n = turn_at(p)
                    tk, qk = n // 2, n % 2
                    act.wait_ge(aqk_ready, n_turned + 1)
                    act.activation(aqkT[g % 2][:, 4 * qk:4 * qk + 4, tk * P:(tk + 1) * P],
                                   T[:, n % 2, :].rearrange("p (c n) -> p c n", n=P), ACT.Copy).then_inc(aqk_out, 1)
                    n_turned += 1
                k = head_at(p, 1)
                if k is not None:
                    act.wait_ge(as_out, k + 1)
                    if k >= 2:
                        act.wait_ge(aeT_ready, k - 1)
                    act.activation(a_e[:, k % 2, 0:P], scr[:, k % 2, 0:P], ACT.Exp, bias=anm[:, 2 * k:2 * k + 1],
                                   accum_out=aden[:, 2 * k:2 * k + 1])
                    act.activation(a_e[:, k % 2, P:384], scr[:, k % 2, P:384], ACT.Exp, bias=anm[:, 2 * k + 1:2 * k + 2],
                                   accum_out=aden[:, 2 * k + 1:2 * k + 2]).then_inc(ae_ready, 1)
                k = head_at(p, 5)
                if k is not None:
                    g, h = k // AH, k % AH
                    act.wait_ge(ao_ready, k + 1)
                    act.activation(tile(3 * g)[:, :, h * ADH:(h + 1) * ADH],
                                   AC[:, 3, 0:256].rearrange("p (t n) -> p t n", t=TOK), ACT.Copy).then_inc(ao_out, 1)
                    if k == N_AH - 1:
                        act.wait_ge(lse_diff, 1)
                        act.activation(afac, adiff, ACT.Exp).then_inc(lse_exp, 1)
                j = (p - (U_GATE - POS0)) // UP
                if j >= 0 and p % UP == UP - 1:
                    act.wait_ge(unit_used, done(U_GATE + UP * (j + 1)))
                    act.activation(tile((1, 2, 4, 5)[j]), (G, AC)[j % 2][:, 0:2, :], ACT.Sigmoid).then_inc(gate_read, 1)
            down_his(0, U_ATT_OUT, T_ATT, 2)
            for i in range(2, N_ADA):
                mod_rows(i)
            down_his(0, U_WO, T_MERGE, 4)
            act.dma_start(W[:, 0:D], A["norm2_g"].partition_broadcast(P)).then_inc(norm2_loaded, 16)
            act.dma_start(W[:, D:2 * D], A["norm_f_g"].partition_broadcast(P)).then_inc(normf_loaded, 16)
            act.wait_ge(x1_ready, 1)
            sumsq(1)
            root(R_NORM2, sm[:, 16:18])
            turn_hi(T_H2, xT_hi, 0, 4)
            turn_hi(T_H2 + 2, xT_hi, 4, 4)
            activate("mlp", done(U_MLP + UP))
            his(U_MLP + 4, U_MLP + 8)
            with act.Fori(0, FF_TILES - 2) as e:
                ffn_step("mlp", 0, FF_TILES - 1, e * 8 + U_MLP, 8, e * 2 + T_MLP, 4)
            for e in (FF_TILES - 2, FF_TILES - 1):
                ffn_step("mlp", e, FF_TILES - 1, U_MLP, 8 + 8 * e, T_MLP + 2 * e, 4)
            act.wait_ge(x1_ready, 2)
            sumsq(2)
            root(R_FINAL, sm[:, 16:18])
            act.wait_ge(ang_ready, 1)
            act.activation(sinM, sm[:, 64:96].rearrange("p (t n) -> p t n", t=TOK), ACT.Sin)
            act.activation(cosM, sm[:, 96:128].rearrange("p (t n) -> p t n", t=TOK), ACT.Sin).then_inc(trig_ready, 1)
            act.wait_ge(x_ready, 1)
            act.dma_start(arena[:, 17024:18432], A["const2"]).then_inc(cst2_loaded, 16)
            act.dma_start(arena[0:16, 18432:20480], A["row_select"]).then_inc(cst2_loaded, 16)

            with act.Fori(0, LAYERS) as l:
                n = l * L_UNITS + U_LAYERS
                t = l * LT + T_LAYERS
                r = l * LR + R_LAYERS
                act.wait_ge(x_ready, l + 1)
                act.dma_start(mod[:, 0:ROWS2], A["rows2"][bass.ds(l, 1), :].rearrange("o n -> (o n)").partition_broadcast(P))\
                   .then_inc(rows_loaded, 16)
                act.dma_start(cvw, A["conv_col"][bass.ds(l, 1), :, :].rearrange("o p n -> p (o n)")).then_inc(rows_loaded, 16)
                his(0, SLOTS, n)
                turn_hi(t + LT_X, xT_hi, 0, 4)
                turn_hi(t + LT_X + 2, xT_hi, 4, 4)
                his(SLOTS, 12, n)
                act.wait_ge(g_free, l * LM + (G_CREDIT + M_LAYERS + 1))
                for tk in range(TOK):
                    act.activation(HB[:, tk, 0:256], P2[:, tk, 0:256], ACT.Square, accum_out=sm[:, 200 + tk:201 + tk])
                    i = act.activation(HB[:, tk, 256:384], P2[:, tk, 256:384], ACT.Square, accum_out=sm[:, 202 + tk:203 + tk])
                i.then_inc(mla_sumsq, 1)
                his(12, 16, n)
                root(r, sm[:, 200:204])
                act.wait_ge(sp_in, l + 1)
                act.wait_ge(rows_loaded, l * 32 + 32)
                act.activation(sp_e, sp_e, ACT.Exp)
                act.activation(ea, row2["a_log"], ACT.Exp).then_inc(sp_exp, 1)
                his(16, 20, n)
                turn_hi(t + LT_MLA, yT_hi, 0, 3)
                his(20, L_OUT, n)
                for tk in range(TOK):
                    act.wait_ge(unit_used, done(n + L_OUT))
                    kv = (G if tk == 0 else T)[:, :, :].rearrange("p c (h d) -> p (c h) d", d=NOPE + MV)
                    act.activation(KF[:, tk, :].rearrange("p (h d) -> p h d", d=QD)[:, :, 0:NOPE], kv[:, :, 0:NOPE], ACT.Copy)
                    act.activation(V2[:, tk, :].rearrange("p (h d) -> p h d", d=MV), kv[:, :, NOPE:], ACT.Copy).then_inc(kv_out, 1)
                his(L_OUT, L_OUT + SLOTS, n)
                for m in range(8):
                    qk, tk, hg = m // 4, m // 2 % 2, m % 2
                    act.wait_ge(mqkT_ready, l * 8 + m + 1)
                    act.activation((mqT, mkT)[qk][0:QD, 4 * hg:4 * hg + 4, tk * P:(tk + 1) * P],
                                   T[0:QD, m % 2, :].rearrange("p (c n) -> p c n", n=P), ACT.Copy).then_inc(mqkT_out, 1)
                for h in range(MH):
                    act.wait_ge(mmax_ready, l * MH + h + 1)
                    if h >= 2:
                        act.wait_ge(meT_ready, l * MH + h - 1)
                    for tk in range(TOK):
                        i = act.activation(me[:, h % 2, tk, :], G[:, h % 2, tk * S:(tk + 1) * S], ACT.Exp, scale=QD ** -0.5,
                                           bias=mnm[:, 2 * h + tk:2 * h + tk + 1], accum_out=mden[:, 2 * h + tk:2 * h + tk + 1])
                    i.then_inc(me_ready, 1)
                act.wait_ge(rows_T, l + 1)
                act.activation(rowT[0:16, :], T[0:16, 0, 0:S], ACT.Copy).then_inc(rows_out, 1)
                for tk in range(TOK):
                    act.wait_ge(lqk_T, l * TOK + tk + 1)
                    act.activation(lqkT[:, :, tk * P:(tk + 1) * P], AC[:, tk, :].rearrange("p (c n) -> p c n", n=P), ACT.Copy)\
                       .then_inc(lqk_out, 1)
                act.wait_ge(lmax_ready, l + 1)
                act.activation(lfloor, lfloor, ACT.Exp, scale=-1.0)
                for j in range(2 * LH):
                    c = j % 2 * LH + j // 2
                    for tk in range(TOK):
                        i = act.activation(lw[:, j, tk, :], lw[:, j, tk, :], ACT.Exp, bias=lnm[:, tk * 8 + c:tk * 8 + c + 1])
                    i.then_inc(lexp_ready, 1)
                act.activation(P2[:, :, IN2["mo"]:IN2["mo"] + 256], P2[:, :, IN2["mo"]:IN2["mo"] + 256], ACT.Sigmoid).then_inc(lgate, 1)
                for h in range(LH):
                    act.wait_ge(lpT_ready, l * LH + h + 1)
                    if h >= 2:
                        act.wait_ge(lnum_ready, l * LH + h - 1)
                    act.activation(lpT[:, h % 2, :], T[:, h % 2, :], ACT.Copy).then_inc(lpT_out, 1)
                root(r + 1, sm[:, 64:72])
                for m in range(3):
                    act.wait_ge(sx_T, l * 3 + m + 1)
                    if m < 2:
                        i = act.activation(xpad[:, 0:4, 2 + m * P:2 + (m + 1) * P], AC[:, m, :].rearrange("p (c n) -> p c n", n=P), ACT.Copy)
                    else:
                        i = act.activation(xpad[:, 4:6, 2:2 + S], AC[:, 2, :].rearrange("p (c n) -> p c n", n=S), ACT.Copy)
                    i.then_inc(sx_out, 1)
                act.wait_ge(conv_done, l + 1)
                for c in range(XBC_CH):
                    i = act.activation(xc[:, c, :], xc[:, c, :], ACT.Silu, bias=cv_b[:, c:c + 1])
                act.activation(P2[:, :, IN2["z"]:IN2["z"] + 256], P2[:, :, IN2["z"]:IN2["z"] + 256], ACT.Silu).then_inc(conv_act, 1)
                for j in range(2 * SH):
                    c = j % 2 * SH + j // 2
                    act.wait_ge(srow_out, l * 8 + j + 1)
                    for st in range(TOK):
                        i = act.activation(sw[:, j, st, :], sw[:, j, st, :], ACT.Exp, bias=ncs[:, st * 8 + c:st * 8 + c + 1])
                    i.then_inc(sexp_ready, 1)
                root(r + 2, sm[:, 64:68])
                down_his(n, L_OUT, t + LT_OUT, 4)
                root(r + 3, sm[:, 16:18])
                turn_hi(t + LT_X2, xT_hi, 0, 4)
                turn_hi(t + LT_X2 + 2, xT_hi, 4, 4)
                his(L_MOE + 3, L_MOE + 4, n)
                act.wait_ge(gexp_in, l + 1)
                act.activation(rt_e, rt_e, ACT.Exp).then_inc(gexp_out, 1)
                activate("moe", done(n + L_MOE + UP))
                his(L_MOE + 4, L_MOE + 8, n)
                with act.Fori(0, 3) as e4:
                    for q in range(4):
                        ffn_step("moe", 0, EXPERTS - 1, e4 * 24 + n, L_MOE + 8 + 6 * q, t + LT_MOE + e4 * 8 + 2 * q, 2)
                for e in range(12, EXPERTS):
                    ffn_step("moe", e, EXPERTS - 1, n, L_MOE + 8 + 6 * e, t + LT_MOE + 2 * e, 2)
                root(r + 4, sm[:, 16:18])
        @block.tensor
        def _(pe):
            def mm3(out, xh, xl, wh, wl, start, stop):
                pe.matmul(out, xh, wh, start=start, stop=False)
                pe.matmul(out, xh, wl, start=False, stop=False)
                return pe.matmul(out, xl, wh, start=False, stop=stop)

            def up_unit(n, k, u, banks):
                pe.wait_ge(lo_ready, n + (k + u + 1))
                s = (k + u) % SLOTS
                for t in range(TOK):
                    for j in range(2):
                        c, w = 2 * u + j, slice(j * NT, (j + 1) * NT)
                        i = mm3(banks[:, t, :], xT_hi[:, c, t * P:(t + 1) * P], xT_lo[:, c, t * P:(t + 1) * P],
                                w_hi[:, s, w], w_lo[:, s, w], c == 0, c == KC - 1)
                i.then_inc(unit_used, 1)

            def up(n, k, banks):
                for u in range(UP):
                    up_unit(n, k, u, banks)

            def down(n, k, nch, first, last, c0=0):
                for c in range(nch):
                    pe.wait_ge(lo_ready, n + (k + c + 1))
                    s = (k + c) % SLOTS
                    for t in range(TOK):
                        for j in range(2):
                            w = slice(j * NT, (j + 1) * NT)
                            i = mm3(AC[:, 2 * t + j, :], yT_hi[:, c0 + c, t * P:(t + 1) * P], yT_lo[:, c0 + c, t * P:(t + 1) * P],
                                    w_hi[:, s, w], w_lo[:, s, w], first and c == 0, last and c == nch - 1)
                    i.then_inc(unit_used, 1)

            def turn(n, src, nch):
                for t in range(TOK):
                    if not (isinstance(n, int) and n < TOK):
                        pe.wait_ge(t_lo, n + t - 1)
                    for c in range(nch):
                        i = pe.transpose(T[:, t, c * P:(c + 1) * P], src[:, t, c * P:(c + 1) * P], ident[:, :])
                    i.then_inc(t_ready, 1)

            def down_pairs(n, k, t, src, pairs, before=None):
                for q in range(pairs + 1):
                    if q < pairs:
                        if before:
                            before(q)
                        turn(t + 2 * q, src(q), 2)
                    if q >= 1:
                        pe.wait_ge(t_lo, t + 2 * q)
                        down(n, k + 2 * (q - 1), 2, q == 1, q == pairs, 2 * ((q - 1) % 2))

            def clear_acc():
                for b in range(4):
                    pe.matmul(AC[:, b, :], zero_r[0:1, :], xT_hi[0:1, 0:2, :].rearrange("p c n -> p (c n)"),
                              start=True, stop=False)

            def ffn_step(e, last, n, k, t, h, h_src, ndown):
                pe.wait_ge(ffn_h, h + 1)
                turn(t, h_src, ndown)
                if e < last:
                    up(n, k, G)
                pe.wait_ge(t_lo, t + TOK)
                down(n, k + UP if e < last else k, ndown, False, e == last)

            pe.wait_ge(tab_wide, 1)
            pe.wait_ge(bias_in_loaded, 32)
            for h in range(N_AH):
                if h >= 2:
                    pe.wait_ge(bias_rows_out, h - 1)
                pe.matmul(T[:, h % 2, :], tab_bc[:, h, :], onehot[:, h // AH, :], start=True, stop=True).then_inc(bias_row, 1)
            def mod_sums(i, ones_m):
                pe.wait_ge(ada_summed, i + 1)
                if i:
                    pe.wait_ge(mod_out, i)
                for b in range(2):
                    k = pe.matmul(G[:, b, :], ones_m, mod[:, i * D + b * NT:i * D + (b + 1) * NT], start=True, stop=True)
                k.then_inc(mod_sum, 1)

            mod_sums(0, ones_a)
            mod_sums(1, ones_a)
            def ret_turn(j):
                for tk in range(TOK):
                    n = 2 * j + tk
                    pe.wait_ge(rope_done, j + 1)
                    if n >= 2:
                        pe.wait_ge(rqk_out, n - 1)
                    for c in range(4):
                        i = pe.transpose(T[:, tk, c * P:(c + 1) * P], tile(j)[:, tk, c * P:(c + 1) * P], ident[:, :])
                    i.then_inc(rqk_ready, 1)

            def ret_scores(h):
                if h >= 2:
                    pe.wait_ge(rs_out, h - 1)
                b = h % 2
                for c in range(2):
                    pe.matmul(T[:, b, 0:S], qkT[:, 8 + 2 * h + c, 0:P], qkT[:, 2 * h + c, :], start=c == 0, stop=c == 1)
                for c in range(2):
                    i = pe.matmul(T[:, b, S:S + P], qkT[:, 8 + 2 * h + c, P:S], qkT[:, 2 * h + c, P:S], start=c == 0, stop=c == 1)
                i.then_inc(rs_ready, 1)

            def ret_out(h):
                b, v = h % 2, tile(4 + h)
                pe.wait_ge(rs_out, h + 1)
                if h >= 1:
                    pe.wait_ge(ro_out, h)
                pe.matmul(AC[:, 2, :], scr[:, b, 0:P], v[:, 0, :], start=True, stop=True)
                pe.matmul(AC[:, 3, :], scr[:, b, P:S], v[:, 0, :], start=True, stop=False)
                pe.matmul(AC[:, 3, :], scr[:, b, S:S + P], v[:, 1, :], start=False, stop=True).then_inc(ro_ready, 1)

            pe.wait_ge(h_ready, 1)
            pe.wait_ge(cst_loaded, 32)
            pe.wait_ge(bias_rows_out, N_AH)
            turn(T_H1, h_sb[:, :, 0:NT], 4)
            turn(T_H1 + 2, h_sb[:, :, NT:D], 4)
            pe.wait_ge(t_lo, T_H1 + 4)
            for j in range(N_RET_IN):
                if j < 10:
                    pe.wait_ge(g_free, G_CREDIT + j - 1)
                else:
                    pe.wait_ge(rg_gated, j - 9)
                up(0, U_RET_IN + j * UP, (G, AC)[j % 2])
                if 1 <= j <= 4:
                    ret_turn(j - 1)
                if j == 5:
                    pe.wait_ge(rqk_out, 8)
                    ret_scores(0)
                    ret_scores(1)
                if 6 <= j < 6 + RH:
                    ret_out(j - 6)
                    if j < 4 + RH:
                        ret_scores(j - 4)
            pe.wait_ge(rg_gated, 3)
            up(0, U_ATT_FIRST, G)
            pe.wait_ge(rg_gated, RH)
            down_pairs(0, U_RET_OUT, T_RET, lambda q: tile(8 + q // 2)[:, :, q % 2 * 256:(q % 2 + 1) * 256], 2 * RH,
                       lambda q: pe.wait_ge(y_ready, q // 2 + 1))
            pe.wait_ge(g_free, G_CREDIT + M_ATT_IN + 1)
            up(0, U_ATT_IN, G)
            pe.wait_ge(acc_free, 1)

            def att_qk_turn(g, n, n_turned, n_eT):
                tk, qk = n // 2, n % 2
                pe.wait_ge(g_free, G_CREDIT + M_ATT_IN + 3 * g + 2)
                if n_turned >= 2:
                    pe.wait_ge(aqk_out, n_turned - 1)
                if n_eT:
                    pe.wait_ge(aeT_out, n_eT)
                for c in range(AH):
                    i = pe.transpose(T[:, n % 2, c * P:(c + 1) * P], tile(3 * g + qk)[:, tk, c * P:(c + 1) * P], ident[:, :])
                i.then_inc(aqk_ready, 1)

            def att_scores(k, n_turned):
                h, qk = k % AH, aqkT[k // AH % 2]
                pe.wait_ge(aqk_out, n_turned)
                if k >= 1:
                    pe.wait_ge(as_out, k)
                pe.matmul(AC[:, 2, 0:P], qk[:, h, 0:P], qk[:, AH + h, 0:P], start=True, stop=True)
                pe.matmul(AC[:, 2, P:384], qk[:, h, P:S], qk[:, AH + h, :], start=True, stop=True).then_inc(as_ready, 1)

            def att_turn(k, n_turned):
                b = k % 2
                pe.wait_ge(ae_ready, k + 1)
                pe.wait_ge(aqk_out, n_turned)
                if k >= 2:
                    pe.wait_ge(aeT_out, k - 1)
                for c in range(3):
                    i = pe.transpose(T[:, b, c * P:(c + 1) * P], a_e[:, b, c * P:(c + 1) * P], ident[:, :])
                i.then_inc(aeT_ready, 1)

            def att_values(k):
                b, v = k % 2, tile(3 * (k // AH) + 2)[:, :, k % AH * ADH:(k % AH + 1) * ADH]
                pe.wait_ge(g_free, G_CREDIT + M_ATT_IN + 3 * (k // AH) + 3)
                pe.wait_ge(aeT_out, k + 1)
                if k >= 1:
                    pe.wait_ge(ao_out, k)
                pe.matmul(AC[:, 3, 0:P], a_eT[b][:, 0:P], v[:, 0, :], start=True, stop=True)
                pe.matmul(AC[:, 3, P:S], a_eT[b][:, P:S], v[:, 0, :], start=True, stop=False)
                pe.matmul(AC[:, 3, P:S], a_eT[b][:, S:384], v[:, 1, :], start=False, stop=True).then_inc(ao_ready, 1)

            n_turned, n_eT = 0, 0
            for p in range(-UP, N_POS):
                j = p // UP + 3
                if p % UP == 0 and p >= 0:
                    if j < N_ATT_IN + 2:
                        pe.wait_ge(g_free, G_CREDIT + M_ATT_IN + j - 1)
                    else:
                        pe.wait_ge(gate_read, j - N_ATT_IN - 1)
                up_unit(0, POS0 + p // UP * UP, p % UP, (AC, G)[j % 2])
                if head_at(p, 3) is not None:
                    att_turn(head_at(p, 3), n_turned)
                    n_eT += 1
                if turn_at(p):
                    att_qk_turn(*turn_at(p), n_turned, n_eT)
                    n_turned += 1
                if head_at(p, 0) is not None:
                    att_scores(head_at(p, 0), n_turned)
                if head_at(p, 4) is not None:
                    att_values(head_at(p, 4))
            pe.wait_ge(att_ready, 1)
            pe.wait_ge(gate_read, N_GATE)
            pe.wait_ge(ao_out, N_AH)
            down_pairs(0, U_ATT_OUT, T_ATT, lambda q: tile(0)[:, :, q * 256:(q + 1) * 256], 2)
            for i in range(2, N_ADA):
                mod_sums(i, ones_b)
            pe.wait_ge(acc_free, 2)
            down_pairs(0, U_WO, T_MERGE, lambda q: tile(10 + q // 2)[:, :, q % 2 * 256:(q % 2 + 1) * 256], 4,
                       lambda q: pe.wait_ge(merged_ready, q // 2 + 1))
            pe.wait_ge(h_ready, 2)
            turn(T_H2, h_sb[:, :, 0:NT], 4)
            turn(T_H2 + 2, h_sb[:, :, NT:D], 4)
            pe.wait_ge(t_lo, T_H2 + 4)
            pe.wait_ge(acc_free, 3)
            pe.wait_ge(zero_ready, 1)
            clear_acc()
            up(0, U_MLP, G)
            with pe.Fori(0, FF_TILES - 2) as e:
                ffn_step(0, FF_TILES - 1, e * 8 + U_MLP, UP, e * 2 + T_MLP, e, tile(1), 4)
            for e in (FF_TILES - 2, FF_TILES - 1):
                ffn_step(e, FF_TILES - 1, U_MLP, UP + 8 * e, T_MLP + 2 * e, e, tile(1), 4)

            pe.wait_ge(cst2_loaded, 32)
            with pe.Fori(0, LAYERS) as l:
                n = l * L_UNITS + U_LAYERS
                tb = l * LT + T_LAYERS
                m = l * LM + (M_LAYERS + G_CREDIT)
                pe.wait_ge(x_ready, l + 1)
                turn(tb + LT_X, x_sb[:, :, 0:NT], 4)
                turn(tb + (LT_X + 2), x_sb[:, :, NT:D], 4)
                pe.wait_ge(t_lo, tb + (LT_X + 4))
                for j in range(N_IN2):
                    pe.wait_ge(g_free, m + (j - 1))
                    up(n, L_IN + j * UP, (G, AC)[j % 2])
                pe.wait_ge(cq_ready, l + 1)
                turn(tb + LT_MLA, P2, 3)
                pe.wait_ge(t_lo, tb + (LT_MLA + TOK))
                pe.wait_ge(g_free, m + N_IN2)
                for c in range(2):
                    pe.wait_ge(lo_ready, n + (L_UQ + c + 1))
                    s = (L_UQ + c) % SLOTS
                    for t in range(TOK):
                        for b, (w0, w1) in enumerate(((0, NT), (NT, MH * QD))):
                            i = mm3(AC[:, 2 * t + b, 0:w1 - w0], yT_hi[:, c, t * P:(t + 1) * P], yT_lo[:, c, t * P:(t + 1) * P],
                                    w_hi[:, s, w0:w1], w_lo[:, s, w0:w1], c == 0, c == 1)
                    i.then_inc(unit_used, 1)
                pe.wait_ge(lo_ready, n + (L_UKV + 1))
                s = L_UKV % SLOTS
                for t in range(TOK):
                    for b in range(2):
                        w = slice(b * NT, (b + 1) * NT)
                        i = mm3((G, T)[t][:, b, :], yT_hi[:, 2, t * P:(t + 1) * P], yT_lo[:, 2, t * P:(t + 1) * P],
                                w_hi[:, s, w], w_lo[:, s, w], True, True)
                i.then_inc(unit_used, 1)
                pe.wait_ge(cum_in, l + 1)
                pe.wait_ge(kv_out, l * TOK + TOK)
                cum = G[:, 0, 0:64].rearrange("p (k n) -> p k n", n=16)
                pe.matmul(cum[:, 0, :], tri_f, cu[:, 0, :], start=True, stop=True)
                pe.matmul(cum[:, 1, :], ones, cu[:, 0, :], start=True, stop=False)
                pe.matmul(cum[:, 1, :], tri_f, cu[:, 1, :], start=False, stop=True)
                pe.matmul(cum[:, 2, :], tri_b, cu[:, 0, :], start=True, stop=False)
                pe.matmul(cum[:, 2, :], ones, cu[:, 1, :], start=False, stop=True)
                pe.matmul(cum[:, 3, :], tri_b, cu[:, 1, :], start=True, stop=True).then_inc(cum_ready, 1)
                for k in range(8):
                    qk, tk, hg = k // 4, k // 2 % 2, k % 2
                    pe.wait_ge((q_ready, kv_ready)[qk], l + 1)
                    if k >= 2:
                        pe.wait_ge(mqkT_out, l * 8 + (k - 1))
                    for c in range(4):
                        h = 4 * hg + c
                        i = pe.transpose(T[0:QD, k % 2, c * P:(c + 1) * P], (Q, KF)[qk][:, tk, h * QD:(h + 1) * QD], ident[:, :])
                    i.then_inc(mqkT_ready, 1)

                def mla_scores(h):
                    if h >= 2:
                        pe.wait_ge(me_ready, l * MH + (h - 1))
                    for t in range(TOK):
                        i = pe.matmul(G[:, h % 2, t * S:(t + 1) * S], mqT[0:QD, h, t * P:(t + 1) * P], mkT[0:QD, h, :], start=True, stop=True)
                    i.then_inc(ms_ready, 1)

                def mla_turn(h):
                    pe.wait_ge(me_ready, l * MH + (h + 1))
                    if h >= 2:
                        pe.wait_ge(meT_out, l * MH + (h - 1))
                    for kt in range(TOK):
                        for t in range(TOK):
                            c = kt * TOK + t
                            i = pe.transpose(T[:, h % 2, c * P:(c + 1) * P], me[:, h % 2, t, kt * P:(kt + 1) * P], ident[:, :])
                    i.then_inc(meT_ready, 1)

                def mla_values(h):
                    pe.wait_ge(meT_out, l * MH + (h + 1))
                    if h >= 2:
                        pe.wait_ge(mo_out, l * MH + (h - 1))
                    for t in range(TOK):
                        for kt in range(TOK):
                            c = kt * TOK + t
                            i = pe.matmul(AC[:, h % 2, t * MV:(t + 1) * MV], meT[:, h % 2, c * P:(c + 1) * P],
                                          V2[:, kt, h * MV:(h + 1) * MV], start=kt == 0, stop=kt == TOK - 1)
                    i.then_inc(mo_ready, 1)

                pe.wait_ge(mqkT_out, l * 8 + 8)
                pe.wait_ge(rows_w, l + 1)
                for h in range(MH + 2):
                    if h < MH:
                        mla_scores(h)
                    if 1 <= h <= MH:
                        mla_turn(h - 1)
                    if h >= 2:
                        mla_values(h - 2)
                pe.wait_ge(meT_out, l * MH + MH)
                for t in range(TOK):
                    i = pe.transpose(T[0:16, 0, t * P:(t + 1) * P], rw[:, t, :], ident[:, :])
                i.then_inc(rows_T, 1)
                pe.wait_ge(mo_out, l * MH + MH)
                for t in range(TOK):
                    for c in range(4):
                        a = IN2["mq"] + c * P
                        i = pe.transpose(AC[:, t, c * P:(c + 1) * P], P2[:, t, a:a + P], ident[:, :])
                    i.then_inc(lqk_T, 1)
                pe.wait_ge(rows_out, l + 1)

                def row(out, c):
                    return pe.matmul(out, sel[0:16, c, :], rowT[0:16, :], start=True, stop=True)

                for j in range(2 * LH):
                    if j >= 2:
                        pe.wait_ge(lrow_out, l * 8 + (j - 1))
                    row(G[:, j % 2, 0:S], j % 2 * LH + j // 2).then_inc(lrow_ready, 1)
                pe.wait_ge(lqk_out, l * TOK + TOK)
                for h in range(LH):
                    a = h % 2 * LDH
                    for t in range(TOK):
                        i = pe.matmul(AC[:, h, t * S:(t + 1) * S], lqkT[a:a + LDH, h // 2, t * P:(t + 1) * P],
                                      lqkT[a:a + LDH, 2 + h // 2, :], start=True, stop=True)
                    i.then_inc(lqk_ready, 1)
                pe.wait_ge(lrow_out, l * 8 + 8)

                def lstm_turn(h):
                    pe.wait_ge(lp_ready, l * LH + (h + 1))
                    if h >= 2:
                        pe.wait_ge(lpT_out, l * LH + (h - 1))
                    for st in range(TOK):
                        for t in range(TOK):
                            c = st * TOK + t
                            i = pe.transpose(T[:, h % 2, c * P:(c + 1) * P], lw[:, 2 * h, t, st * P:(st + 1) * P], ident[:, :])
                    i.then_inc(lpT_ready, 1)

                def lstm_values(h):
                    pe.wait_ge(lpT_out, l * LH + (h + 1))
                    a = IN2["mv"] + h * LDH
                    for t in range(TOK):
                        for st in range(TOK):
                            c = st * TOK + t
                            i = pe.matmul(G[:, 0, t * S + h * LDH:t * S + (h + 1) * LDH], lpT[:, h % 2, c * P:(c + 1) * P],
                                          P2[:, st, a:a + LDH], start=st == 0, stop=st == TOK - 1)
                    i.then_inc(lnum_ready, 1)

                for h in range(LH + 1):
                    if h < LH:
                        lstm_turn(h)
                    if h >= 1:
                        lstm_values(h - 1)
                for k in range(3):
                    for c in range(4):
                        t, ch = (k, c) if k < 2 else (c % 2, 4 + c // 2)
                        a = IN2["xbc"] + ch * P
                        i = pe.transpose(AC[:, k, c * P:(c + 1) * P], P2[:, t, a:a + P], ident[:, :])
                    i.then_inc(sx_T, 1)
                pe.wait_ge(conv_act, l + 1)
                for t in range(TOK):
                    for c in range(2):
                        a = (t * 2 + c) * P
                        i = pe.transpose(T[:, 0, a:a + P], xc[:, c, t * P:(t + 1) * P], ident[:, :])
                i.then_inc(sxt_T, 1)
                for g in range(SG):
                    for st in range(TOK):
                        i = pe.matmul(AC[:, g, st * S:(st + 1) * S], xc[:, 2 + g, st * P:(st + 1) * P], xc[:, 4 + g, :], start=True, stop=True)
                    i.then_inc(scb_ready, 1)
                for j in range(2 * SH):
                    if j >= 2:
                        pe.wait_ge(srow_out, l * 8 + (j - 1))
                    row(AC[:, 2 + j % 2, 0:S], 8 + j % 2 * SH + j // 2).then_inc(srow_ready, 1)
                for h in range(SH):
                    pe.wait_ge(sw_ready, l * 8 + (2 * h + 2))
                    for t, pairs in enumerate((((0, 0), (1, 0), (1, 1)), ((0, 0), (0, 1), (1, 1)))):
                        for k, (d, st) in enumerate(pairs):
                            i = pe.matmul(T[:, 1, t * S + h * SP_:t * S + (h + 1) * SP_], sw[:, 2 * h + d, st, t * P:(t + 1) * P],
                                          xdt[:, st, d, h * SP_:(h + 1) * SP_], start=k == 0, stop=k == 2)
                    i.then_inc(sy_ready, 1)
                pe.wait_ge(sy_out, l + 1)
                down_pairs(n, L_OUT, tb + LT_OUT, lambda q: HB[:, :, q * 256:(q + 1) * 256], 4,
                           lambda q: pe.wait_ge(heads_ready, l + 1) if q == 3 else None)
                pe.wait_ge(x2_ready, l + 1)
                turn(tb + LT_X2, x_sb[:, :, 0:NT], 4)
                turn(tb + (LT_X2 + 2), x_sb[:, :, NT:D], 4)
                pe.wait_ge(t_lo, tb + (LT_X2 + 4))
                pe.wait_ge(lo_ready, n + (L_ROUTER + 1))
                s, nr = L_ROUTER % SLOTS, EGROUPS + EXPERTS
                for t in range(TOK):
                    for c in range(KC):
                        w = slice(c * nr, (c + 1) * nr)
                        i = mm3(G[:, t, 0:nr], xT_hi[:, c, t * P:(t + 1) * P], xT_lo[:, c, t * P:(t + 1) * P],
                                w_hi[:, s, w], w_lo[:, s, w], c == 0, c == KC - 1)
                i.then_inc(unit_used, 1)
                pe.wait_ge(acc_free, l * LC + (C_LAYERS + 1))
                clear_acc()
                pe.wait_ge(g_free, m + LM)
                up(n, L_MOE, G)
                with pe.Fori(0, 3) as e4:
                    for q in range(4):
                        ffn_step(0, EXPERTS - 1, e4 * 24 + n, L_MOE + UP + 6 * q, e4 * 8 + (tb + (LT_MOE + 2 * q)),
                                 l * EXPERTS + e4 * 4 + (FF_TILES + q), moe_h, 2)
                for e in range(12, EXPERTS):
                    ffn_step(e, EXPERTS - 1, n, L_MOE + UP + 6 * e, tb + (LT_MOE + 2 * e), l * EXPERTS + (FF_TILES + e), moe_h, 2)
        @block.vector
        def _(dve):
            dep = dve.drain

            def lo(n, dst_hi, dst_lo, c0, nch):
                for t in range(TOK):
                    dve.wait_ge(t_hi, n + t + 1)
                    s = slice(t * P, (t + 1) * P)
                    dve.tensor_tensor(dst_lo[:, c0:c0 + nch, s], T[:, t, 0:nch * P].rearrange("p (c n) -> p c n", n=P),
                                      dst_hi[:, c0:c0 + nch, s].bitcast(F32), ALU.subtract).then_inc(t_lo, 1)

            def down_los(n, q0, q1):
                for q in range(q0, q1):
                    lo(n + 2 * q, yT_hi, yT_lo, 2 * (q % 2), 2)

            def rstd(n, ap, scale, eps):
                dep()
                dve.tensor_scalar(ap, ap, scale, eps, ALU.mult, ALU.add).then_inc(var_ready, 1)
                dve.wait_ge(std_ready, n + 1)
                dve.reciprocal(ap, ap)
                dep()

            def wide(row, t=TOK):
                return row.unsqueeze(1).to_broadcast([P, t, row.shape[1]])

            def read_tile(dst, banks, n_done):
                dve.wait_ge(unit_used, n_done)
                dve.tensor_copy(dst, banks[:, 0:2, :]).then_inc(g_free, 1)

            def modulated(sc, sh, g_loaded):
                A1 = W[:, 0:D]
                dve.wait_ge(g_loaded, 16)
                dve.scalar_tensor_tensor(A1, mod[:, sc * D:(sc + 1) * D], 1.0, A1, ALU.add, ALU.mult)
                dep()
                for t in range(TOK):
                    dve.scalar_tensor_tensor(h_sb[:, t, :], x_sb[:, t, :], sm[:, 16 + t:17 + t], A1, ALU.mult, ALU.mult)
                dep()
                dve.tensor_tensor(h_sb, h_sb, wide(mod[:, sh * D:(sh + 1) * D]), ALU.add).then_inc(h_ready, 1)

            def ada(i, s0, s1):
                m = mod[:, i * D:(i + 1) * D]
                for s in range(s0, s1):
                    dve.wait_ge(raw_landed[s // PIECE], 16 * (ada_round(i) + 1))
                    dve.scalar_tensor_tensor(m, w_raw[:, s, :], csil[:, s:s + 1], m, ALU.mult, ALU.add).then_inc(ada_used, 1)
                    dep()
                if s1 == KC:
                    dve.memset(sm[:, 892:893], 0.0).then_inc(ada_summed, 1)

            dve.memset(mod[:, 0:2 * D], 0.0).then_inc(mod_cleared_a, 1)
            dve.memset(sm[:, 892:893], 0.0).then_inc(unit_used, SLOTS)
            dve.memset(sm[:, 893:894], 0.0).then_inc(g_free, G_CREDIT)
            dve.memset(zero_r[:, :].bitcast(F32), 0.0).then_inc(zero_ready, 1)
            dve.memset(ones_a, 1.0)
            for k in range(4):
                dve.memset(wt4[:, k:k + 1], 4.0 - k)
            dve.memset(tab[BUCKETS:BUCKETS + 1, :], NEG)
            dep()
            dve.wait_ge(bias_in_loaded, 32)
            dve.tensor_copy(tab_bc, tab.unsqueeze(2).to_broadcast([BUCKETS + 1, N_AH, P])).then_inc(tab_wide, 1)
            dve.wait_ge(c_ready, 1)
            dve.wait_ge(ada_b_loaded, 16)
            ada(0, 0, KC)
            ada(1, 0, KC)
            dve.wait_ge(sumsq_ready, 1)
            rstd(0, sm[:, 16:18], 1.0 / D, 1e-6)
            dve.wait_ge(mod_out, 2)
            modulated(1, 0, norm1_loaded)
            lo(T_H1, xT_hi, xT_lo, 0, 4)
            lo(T_H1 + 2, xT_hi, xT_lo, 4, 4)
            dve.wait_ge(bias_stored, 16)
            dve.wait_ge(cst_loaded, 32)

            def rotate(j):
                x = tile(j).rearrange("p t (h x n) -> p t h x n", h=2, x=2)
                x1, x2 = x[:, :, :, 0, :], x[:, :, :, 1, :]
                t1, t2 = [tile(8)[:, a, :].rearrange("p (t h n) -> p t h n", t=TOK, h=2) for a in range(2)]
                c, s = [r.unsqueeze(2).to_broadcast([P, TOK, 2, P]) for r in (cosR, sinR)]
                dep()
                dve.tensor_tensor(t1, x1, s, ALU.mult)
                dve.tensor_tensor(t2, x2, s, ALU.mult)
                dep()
                dve.tensor_tensor(x1, x1, c, ALU.mult)
                dve.tensor_tensor(x2, x2, c, ALU.mult)
                dep()
                dve.tensor_tensor(x1, x1, t2, ALU.subtract)
                dve.tensor_tensor(x2, x2, t1, ALU.add).then_inc(rope_done, 1)
                dep()

            def ret_in_tile(j):
                read_tile(tile(j), (G, AC)[j % 2], done(U_RET_IN + (j + 1) * UP))

            def decayed(h):
                dve.wait_ge(rs_ready, h + 1)
                if h >= 2:
                    dve.wait_ge(ro_ready, h - 1)
                dve.tensor_tensor(scr[:, h % 2, :], T[:, h % 2, 0:384], decay[:, h, :], ALU.mult).then_inc(rs_out, 1)

            def group_norm(h):
                o, cols = tile(h), slice(h * RDV, (h + 1) * RDV)
                ks = range(2 * h, 2 * h + TOK)
                dve.wait_ge(ro_out, h + 1)
                for k in ks:
                    dve.bn_stats(bst[:, k, :], o[:, k % 2, :])
                dep()
                for k in ks:
                    dve.bn_aggr(mv[:, k, :], bst[:, k, :])
                dep()
                sd = sm[:, 32 + 2 * h:34 + 2 * h]
                dve.tensor_copy(sd, mv[:, 2 * h:2 * h + 2, 1])
                rstd(R_GN + h, sd, 1.0, 1e-5)
                for k in ks:
                    dve.tensor_scalar(o[:, k % 2, :], o[:, k % 2, :], mv[:, k, 0:1], sd[:, k % 2:k % 2 + 1], ALU.subtract, ALU.mult)
                dve.wait_ge(gn_g_loaded, 16)
                dve.wait_ge(gn_b_loaded, 16)
                dep()
                dve.tensor_tensor(o, o, wide(mod[:, cols]), ALU.mult)
                dep()
                dve.tensor_tensor(o, o, wide(W[:, cols]), ALU.add)
                dep()

            def gated(h):
                dve.wait_ge(rg_gated, h + 1)
                dve.tensor_tensor(tile(8 + h), tile(8 + h), tile(h), ALU.mult).then_inc(y_ready, 1)

            dve.wait_ge(ada_b2_loaded, 16)
            ada(2, 0, 4)
            ret_in_tile(0)
            rotate(0)
            ada(2, 4, KC)
            for j in range(1, 4):
                ret_in_tile(j)
                rotate(j)
            ada(3, 0, 4)
            ret_in_tile(4)
            ada(3, 4, KC)
            ret_in_tile(5)
            decayed(0)
            decayed(1)
            ret_in_tile(6)
            group_norm(0)
            decayed(2)
            ret_in_tile(7)
            group_norm(1)
            decayed(3)
            ada(4, 0, 4)
            group_norm(2)
            gated(0)
            ada(4, 4, KC)
            group_norm(3)
            gated(1)
            gated(2)
            gated(3)
            read_tile(tile(0), G, done(U_ATT_FIRST + UP))
            for q in range(2 * RH):
                down_los(T_RET, q, q + 1)
                if 2 <= q < 6:
                    ada(5, 2 * (q - 2), 2 * (q - 1))
            acc_ct = AC[:, :, :].rearrange("p (t c) n -> p t c n", t=TOK)
            dve.wait_ge(unit_used, done(U_RET_OUT + 4 * RH))
            dve.tensor_copy(tile(10), acc_ct[:, :, 0, :])
            dve.tensor_copy(tile(11), acc_ct[:, :, 1, :]).then_inc(acc_free, 1)
            read_tile(tile(1), G, done(U_ATT_IN + UP))
            for p in range(-UP, N_POS):
                k = head_at(p, 3)
                if k is not None:
                    dve.wait_ge(aeT_ready, k + 1)
                    if k >= 2:
                        dve.wait_ge(ao_ready, k - 1)
                    dve.tensor_copy(a_eT[k % 2], T[:, k % 2, 0:384]).then_inc(aeT_out, 1)
                k = head_at(p, 0)
                if k is not None:
                    g, h = k // AH, k % AH
                    s = scr[:, k % 2, :]
                    if h == 0:
                        dve.wait_ge(rel_loaded[g], 32)
                    dve.wait_ge(as_ready, k + 1)
                    if k >= 2:
                        dve.wait_ge(ae_ready, k - 1)
                    dve.scalar_tensor_tensor(s, AC[:, 2, 0:384], ADH ** -0.5, rel[g][:, h, :], ALU.mult, ALU.add)
                    dep()
                    dve.tensor_reduce(amx[:, 2 * k:2 * k + 1], s[:, 0:P], AX.X, ALU.max)
                    dve.tensor_reduce(amx[:, 2 * k + 1:2 * k + 2], s[:, P:384], AX.X, ALU.max)
                    dep()
                    dve.tensor_scalar(anm[:, 2 * k:2 * k + 2], amx[:, 2 * k:2 * k + 2], -1.0, None, ALU.mult).then_inc(as_out, 1)
                if p % UP == UP - 1 and p < U_GATE - POS0:
                    j = p // UP + 3
                    read_tile(tile(j), (AC, G)[j % 2], done(POS0 + p + 1))
            dve.memset(ones_b, 1.0)
            dve.tensor_tensor(aM, amx[:, 0:8], amx[:, 8:16], ALU.max)
            dep()
            dve.tensor_tensor(aM, aM, amx[:, 16:24], ALU.max)
            dep()
            dve.tensor_tensor(adiff.rearrange("p (g n) -> p g n", g=3), amx.rearrange("p (g n) -> p g n", g=3),
                              aM.unsqueeze(1).to_broadcast([P, 3, 8]), ALU.subtract).then_inc(lse_diff, 1)
            dve.wait_ge(lse_exp, 1)
            dve.tensor_tensor(aden, aden, afac, ALU.mult)
            dep()
            dve.tensor_reduce(aD, aden.rearrange("p (g n) -> p n g", g=3), AX.X, ALU.add)
            dep()
            dve.reciprocal(aD, aD)
            dep()
            dve.tensor_tensor(afac.rearrange("p (g n) -> p g n", g=3), afac.rearrange("p (g n) -> p g n", g=3),
                              aD.unsqueeze(1).to_broadcast([P, 3, 8]), ALU.mult)
            dep()
            dve.wait_ge(ao_out, N_AH)
            for g in range(3):
                for h in range(AH):
                    for t in range(TOK):
                        k = (g * AH + h) * 2 + t
                        o, a = tile(3 * g)[:, t, h * ADH:(h + 1) * ADH], tile(0)[:, t, h * ADH:(h + 1) * ADH]
                        if g == 0:
                            dve.tensor_scalar(o, o, afac[:, k:k + 1], None, ALU.mult)
                        else:
                            i = dve.scalar_tensor_tensor(a, o, afac[:, k:k + 1], a, ALU.mult, ALU.add)
                if g < 2:
                    dep()
            i.then_inc(att_ready, 1)
            down_los(T_ATT, 0, 2)
            dve.wait_ge(gate_read, N_GATE)
            dve.wait_ge(unit_used, done(U_WO))
            for n in range(2):
                i = dve.tensor_tensor(tile(4 + n), tile(4 + n), acc_ct[:, :, n, :], ALU.mult)
                if n == 1:
                    i.then_inc(acc_free, 1)
                dve.tensor_tensor(tile(10 + n), tile(10 + n), tile(1 + n), ALU.mult)
            dep()
            for n in range(2):
                dve.tensor_tensor(tile(10 + n), tile(10 + n), tile(4 + n), ALU.add).then_inc(merged_ready, 1)
            down_los(T_MERGE, 0, 4)
            def gated_residual(g, n_done):
                dve.wait_ge(unit_used, n_done)
                tmp = arena[:, 10240:12288].rearrange("p (t n) -> p t n", t=TOK)
                dve.tensor_tensor(tmp, AC_tok, wide(mod[:, g * D:(g + 1) * D]), ALU.mult).then_inc(acc_free, 1)
                dep()
                dve.tensor_tensor(x_sb[:, :, :], x_sb[:, :, :], tmp, ALU.add).then_inc(x1_ready, 1)

            dve.wait_ge(mod_out, N_ADA)
            gated_residual(2, done(U_MLP))
            dve.wait_ge(sumsq_ready, 2)
            rstd(R_NORM2, sm[:, 16:18], 1.0 / D, 1e-6)
            modulated(4, 3, norm2_loaded)
            lo(T_H2, xT_hi, xT_lo, 0, 4)
            lo(T_H2 + 2, xT_hi, xT_lo, 4, 4)
            def mlp_hidden(e):
                dve.wait_ge(act_out, e + 1)
                dve.tensor_tensor(tile(1), tile(0), tile(0), ALU.mult).then_inc(ffn_h, 1)

            mlp_hidden(0)
            with dve.Fori(0, FF_TILES - 1) as e:
                lo(e * 2 + T_MLP, yT_hi, yT_lo, 0, 4)
                mlp_hidden(e + 1)
            lo(T_MLP + 2 * (FF_TILES - 1), yT_hi, yT_lo, 0, 4)
            gated_residual(5, done(U_LAYERS))
            dve.wait_ge(sumsq_ready, 3)
            dve.wait_ge(normf_loaded, 16)
            rstd(R_FINAL, sm[:, 16:18], 1.0 / D, 1e-6)
            for t in range(TOK):
                dve.scalar_tensor_tensor(x_sb[:, t, :], x_sb[:, t, :], sm[:, 16 + t:17 + t], W[:, D:2 * D], ALU.mult, ALU.mult)
            dve.wait_ge(pos_loaded, 32)
            pos, ang, turns = sm[:, 18:20], sm[:, 128:160], sm[:, 160:192]
            dve.tensor_copy(pos, pos_i[:, :])
            dep()
            for t in range(TOK):
                dve.tensor_scalar(ang[:, t * 16:(t + 1) * 16], inv_row, pos[:, t:t + 1], None, ALU.mult)
            dep()
            big = 1.5 * 2.0 ** 23
            c2 = float(np.float32(2 * np.pi - 6.28125))
            c3 = 2 * np.pi - 6.28125 - c2
            for quarter, dst in ((0.0, sm[:, 64:96]), (0.25, sm[:, 96:128])):
                dve.tensor_scalar(turns, ang, 1 / (2 * np.pi), quarter, ALU.mult, ALU.add)
                dep()
                dve.tensor_scalar(turns, turns, big, None, ALU.add)
                dep()
                dve.tensor_scalar(turns, turns, big, None, ALU.subtract)
                dep()
                dve.scalar_tensor_tensor(dst, turns, -6.28125, ang, ALU.mult, ALU.add)
                dep()
                dve.scalar_tensor_tensor(dst, turns, -c2, dst, ALU.mult, ALU.add)
                dep()
                dve.scalar_tensor_tensor(dst, turns, -c3, dst, ALU.mult, ALU.add)
                dep()
                dve.tensor_scalar(dst, dst, quarter * 2 * np.pi, 3.1415925, ALU.add, ALU.min)
                dep()
                i = dve.tensor_scalar(dst, dst, -3.1415925, None, ALU.max)
                if quarter == 0.0:
                    dep()
            i.then_inc(ang_ready, 1)
            dve.wait_ge(trig_ready, 1)
            dve.memset(sm[:, 893:894], 0.0).then_inc(x_ready, 1)

            def layer_norm(n, g, b, out_sem):
                dep()
                xh = x_sb[:, :, :].rearrange("p t (c n) -> p t c n", n=NT)
                for t in range(TOK):
                    for c in range(2):
                        dve.bn_stats(bst[:, 2 * t + c, :], xh[:, t, c, :])
                dep()
                for t in range(TOK):
                    dve.bn_aggr(mv[:, t, :], bst[:, 2 * t:2 * t + 2, :])
                dep()
                dve.tensor_copy(sm[:, 16:18], mv[:, 0:2, 1])
                rstd(n, sm[:, 16:18], 1.0, 1e-5)
                for t in range(TOK):
                    dve.tensor_scalar(x_sb[:, t, :], x_sb[:, t, :], mv[:, t, 0:1], sm[:, 16 + t:17 + t], ALU.subtract, ALU.mult)
                dep()
                dve.tensor_tensor(x_sb[:, :, :], x_sb[:, :, :], wide(row2[g]), ALU.mult)
                dep()
                dve.tensor_tensor(x_sb[:, :, :], x_sb[:, :, :], wide(row2[b]), ALU.add).then_inc(out_sem, 1)

            def rope(x1, x2, t1, t2, c, s):
                dve.tensor_tensor(t1, x1, s, ALU.mult)
                dve.tensor_tensor(t2, x2, s, ALU.mult)
                dep()
                dve.tensor_tensor(x1, x1, c, ALU.mult)
                dve.tensor_tensor(x2, x2, c, ALU.mult)
                dep()
                dve.tensor_tensor(x1, x1, t2, ALU.subtract)
                return dve.tensor_tensor(x2, x2, t1, ALU.add)

            def first_max(v, m, hot):
                dve.tensor_reduce(m, v, AX.X, ALU.max)
                dep()
                dve.tensor_tensor(hot, v, m.to_broadcast([P, TOK, 4]), ALU.is_ge)
                dep()
                dve.tensor_tensor(hot, hot, wide(wt4), ALU.mult)
                dep()
                dve.tensor_reduce(r_w[:, :, 0:1], hot, AX.X, ALU.max)
                dep()
                dve.tensor_tensor(hot, hot, r_w[:, :, 0:1].to_broadcast([P, TOK, 4]), ALU.is_equal)
                dep()

            with dve.Fori(0, LAYERS) as l:
                n = l * L_UNITS + U_LAYERS
                tb = l * LT + T_LAYERS
                r = l * LR + R_LAYERS
                lo(tb + LT_X, xT_hi, xT_lo, 0, 4)
                lo(tb + (LT_X + 2), xT_hi, xT_lo, 4, 4)

                def in_tile(j):
                    read_tile(P2[:, :, j * NT:(j + 1) * NT], (G, AC)[j % 2], n + done(L_IN + (j + 1) * UP))

                in_tile(0)
                dep()
                dve.wait_ge(rows_loaded, l * 32 + 32)
                dve.tensor_tensor(GT, P2[:, :, IN2["mg"]:IN2["mg"] + 24], wide(row2["gate_bias"]), ALU.add)
                dep()
                dve.tensor_scalar(SI[:, :, 0:4], GT[:, :, 4:8], -1.0, None, ALU.mult)
                dve.tensor_scalar(SI[:, :, 4:8], GT[:, :, 12:16], -1.0, None, ALU.mult)
                dve.tensor_copy(SI[:, :, 8:16], GT[:, :, 16:24])
                dep()
                dve.scalar_tensor_tensor(sp_e, SI, -1.0, SI, ALU.mult, ALU.min).then_inc(sp_in, 1)
                dve.wait_ge(mla_sumsq, l + 1)
                dve.tensor_scalar(sm[:, 200:202], sm[:, 200:202], 1.0 / 256, 1e-6, ALU.mult, ALU.add)
                rstd(r, sm[:, 202:204], 1.0 / 128, 1e-6)
                dve.reciprocal(sm[:, 200:202], sm[:, 200:202])
                in_tile(1)
                dep()
                for t in range(TOK):
                    dve.scalar_tensor_tensor(P2[:, t, 0:256], P2[:, t, 0:256], sm[:, 200 + t:201 + t], row2["q_norm"], ALU.mult, ALU.mult)
                    i = dve.scalar_tensor_tensor(P2[:, t, 256:384], P2[:, t, 256:384], sm[:, 202 + t:203 + t], row2["kv_norm"], ALU.mult, ALU.mult)
                i.then_inc(cq_ready, 1)
                for j in range(2, N_IN2):
                    in_tile(j)
                dve.wait_ge(sp_exp, l + 1)
                dve.tensor_scalar(w_sp, sp_e, 2.0, None, ALU.add)
                dep()
                dve.reciprocal(w_sp, w_sp)
                dep()
                dve.tensor_tensor(z_sp, sp_e, w_sp, ALU.mult)
                dep()
                dve.tensor_tensor(w_sp, z_sp, z_sp, ALU.mult)
                dep()
                dve.tensor_scalar(q_sp, w_sp, 1.0 / 17, 1.0 / 15, ALU.mult, ALU.add)
                dep()
                for k in (13, 11, 9, 7, 5, 3, 1):
                    dve.tensor_tensor(q_sp, q_sp, w_sp, ALU.mult)
                    dep()
                    dve.tensor_scalar(q_sp, q_sp, 1.0 / k, None, ALU.add)
                    dep()
                dve.scalar_tensor_tensor(q_sp, q_sp, 2.0, z_sp, ALU.mult, ALU.mult)
                dep()
                dve.scalar_tensor_tensor(SP, SI, 0.0, q_sp, ALU.max, ALU.add)
                dep()
                dve.tensor_scalar(cu[:, :, 0:8], SP[:, :, 0:8], -1.0, None, ALU.mult)
                dve.scalar_tensor_tensor(cu[:, :, 8:16], SP[:, :, 8:16], -1.0, wide(ea), ALU.mult, ALU.mult).then_inc(cum_in, 1)
                lo(tb + LT_MLA, yT_hi, yT_lo, 0, 3)
                dve.wait_ge(unit_used, n + done(L_UKV))
                for t in range(TOK):
                    dve.tensor_copy(Q[:, t, :], AC_tok[:, t, 0:MH * QD])
                dep()
                qh = Q.rearrange("p t (h d) -> p t h d", d=QD)
                t1, t2 = [scr[:, b, 0:256].rearrange("p (t h n) -> p t h n", t=TOK, h=MH) for b in range(2)]
                hr = ROPE // 2
                rope(qh[:, :, :, NOPE:NOPE + hr], qh[:, :, :, NOPE + hr:QD], t1, t2,
                     *[v.unsqueeze(2).to_broadcast([P, TOK, MH, hr]) for v in (cosM, sinM)]).then_inc(q_ready, 1)
                dep()
                kr = P2[:, :, IN2["kr"]:IN2["kr"] + ROPE]
                rope(kr[:, :, 0:hr], kr[:, :, hr:ROPE], scr[:, 0, 0:32].rearrange("p (t n) -> p t n", t=TOK),
                     scr[:, 1, 0:32].rearrange("p (t n) -> p t n", t=TOK), cosM, sinM)
                dep()
                dve.wait_ge(kv_out, l * TOK + TOK)
                dve.tensor_copy(KF.rearrange("p t (h d) -> p t h d", d=QD)[:, :, :, NOPE:QD],
                                kr.unsqueeze(2).to_broadcast([P, TOK, MH, ROPE])).then_inc(kv_ready, 1)
                dve.wait_ge(cum_ready, l + 1)
                for d in range(2):
                    dve.tensor_copy(cs.rearrange("p t (k d h) -> p t k d h", k=2, d=2)[:, :, :, d, :],
                                    G[:, 0, 32 * d:32 * d + 32].rearrange("p (t k d h) -> p t k d h", t=TOK, k=2, d=2)[:, :, :, d, :])
                dep()
                for d in range(2):
                    dve.tensor_tensor(rw[:, :, 4 * d:4 * d + 4], GT[:, :, 8 * d:8 * d + 4], cs[:, :, 4 * d:4 * d + 4], ALU.subtract)
                dve.tensor_copy(rw[:, :, 8:16], cs[:, :, 8:16])
                dve.tensor_scalar(ncs.rearrange("p (t c) -> p t c", t=TOK), cs[:, :, 8:16], -1.0, None, ALU.mult).then_inc(rows_w, 1)

                def mla_eT(h):
                    dve.wait_ge(meT_ready, l * MH + (h + 1))
                    if h >= 2:
                        dve.wait_ge(mo_ready, l * MH + (h - 1))
                    dve.tensor_copy(meT[:, h % 2, :], T[:, h % 2, :]).then_inc(meT_out, 1)

                def mla_out(h):
                    dve.wait_ge(mo_ready, l * MH + (h + 1))
                    dve.reciprocal(mrden[:, 2 * h:2 * h + 2], mden[:, 2 * h:2 * h + 2])
                    dep()
                    dve.tensor_tensor(HB[:, :, h * MV:(h + 1) * MV], AC[:, h % 2, 0:2 * MV].rearrange("p (t n) -> p t n", t=TOK),
                                      mrden[:, 2 * h:2 * h + 2].unsqueeze(2).to_broadcast([P, TOK, MV]), ALU.mult).then_inc(mo_out, 1)

                for h in range(MH):
                    dve.wait_ge(ms_ready, l * MH + (h + 1))
                    dve.tensor_reduce(mmax[:, 2 * h:2 * h + 2], G[:, h % 2, :].rearrange("p (t n) -> p t n", t=TOK), AX.X, ALU.max)
                    dep()
                    dve.tensor_scalar(mnm[:, 2 * h:2 * h + 2], mmax[:, 2 * h:2 * h + 2], -QD ** -0.5, None, ALU.mult).then_inc(mmax_ready, 1)
                    if h >= 1:
                        mla_eT(h - 1)
                    if h >= 2:
                        mla_out(h - 2)
                mla_eT(MH - 1)
                mla_out(MH - 2)
                mla_out(MH - 1)
                by_c = [v.rearrange("p (t c) -> p t c", t=TOK) for v in (lMx, lfloor, lden)]
                dve.wait_ge(meT_out, l * MH + MH)
                for j in range(2 * LH):
                    dve.wait_ge(lrow_ready, l * 8 + (j + 1))
                    dve.tensor_tensor(lw[:, j, :, :], wide(G[:, j % 2, 0:S]), (mask_f, mask_b)[j % 2], ALU.add).then_inc(lrow_out, 1)
                dep()
                for j in range(2 * LH):
                    c = j % 2 * LH + j // 2
                    dve.tensor_reduce(by_c[0][:, :, c:c + 1], lw[:, j, :, :], AX.X, ALU.max)
                dep()
                dve.tensor_scalar(lnm, lMx, -1.0, None, ALU.mult)
                dve.tensor_tensor(by_c[1], by_c[0], cs[:, :, 0:8], ALU.add).then_inc(lmax_ready, 1)
                for j in range(2 * LH):
                    c, h = j % 2 * LH + j // 2, j // 2
                    dve.wait_ge(lexp_ready, l * 8 + (j + 1))
                    dve.wait_ge(lqk_ready, l * LH + (h + 1))
                    for t in range(TOK):
                        dve.scalar_tensor_tensor(lw[:, j, t, :], AC[:, h, t * S:(t + 1) * S], LDH ** -0.5, lw[:, j, t, :],
                                                 ALU.mult, ALU.mult, accum_out=lden[:, t * 8 + c:t * 8 + c + 1])
                dep()
                dve.scalar_tensor_tensor(lden, lden, -1.0, lden, ALU.mult, ALU.max)
                dep()
                dve.tensor_tensor(lden, lden, lfloor, ALU.max)
                dep()
                dve.reciprocal(lden, lden)
                dep()
                for h in range(LH):
                    for t in range(TOK):
                        kb = t * 8 + LH + h
                        dve.tensor_scalar(lw[:, 2 * h + 1, t, :], lw[:, 2 * h + 1, t, :], lden[:, kb:kb + 1], None, ALU.mult)
                    dep()
                    for t in range(TOK):
                        kf = t * 8 + h
                        i = dve.scalar_tensor_tensor(lw[:, 2 * h, t, :], lw[:, 2 * h, t, :], lden[:, kf:kf + 1], lw[:, 2 * h + 1, t, :], ALU.mult, ALU.add)
                    i.then_inc(lp_ready, 1)
                dve.wait_ge(lnum_ready, l * LH + LH)
                num = G[:, 0, :].rearrange("p (k n) -> p k n", n=LDH)
                cen8, csq8 = [v.rearrange("p (k n) -> p k n", n=LDH) for v in (cen, csq)]
                dve.tensor_reduce(lsum, num, AX.X, ALU.add)
                dep()
                dve.tensor_scalar(lsum, lsum, -1.0 / LDH, None, ALU.mult)
                dep()
                dve.tensor_tensor(cen8, num, lsum.unsqueeze(2).to_broadcast([P, 8, LDH]), ALU.add)
                dep()
                dve.tensor_tensor(csq, cen, cen, ALU.mult)
                dep()
                dve.tensor_reduce(sm[:, 64:72], csq8, AX.X, ALU.add)
                rstd(r + 1, sm[:, 64:72], 1.0 / LDH, 1e-5)
                dve.tensor_tensor(cen8, cen8, sm[:, 64:72].unsqueeze(2).to_broadcast([P, 8, LDH]), ALU.mult)
                dep()
                cen2 = cen.rearrange("p (t n) -> p t n", t=TOK)
                dve.tensor_tensor(cen2, cen2, wide(row2["mlstm_norm"]), ALU.mult)
                dep()
                dve.wait_ge(lgate, l + 1)
                dve.tensor_tensor(HB[:, :, 512:768], cen2, P2[:, :, IN2["mo"]:IN2["mo"] + 256], ALU.mult)
                dve.memset(xpad[:, :, 0:2], 0.0)
                dve.memset(xpad[:, :, S + 2:S + 4], 0.0)
                dep()
                dve.wait_ge(sx_out, l * 3 + 3)
                for k in range(CONV):
                    for c in range(XBC_CH):
                        src = xpad[:, c, k:k + S]
                        if k == 0:
                            dve.tensor_scalar(xc[:, c, :], src, cv_w[:, c, 0:1], None, ALU.mult)
                        else:
                            i = dve.scalar_tensor_tensor(xc[:, c, :], src, cv_w[:, c, k:k + 1], xc[:, c, :], ALU.mult, ALU.add)
                    if k < CONV - 1:
                        dep()
                i.then_inc(conv_done, 1)
                for j in range(2 * SH):
                    dve.wait_ge(srow_ready, l * 8 + (j + 1))
                    dve.tensor_tensor(sw[:, j, :, :], wide(AC[:, 2 + j % 2, 0:S]), (mask_b, mask_f)[j % 2], ALU.add).then_inc(srow_out, 1)
                    if j == 0:
                        dve.wait_ge(sxt_T, l + 1)
                        dve.tensor_copy(XT, T[:, 0, :].rearrange("p (t n) -> p t n", t=TOK))
                dep()
                xh = XT.rearrange("p t (h n) -> p t h n", h=SH)
                for d in range(2):
                    dve.tensor_tensor(xdt[:, :, d, :].rearrange("p t (h n) -> p t h n", h=SH), xh,
                                      SP[:, :, 8 + 4 * d:12 + 4 * d].unsqueeze(3).to_broadcast([P, TOK, SH, SP_]), ALU.mult)
                dep()
                dve.wait_ge(scb_ready, l * SG + SG)
                for j in range(2 * SH):
                    dve.wait_ge(sexp_ready, l * 8 + (j + 1))
                    dve.tensor_tensor(sw[:, j, :, :], sw[:, j, :, :], AC[:, j // 4, :].rearrange("p (t n) -> p t n", t=TOK), ALU.mult)\
                       .then_inc(sw_ready, 1)
                dve.wait_ge(conv_act, l + 1)
                ysh = ys.rearrange("p t (h n) -> p t h n", h=SH)
                dve.tensor_tensor(ysh, xh, row2["d_skip"].unsqueeze(1).unsqueeze(3).to_broadcast([P, TOK, SH, SP_]), ALU.mult)
                dep()
                dve.wait_ge(sy_ready, l * SH + SH)
                dve.tensor_tensor(ys, ys, T[:, 1, :].rearrange("p (t n) -> p t n", t=TOK), ALU.add).then_inc(sy_out, 1)
                dep()
                dve.tensor_tensor(ys, ys, P2[:, :, IN2["z"]:IN2["z"] + 256], ALU.mult)
                dep()
                dve.tensor_tensor(ysq, ys, ys, ALU.mult)
                dep()
                dve.tensor_reduce(sm[:, 64:68], ysq.rearrange("p t (g n) -> p (t g) n", g=SG), AX.X, ALU.add)
                rstd(r + 2, sm[:, 64:68], 1.0 / P, 1e-6)
                ysg = ys.rearrange("p t (g n) -> p (t g) n", g=SG)
                dve.tensor_tensor(ysg, ysg, sm[:, 64:68].unsqueeze(2).to_broadcast([P, 4, P]), ALU.mult)
                dep()
                dve.tensor_tensor(HB[:, :, 768:1024], ys, wide(row2["ssd_norm"]), ALU.mult).then_inc(heads_ready, 1)
                down_los(tb + LT_OUT, 0, 4)
                dve.wait_ge(unit_used, n + done(L_ROUTER))
                dve.scalar_tensor_tensor(x_sb[:, :, :], x_sb[:, :, :], ALPHA, AC_tok, ALU.mult, ALU.add).then_inc(acc_free, 1)
                layer_norm(r + 3, "ln1_g", "ln1_b", x2_ready)
                lo(tb + LT_X2, xT_hi, xT_lo, 0, 4)
                lo(tb + (LT_X2 + 2), xT_hi, xT_lo, 4, 4)
                dve.wait_ge(unit_used, n + done(L_MOE))
                dve.tensor_tensor(rlog, G[:, :, 0:EGROUPS + EXPERTS], wide(row2["router_b"]), ALU.add).then_inc(g_free, 1)
                dep()
                first_max(rlog[:, :, 0:4], r_m[:, :, 0:1], r_g)
                dve.tensor_tensor(rt_e[:, :, 0:4], rlog[:, :, 0:4], r_m[:, :, 0:1].to_broadcast([P, TOK, 4]), ALU.subtract)
                dve.tensor_tensor(r_pr, rlog[:, :, 4:20].rearrange("p t (g e) -> p t g e", g=EGROUPS),
                                  r_g.unsqueeze(3).to_broadcast([P, TOK, EGROUPS, EPG]), ALU.mult)
                dep()
                dve.tensor_reduce(r_el, r_pr.rearrange("p t g e -> p t e g"), AX.X, ALU.add)
                dep()
                first_max(r_el, r_m[:, :, 0:1], r_1)
                dve.scalar_tensor_tensor(r_el2, r_1, NEG, r_el, ALU.mult, ALU.add)
                dep()
                first_max(r_el2, r_m[:, :, 1:2], r_2)
                dve.tensor_tensor(rt_e[:, :, 4:5], r_m[:, :, 1:2], r_m[:, :, 0:1], ALU.subtract).then_inc(gexp_in, 1)
                dve.wait_ge(gexp_out, l + 1)
                dve.tensor_reduce(r_w[:, :, 0:1], rt_e[:, :, 0:4], AX.X, ALU.add)
                dve.tensor_scalar(r_w[:, :, 1:2], rt_e[:, :, 4:5], 1.0, None, ALU.add)
                dep()
                dve.tensor_tensor(r_w[:, :, 2:3], r_w[:, :, 0:1], r_w[:, :, 1:2], ALU.mult)
                dep()
                dve.reciprocal(r_w[:, :, 2:3], r_w[:, :, 2:3])
                dve.tensor_tensor(r_2, r_2, rt_e[:, :, 4:5].to_broadcast([P, TOK, 4]), ALU.mult)
                dep()
                dve.tensor_tensor(r_1, r_1, r_2, ALU.add)
                dep()
                dve.tensor_tensor(r_1, r_1, r_w[:, :, 2:3].to_broadcast([P, TOK, 4]), ALU.mult)
                dep()
                dve.tensor_tensor(comb.rearrange("p (t g e) -> p t g e", t=TOK, g=EGROUPS),
                                  r_g.unsqueeze(3).to_broadcast([P, TOK, EGROUPS, EPG]),
                                  r_1.unsqueeze(2).to_broadcast([P, TOK, EGROUPS, EPG]), ALU.mult)
                dep()

                def moe_hidden(e0, e):
                    dve.wait_ge(act_out, l * EXPERTS + e0 + (FF_TILES + e + 1))
                    for t in range(TOK):
                        i = dve.scalar_tensor_tensor(moe_h[:, t, :], ffn_a[:, t, :], comb[:, bass.ds(e0 + (t * EXPERTS + e), 1)],
                                                     G[:, t, DE:2 * DE], ALU.mult, ALU.mult)
                    i.then_inc(ffn_h, 1)

                moe_hidden(0, 0)
                with dve.Fori(0, 3) as e4:
                    for q in range(4):
                        lo(e4 * 8 + (tb + (LT_MOE + 2 * q)), yT_hi, yT_lo, 0, 2)
                        moe_hidden(e4 * 4, q + 1)
                for e in range(12, EXPERTS):
                    lo(tb + (LT_MOE + 2 * e), yT_hi, yT_lo, 0, 2)
                    if e + 1 < EXPERTS:
                        moe_hidden(0, e + 1)
                dve.wait_ge(unit_used, n + done(L_UNITS))
                dve.scalar_tensor_tensor(x_sb[:, :, :], x_sb[:, :, :], ALPHA, AC_tok, ALU.mult, ALU.add).then_inc(acc_free, 1)
                layer_norm(r + 4, "ln2_g", "ln2_b", x_ready)


def up_units(w):
    n = w.shape[1] // NT
    return w.reshape(UP, 2, P, n, NT).transpose(3, 0, 2, 1, 4).reshape(n * UP, P, UNIT)


def down_units(w):
    return w.reshape(-1, P, UNIT)


def padded(w, cols):
    return np.concatenate([w, np.zeros(w.shape[:-1] + (cols - w.shape[-1],), np.float32)], axis=-1)


def ffn_units(ups, downs):
    parts = [ups[0]]
    for e in range(len(ups)):
        if e + 1 < len(ups):
            parts.append(ups[e + 1])
        parts.append(downs[e])
    return parts


def weight_stream(a):
    w_in = up_units(a["w_in"][0])
    parts = [w_in[:U_RET_OUT], down_units(a["w_ret_out"][0]), w_in[U_RET_OUT:], down_units(a["w_att_out"][0]), down_units(a["w_o"][0])]
    ff1 = up_units(a["w_ff1"][0]).reshape(FF_TILES, UP, P, UNIT)
    ff2 = down_units(a["w_ff2"][0]).reshape(FF_TILES, 4, P, UNIT)
    parts += ffn_units(ff1, ff2)
    for l in range(LAYERS):
        w = a["w_in_2"][l]
        at, sizes = {}, (("cq", 256), ("ckv", 128), ("kr", 32), ("mq", 256), ("mk", 256), ("mv", 256), ("mo", 256),
                         ("mg", 16), ("z", 256), ("xbc", XBC), ("dt", 8))
        c = 0
        for name, n in sizes:
            at[name] = w[:, c:c + n]
            c += n
        first = padded(np.concatenate([at[k] for k in ("cq", "ckv", "kr", "mg", "dt")], axis=1), NT)
        rest = np.concatenate([at[k] for k in ("mq", "mk", "mv", "mo", "xbc", "z")], axis=1)
        parts.append(up_units(np.concatenate([first, rest], axis=1)))
        parts.append(padded(a["mla_w_uq_2"][l].reshape(2, P, MH * QD), UNIT))
        parts.append(a["mla_w_ukv_2"][l].reshape(1, P, UNIT))
        parts.append(down_units(a["w_out_2"][l]))
        we = a["router_expert_w_2"][l].transpose(1, 0, 2).reshape(D, EXPERTS)
        router = np.concatenate([a["router_group_w_2"][l], we], axis=1)
        parts.append(padded(router.reshape(KC, P, -1).transpose(1, 0, 2).reshape(1, P, -1), UNIT))
        both = np.concatenate([a["expert_w_gate_2"][l], a["expert_w_up_2"][l]], axis=2)
        parts += ffn_units([up_units(w) for w in both], [down_units(w) for w in a["expert_w_down_2"][l]])
    units = np.concatenate(parts, axis=0).reshape(UNITS // RAW, RAW, P, UNIT)
    ada = a["w_ada"][0].reshape(KC, P, N_ADA, D).transpose(2, 0, 1, 3)
    units = np.insert(units, ADA_BEFORE, ada, axis=0)
    return np.ascontiguousarray(units.reshape(-1, PIECE, P, UNIT).transpose(0, 2, 1, 3)).reshape(-1, P, PIECE * UNIT)


def bucket_of(dist):
    exact = BUCKETS // 2
    d = np.maximum(dist, 1).astype(np.float32)
    scale = np.float32(np.log(MAX_DIST / exact))
    large = exact + (np.log(d / np.float32(exact)) / scale * np.float32(BUCKETS - exact)).astype(np.int32)
    return np.where(dist < exact, dist, np.minimum(large, BUCKETS - 1))


def shape_constants():
    f = np.float32
    idx = np.arange(P, dtype=f)
    log_g = np.log1p(-(2.0 ** (-5.0 - np.arange(RH))))
    s, t = np.arange(P)[:, None], np.arange(S)[None, :]
    dec = np.where(t >= s, np.exp(log_g[:, None, None] * np.maximum(t - s, 0)), 0.0) * RDK ** -0.5
    decay = np.concatenate([dec, dec[:, :, 0:P]], axis=2).transpose(1, 0, 2).reshape(P, -1).astype(f)
    half = RDK // 2
    inv = f(10000.0) ** (-np.arange(half, dtype=f) / f(half))
    ang = np.arange(S, dtype=f)[:, None] * inv[None, :]
    by_p = lambda v: v.reshape(TOK, P, half).transpose(1, 0, 2).reshape(P, -1).astype(f)
    const1 = np.concatenate([decay, by_p(np.cos(ang)), by_p(np.sin(ang))], axis=1)
    onehot = np.zeros((BUCKETS + 1, len(GROUPS), NT), f)
    for g, (win, dil) in enumerate(GROUPS):
        for c in range(NT):
            d = S - 1 - c
            ok = 0 <= d <= win and d % dil == 0
            onehot[bucket_of(np.array([d]))[0] if ok else BUCKETS, g, c] = 1.0
    u, v = np.arange(P)[:, None], np.arange(P)[None, :]
    tri_f, tri_b = (u <= v).astype(f), (u >= v).astype(f)
    first, second = np.arange(S)[:, None], np.arange(S)[None, :]
    tiles = lambda m: m.reshape(TOK, P, S).transpose(1, 0, 2).reshape(P, -1)
    mask_f = tiles(np.where(second <= first, 0.0, NEG).astype(f))
    mask_b = tiles(np.where(second >= first, 0.0, NEG).astype(f))
    const2 = np.concatenate([tri_f, tri_b, np.ones((P, P), f), mask_f, mask_b], axis=1)
    select = np.zeros((16, 16, P), f)
    for c in range(16):
        select[c, c, :] = 1.0
    hr = ROPE // 2
    inv_freq = f(10000.0) ** (-np.arange(0, ROPE, 2, dtype=f) / f(ROPE))
    return {"identity": np.eye(P, dtype=f), "const1": const1, "onehot": onehot.reshape(BUCKETS + 1, -1), "const2": const2,
            "row_select": select.reshape(16, -1), "inv_freq": inv_freq.astype(f).reshape(hr)}


def kernel(**inputs):
    import concourse.bacc as bacc
    from concourse.bass_utils import run_bass_kernel_spmd

    a = {k: np.asarray(v) for k, v in inputs.items()}
    arrays = shape_constants()
    arrays["w_stream"] = weight_stream(a)
    arrays["c_col"] = a["c"].reshape(KC, P).T
    arrays["x"] = a["x"]
    arrays["rel_bias"] = a["rel_bias"]
    arrays["b_ada"] = a["b_ada"]
    for name, src in (("norm1_g", "norm1_g"), ("norm2_g", "norm2_g"), ("norm_f_g", "norm_f_g"), ("gn_g", "ret_gn_g"), ("gn_b", "ret_gn_b")):
        arrays[name] = a[src].reshape(-1)
    arrays["pos_col"] = a["positions_2"].reshape(TOK, P).T
    rows = [np.concatenate([a[n][l].reshape(-1) for n in
                            ("ln1_g_2", "ln1_b_2", "ln2_g_2", "ln2_b_2", "mla_q_norm_2", "mla_kv_norm_2", "mlstm_gate_bias_2",
                             "ssd_dt_bias_2", "ssd_a_log_2", "ssd_d_2", "ssd_norm_2", "mlstm_norm_2", "router_group_b_2",
                             "router_expert_b_2")]) for l in range(LAYERS)]
    arrays["rows2"] = np.stack(rows)
    conv = [np.concatenate([a["ssd_conv_w_2"][l].T.reshape(XBC_CH, P, CONV).transpose(1, 0, 2).reshape(P, -1),
                            a["ssd_conv_b_2"][l].reshape(XBC_CH, P).T], axis=1) for l in range(LAYERS)]
    arrays["conv_col"] = np.stack(conv)
    arrays = {n: np.ascontiguousarray(v) for n, v in arrays.items()}

    nc = bacc.Bacc("TRN2", target_bir_lowering=False, num_devices=1)
    A = {n: nc.dram_tensor(n, v.shape, mybir.dt.from_np(v.dtype), kind="ExternalInput").ap() for n, v in arrays.items()}
    A["rel_scratch"] = nc.dram_tensor("rel_scratch", (N_AH, P + 1, NT), F32, kind="Internal").ap()
    A["out"] = nc.dram_tensor("out", a["x"].shape, F32, kind="ExternalOutput").ap()
    program(nc, A)
    r = run_bass_kernel_spmd(nc, [arrays], core_ids=[0])
    return r.results[0]["out"]
```

```python
from contextlib import ExitStack

import concourse.bass as bass
import numpy as np
from concourse import mybir

F32 = mybir.dt.float32
F32R = mybir.dt.float32r
I32 = mybir.dt.int32
ALU = mybir.AluOpType
ACT = mybir.ActivationFunctionType
AX = mybir.AxisListType

P = 128
S = 256
TOK = S // P
D = 1024
KC = D // P
NT = 512
RH, RDK, RDV = 4, 256, 512
GROUPS = ((128, 1), (512, 4), (2048, 16))
AH, ADH = 4, 128
N_AH = len(GROUPS) * AH
BUCKETS, MAX_DIST = 32, 2048
FF_TILES = 4096 // NT
LAYERS = 2
MH, NOPE, ROPE, MV = 8, 64, 32, 64
QD = NOPE + ROPE
LH, LDH = 4, 64
SH, SP_, SG, SN = 4, 64, 2, 128
CONV = 5
XBC = SH * SP_ + 2 * SG * SN
XBC_CH = XBC // P
EXPERTS, EGROUPS, EPG = 16, 4, 4
DE = 256
ALPHA = (2 * LAYERS) ** 0.25
NEG = -1e30

UNIT = 1024
SLOTS = 4
RAW = 8
PIECE = 2
UP = 4
N_RET_IN = 12
N_ATT_IN = 9
N_GATE = 4
U_RET_IN = 0
U_ATT_FIRST = U_RET_IN + N_RET_IN * UP
U_RET_OUT = U_ATT_FIRST + UP
U_ATT_IN = U_RET_OUT + RH * 4
U_GATE = U_ATT_IN + (N_ATT_IN - 1) * UP
U_ATT_OUT = U_GATE + N_GATE * UP
U_WO = U_ATT_OUT + 4
U_MLP = U_WO + 8
U_LAYERS = U_MLP + FF_TILES * 8
ADA_BEFORE = (0, 0, 2, 4, 5, 8)
ADA_ORDER = (1, 0, 2, 3, 4, 5)
N_ADA = len(ADA_BEFORE)
assert KC == RAW
L_IN = 0
N_IN2 = 5
L_UKV = L_IN + 2 * UP
L_UQ = L_UKV + 1
L_REST = L_UQ + 2
N_POS2 = 3 * UP
L_OUT = L_REST + N_POS2
L_ROUTER = L_OUT + 8
L_MOE = L_ROUTER + 1
L_UNITS = L_MOE + EXPERTS * 6
UNITS = U_LAYERS + LAYERS * L_UNITS
assert UNITS % RAW == 0 and L_UNITS % RAW == 0 and U_LAYERS % RAW == 0

M_ATT_IN = 8
M_LAYERS = M_ATT_IN + N_ATT_IN
LM_ROUTER = N_IN2
LM = LM_ROUTER + 1
T_H1 = 0
T_RET = T_H1 + 4
T_ATT = T_RET + 4 * RH
T_MERGE = T_ATT + 4
T_H2 = T_MERGE + 8
T_MLP = T_H2 + 4
T_LAYERS = T_MLP + 2 * FF_TILES
LT_X = 0
LT_MLA = LT_X + 4
LT_OUT = LT_MLA + 2
LT_X2 = LT_OUT + 8
LT_MOE = LT_X2 + 4
LT = LT_MOE + 2 * EXPERTS
R_GN = 1
R_NORM2 = R_GN + RH
R_FINAL = R_NORM2 + TOK
R_LAYERS = R_FINAL + 1
LR = 7
ACC_ATT = 2
ACC_WO = 3
ACC_MLP = 4
ACC_LAYERS = 4
LACC = 2
G_CREDIT = 2

ROW2 = {}
_at = 0
for _n, _w in (("ln1_g", D), ("ln1_b", D), ("ln2_g", D), ("ln2_b", D), ("q_norm", 256), ("kv_norm", 128),
               ("gate_bias", 24), ("a_log", 8), ("d_skip", 4), ("ssd_norm", 256), ("mlstm_norm", 256),
               ("router_b", 20)):
    ROW2[_n] = (_at, _at + _w)
    _at += _w
ROWS2 = _at

IN2 = {"cq": 0, "ckv": 256, "kr": 384, "mg": 416, "dt": 432, "xbc": 512, "z": 1280,
       "mq": 1536, "mk": 1792, "mv": 2048, "mo": 2304}


POS0 = U_ATT_IN + 2 * UP
N_POS = U_ATT_OUT - POS0
PER_GROUP = 3 * UP


def head_at(p, after):
    q = p - after
    g, h = q // PER_GROUP, q % PER_GROUP // 2
    return g * AH + h if q >= 0 and q % 2 == 0 and g < len(GROUPS) and h < AH else None


def turn_at(p):
    g, n = (p + UP) // PER_GROUP, (p + UP) % PER_GROUP
    return (g, n) if n < 4 and g < len(GROUPS) else None


def ring_round(r):
    return r + sum(b <= r for b in ADA_BEFORE)


def ada_round(i):
    return i + ADA_BEFORE[i]


def program(nc, A):
    ctx = ExitStack()
    with ctx:
        def sb(name, shape, dt=F32):
            return ctx.enter_context(nc.sbuf_tensor(name, shape, dt))

        def pb(name, shape):
            return ctx.enter_context(nc.psum_tensor(name, shape, F32))

        def sem(name):
            return ctx.enter_context(nc.semaphore(name))

        w_raw = sb("w_raw", [P, RAW, UNIT])
        w_hi = sb("w_hi", [P, SLOTS, UNIT], F32R)
        w_lo = sb("w_lo", [P, SLOTS, UNIT], F32R)
        xT_hi = sb("xT_hi", [P, KC, S], F32R)
        xT_lo = sb("xT_lo", [P, KC, S], F32R)
        yT_hi = sb("yT_hi", [P, 4, S], F32R)
        yT_lo = sb("yT_lo", [P, 4, S], F32R)
        zero_r = sb("zero_r", [1, P], F32R)
        x_sb = sb("x_sb", [P, TOK, D])
        mod = sb("mod", [P, 6 * D])
        ident = sb("ident", [P, P])
        arena = sb("arena", [P, 20480])
        scr = sb("scr", [P, 2, 384])
        sm = sb("sm", [P, 896])
        pos_i = sb("pos_i", [P, TOK], I32)
        G = pb("G", [P, 2, NT])
        AC = pb("AC", [P, 4, NT])
        T = pb("T", [P, 2, NT])
        AC_tok = AC[:, :, :].rearrange("p (t c) n -> p t (c n)", t=TOK)

        raw_landed = [sem("raw_landed%d" % s) for s in range(RAW // PIECE)]
        c_loaded = sem("c_loaded")
        mod_cleared_a = sem("mod_cleared_a")
        ada_b_loaded = sem("ada_b_loaded")
        ada_used = sem("ada_used")
        x_loaded = sem("x_loaded")
        norm1_loaded = sem("norm1_loaded")
        ident_loaded = sem("ident_loaded")
        cst_loaded = sem("cst_loaded")
        pos_loaded = sem("pos_loaded")
        lo_ready = sem("lo_ready")
        x_ready = sem("x_ready")
        out_stored = sem("out_stored")
        mod_cleared_b = sem("mod_cleared_b")
        hi_ready = sem("hi_ready")
        sexp_ready = sem("sexp_ready")
        sw_ready = sem("sw_ready")
        unit_used = sem("unit_used")
        t_ready = sem("t_ready")
        t_hi = sem("t_hi")
        var_ready = sem("var_ready")
        std_ready = sem("std_ready")
        act_out = sem("act_out")
        mod_sum = sem("mod_sum")
        mod_out = sem("mod_out")
        bias_in_loaded = sem("bias_in_loaded")
        ada_b2_loaded = sem("ada_b2_loaded")
        c_ready = sem("c_ready")
        bias_row = sem("bias_row")
        bias_rows_out = sem("bias_rows_out")
        sumsq_ready = sem("sumsq_ready")
        bias_stored = sem("bias_stored")
        h_ready = sem("h_ready")
        gn_g_loaded = sem("gn_g_loaded")
        gn_b_loaded = sem("gn_b_loaded")
        rqk_ready = sem("rqk_ready")
        rqk_out = sem("rqk_out")
        ro_ready = sem("ro_ready")
        ro_out = sem("ro_out")
        rg_gated = sem("rg_gated")
        y_ready = sem("y_ready")
        rel_loaded = [sem("rel_loaded%d" % g) for g in range(len(GROUPS))]
        aqk_ready = sem("aqk_ready")
        aqk_out = sem("aqk_out")
        as_out = sem("as_out")
        aeT_ready = sem("aeT_ready")
        ae_ready = sem("ae_ready")
        ao_ready = sem("ao_ready")
        ao_out = sem("ao_out")
        lse_diff = sem("lse_diff")
        lse_exp = sem("lse_exp")
        gate_read = sem("gate_read")
        norm2_loaded = sem("norm2_loaded")
        cst2_loaded = sem("cst2_loaded")
        normf_loaded = sem("normf_loaded")
        ang_ready = sem("ang_ready")
        trig_ready = sem("trig_ready")
        rows_loaded = sem("rows_loaded")
        g_free = sem("g_free")
        mla_sumsq = sem("mla_sumsq")
        sp_in = sem("sp_in")
        sp_exp = sem("sp_exp")
        kv_out = sem("kv_out")
        mqkT_ready = sem("mqkT_ready")
        mqkT_out = sem("mqkT_out")
        sx_T = sem("sx_T")
        sx_out = sem("sx_out")
        rows_T = sem("rows_T")
        rows_out = sem("rows_out")
        mmax_ready = sem("mmax_ready")
        meT_ready = sem("meT_ready")
        me_ready = sem("me_ready")
        lqk_T = sem("lqk_T")
        lqk_out = sem("lqk_out")
        conv_done = sem("conv_done")
        conv_act = sem("conv_act")
        lmax_ready = sem("lmax_ready")
        lpT_ready = sem("lpT_ready")
        lexp_ready = sem("lexp_ready")
        lfl_in = sem("lfl_in")
        lfl_out = sem("lfl_out")
        sxt_T = sem("sxt_T")
        sxt_out = sem("sxt_out")
        scb_ready = sem("scb_ready")
        scb_out = sem("scb_out")
        lnum_ready = sem("lnum_ready")
        lpT_out = sem("lpT_out")
        srow_ready = sem("srow_ready")
        sy_ready = sem("sy_ready")
        lgate = sem("lgate")
        gexp_in = sem("gexp_in")
        gexp_out = sem("gexp_out")
        t_lo = sem("t_lo")
        acc_ready = sem("acc_ready")
        ffn_h = sem("ffn_h")
        tab_wide = sem("tab_wide")
        ada_summed = sem("ada_summed")
        rope_done = sem("rope_done")
        rs_out = sem("rs_out")
        rs_ready = sem("rs_ready")
        acc_free = sem("acc_free")
        aeT_out = sem("aeT_out")
        as_ready = sem("as_ready")
        att_ready = sem("att_ready")
        merged_ready = sem("merged_ready")
        zero_ready = sem("zero_ready")
        cq_ready = sem("cq_ready")
        cum_in = sem("cum_in")
        cum_ready = sem("cum_ready")
        q_ready = sem("q_ready")
        ms_ready = sem("ms_ready")
        meT_out = sem("meT_out")
        mo_out = sem("mo_out")
        mo_ready = sem("mo_ready")
        lrow_ready = sem("lrow_ready")
        q_out = sem("q_out")
        rows_w = sem("rows_w")
        lp_ready = sem("lp_ready")
        lmul_ready = sem("lmul_ready")
        lqk_ready = sem("lqk_ready")
        lstm_ready = sem("lstm_ready")
        x2_ready = sem("x2_ready")
        logits_out = sem("logits_out")
        logits_ready = sem("logits_ready")
        kv_ready = sem("kv_ready")
        heads_ready = sem("heads_ready")

        def tile(j):
            return arena[:, j * 1024:(j + 1) * 1024].rearrange("p (t n) -> p t n", t=TOK)

        qkT = arena[:, 12288:16384].rearrange("p (c s) -> p c s", s=S)
        W = arena[:, 16384:18432]
        decay = arena[:, 18432:19968].rearrange("p (h n) -> p h n", h=RH)
        cosR = arena[:, 19968:20224].rearrange("p (t n) -> p t n", t=TOK)
        sinR = arena[:, 20224:20480].rearrange("p (t n) -> p t n", t=TOK)
        onehot = arena[0:BUCKETS + 1, 0:1536].rearrange("p (g n) -> p g n", g=len(GROUPS))
        tab_bc = arena[0:BUCKETS + 1, 1536:3072].rearrange("p (h n) -> p h n", h=N_AH)
        tab = sm[0:BUCKETS + 1, 480:480 + N_AH]
        row_banks = [T[:, 0, :], T[:, 1, :]] + [AC[:, b, :] for b in range(4)]
        bias_vec = arena[:, 6144:12288].rearrange("p (h n) -> p h n", h=N_AH)
        h_sb = arena[:, 3072:5120].rearrange("p (t n) -> p t n", t=TOK)
        ones_col = sm[:, 894:895]
        norm2_row = arena[:, 12288:13312]
        var = [sm[:, 16 + t:17 + t] for t in range(TOK)]
        ccol, csil = sm[:, 0:8], sm[:, 8:16]
        aqkT = [qkT[:, 8 * b:8 * b + 8, :] for b in range(2)]
        rel = [W[:, 0:1536], mod[:, 0:1536], arena[:, 18432:19968]]
        rel = [r.rearrange("p (h n) -> p h n", h=AH) for r in rel]
        a_e = arena[:, 9 * 1024:9 * 1024 + 768].rearrange("p (b n) -> p b n", b=2)
        a_eT = [W[:, 1536:1920], mod[:, 1536:1920]]
        amx, anm, aden = sm[:, 64:88], sm[:, 88:112], sm[:, 112:136]
        aM, adiff, afac, aD = sm[:, 136:144], sm[:, 144:168], sm[:, 168:192], sm[:, 192:200]

        P2 = arena[:, 0:5120].rearrange("p (t n) -> p t n", t=TOK)
        HB = arena[:, 5120:7168].rearrange("p (t n) -> p t n", t=TOK)
        WK = 7168
        tri_f, tri_b, ones = arena[:, 17024:17152], arena[:, 17152:17280], arena[:, 17280:17408]
        masks, sel = arena[:, 17408:18432], arena[0:32, 18432:18448]
        mask_f, mask_b = yT_lo[:, 0:2, :], yT_lo[:, 2:4, :]
        sel_r, ident_r, rowT = yT_hi[0:32, 0, 0:16], yT_hi[:, 1, 0:P], yT_hi[0:32, 2, :]
        row2 = {n: mod[:, a:b] for n, (a, b) in ROW2.items()}
        V2 = mod[:, ROWS2 + 8:ROWS2 + 8 + 1024].rearrange("p (t n) -> p t n", t=TOK)
        cvw = sm[:, 400:436]
        cv_w, cv_b = cvw[:, 0:30].rearrange("p (c k) -> p c k", k=CONV), cvw[:, 30:36]
        inv_row = sm[:, 436:452]
        cosM = sm[:, 368:400].rearrange("p (t n) -> p t n", t=TOK)
        sinM = sm[:, 860:892].rearrange("p (t n) -> p t n", t=TOK)

        about_zero, about_mean, norm_eps = [sm[:, a:a + 1] for a in (20, 21, 22)]
        Q = arena[:, WK:WK + 1536].rearrange("p (t n) -> p t n", t=TOK)
        KF = arena[:, WK + 1536:WK + 3072].rearrange("p (t n) -> p t n", t=TOK)
        mqT = arena[:, WK + 3096:WK + 5144].rearrange("p (h s) -> p h s", s=S)
        mkT = arena[:, WK + 5144:WK + 7192].rearrange("p (h s) -> p h s", s=S)
        me = arena[:, WK + 7192:WK + 8216].rearrange("p (b t s) -> p b t s", b=2, t=TOK)
        meT = arena[:, WK + 8216:WK + 9240].rearrange("p (b n) -> p b n", b=2)
        mmax, mnm, mden, mrden = sm[:, 64:80], sm[:, 80:96], sm[:, 96:112], sm[:, 112:128]
        lw = arena[:, WK + 3096:WK + 5144].rearrange("p (j t s) -> p j t s", j=4, t=TOK)
        lqkT = [HB[:, c // 2, 512 + c % 2 * S:512 + (c % 2 + 1) * S] for c in range(4)]
        lpT = arena[:, WK + 7192:WK + 8216].rearrange("p (b n) -> p b n", b=2)
        cen = arena[:, WK + 8216:WK + 8728]
        csq = arena[:, WK + 8728:WK + 9240]
        lMx, lnm, lfloor, lden = sm[:, 128:144], sm[:, 144:160], sm[:, 160:176], sm[:, 176:192]
        xpad = arena[:, WK:WK + 1560].rearrange("p (c s) -> p c s", c=XBC_CH)
        xc = arena[:, WK + 1560:WK + 3096].rearrange("p (c s) -> p c s", c=XBC_CH)
        XT = arena[:, WK:WK + 512].rearrange("p (t n) -> p t n", t=TOK)
        xdt = arena[:, WK + 512:WK + 1536].rearrange("p (t d n) -> p t d n", t=TOK, d=2)
        cbs = [scr[:, :, :].rearrange("p b n -> p (b n)")[:, 0:512], arena[:, WK + 1560:WK + 2072]]
        sw = arena[:, WK + 5144:WK + 7192].rearrange("p (j t s) -> p j t s", j=4, t=TOK)
        ys = arena[:, WK + 5144:WK + 5656].rearrange("p (t n) -> p t n", t=TOK)
        ysq = arena[:, WK + 5656:WK + 6168].rearrange("p (t n) -> p t n", t=TOK)
        ffn_a = arena[:, WK:WK + 512].rearrange("p (t n) -> p t n", t=TOK)
        logitsT = arena[0:EGROUPS + EXPERTS, WK + 1024:WK + 1024 + S]
        moe_h = arena[:, WK + 512:WK + 1024].rearrange("p (t n) -> p t n", t=TOK)
        bst = sm[:, 208:304].rearrange("p (k n) -> p k n", n=6)
        mv = sm[:, 304:336].rearrange("p (k n) -> p k n", n=2)
        comb = sm[:, 336:368]
        lsum = sm[:, 72:80]
        wt4 = sm[:, 496:500]
        GT = sm[:, 500:548].rearrange("p (t n) -> p t n", t=TOK)
        SI = sm[:, 548:580].rearrange("p (t n) -> p t n", t=TOK)
        sp_e = sm[:, 580:612].rearrange("p (t n) -> p t n", t=TOK)
        z_sp = sm[:, 612:644].rearrange("p (t n) -> p t n", t=TOK)
        w_sp = sm[:, 644:676].rearrange("p (t n) -> p t n", t=TOK)
        q_sp = sm[:, 676:708].rearrange("p (t n) -> p t n", t=TOK)
        SP = sm[:, 708:740].rearrange("p (t n) -> p t n", t=TOK)
        ea = sm[:, 740:748]
        cu = sm[:, 748:780].rearrange("p (t n) -> p t n", t=TOK)
        cs = sm[:, 780:812].rearrange("p (t n) -> p t n", t=TOK)
        rows16 = sm[:, 812:844].rearrange("p (t n) -> p t n", t=TOK)
        rw = sm[:, 612:676].rearrange("p (t n) -> p t n", t=TOK)
        ncs = sm[:, 844:860]
        rt_e = sm[:, 64:74].rearrange("p (t n) -> p t n", t=TOK)
        rlog = sm[:, 612:652].rearrange("p (t n) -> p t n", t=TOK)
        r_m = sm[:, 652:656].rearrange("p (t n) -> p t n", t=TOK)
        r_g, r_1, r_2 = [sm[:, a:a + 8].rearrange("p (t n) -> p t n", t=TOK) for a in (656, 664, 672)]
        r_el = sm[:, 680:688].rearrange("p (t n) -> p t n", t=TOK)
        r_pr = sm[:, 688:720].rearrange("p (t g e) -> p t g e", t=TOK, g=EGROUPS)
        r_w = sm[:, 720:728].rearrange("p (t n) -> p t n", t=TOK)
        r_el2 = sm[:, 728:736].rearrange("p (t n) -> p t n", t=TOK)

        block = ctx.enter_context(nc.Block())

        def done(n):
            return n + SLOTS

        @block.sync
        def _(sp):
            def piece(at, s):
                src = A["w_stream"][at] if isinstance(at, int) else A["w_stream"][bass.ds(at, 1), :, :].rearrange("o p n -> p (o n)")
                sp.dma_start(w_raw[:, s * PIECE:(s + 1) * PIECE, :].rearrange("p u n -> p (u n)"), src).then_inc(raw_landed[s], 16)

            n_ring = RAW // PIECE
            sp.dma_start(ccol, A["c_col"]).then_inc(c_loaded, 16)
            for s in range(n_ring):
                piece(s, s)
                if s == 0:
                    sp.wait_ge(mod_cleared_a, 1)
                    sp.dma_start(mod[0:1, 0:2 * D], A["b_ada"][:, 0:2 * D]).then_inc(ada_b_loaded, 16)
            rounds = sorted([(ada_round(i), "ada", i) for i in range(N_ADA)]
                            + [(ring_round(r), "unit", r) for r in range(ADA_BEFORE[-1] + 1)])
            for (_, kind, k), (at, _, _) in zip(rounds, rounds[1:]):
                for s in range(n_ring):
                    used = k * RAW + PIECE * (s + 1)
                    sp.wait_ge(ada_used if kind == "ada" else lo_ready, used)
                    piece(at * n_ring + s, s)
                    if at == 1 and s == 1:
                        sp.dma_start(x_sb[:, :, :], A["x"].rearrange("b (t p) d -> p (b t) d", p=P)).then_inc(x_loaded, 16)
                        sp.dma_start(W[:, 0:D], A["norm1_g"].partition_broadcast(P)).then_inc(norm1_loaded, 16)
                if at == 1:
                    sp.dma_start(ident[:, :], A["identity"]).then_inc(ident_loaded, 16)
                if at == 2:
                    sp.dma_start(arena[:, 18432:20480], A["const1"]).then_inc(cst_loaded, 16)
                    sp.dma_start(inv_row, A["inv_freq"].partition_broadcast(P)).then_inc(pos_loaded, 16)
                    sp.dma_start(pos_i[:, :], A["pos_col"]).then_inc(pos_loaded, 16)
            with sp.Fori(ADA_BEFORE[-1] + 1, UNITS // RAW) as i:
                for s in range(n_ring):
                    sp.wait_ge(lo_ready, i * RAW + PIECE * (s + 1) - RAW)
                    piece(i * n_ring + (N_ADA * n_ring + s), s)
            for t in range(TOK):
                sp.wait_ge(x_ready, LAYERS * TOK + t + 1)
                sp.dma_start(A["out"][0, t * P:(t + 1) * P, :], x_sb[:, t, :]).then_inc(out_stored, 16)
            sp.wait_ge(out_stored, 16 * TOK)

        @block.gpsimd
        def _(pool):
            pool.memset(mod[:, 2 * D:], 0.0).then_inc(mod_cleared_b, 1)
            def lo(n, k):
                pool.wait_ge(hi_ready, n + (k + 1))
                pool.tensor_tensor(w_lo[:, k % SLOTS, :], w_raw[:, k % RAW, :],
                                   w_hi[:, k % SLOTS, :].bitcast(F32), ALU.subtract).then_inc(lo_ready, 1)

            def lo_round(n):
                for s in range(RAW):
                    lo(n, s)

            with pool.Fori(0, U_LAYERS // RAW) as i:
                lo_round(i * RAW)
            ahead = L_OUT + SLOTS
            with pool.Fori(0, LAYERS) as l:
                n = l * L_UNITS + U_LAYERS
                with pool.Fori(0, ahead // RAW) as i:
                    lo_round(i * RAW + n)
                for k in range(ahead // RAW * RAW, ahead):
                    lo(n, k)
                for j in range(2 * SH):
                    pool.wait_ge(sexp_ready, l * 8 + (j + 1))
                    pool.tensor_tensor(sw[:, j % 4, :, :], sw[:, j % 4, :, :], cbs[j // 4].rearrange("p (t n) -> p t n", t=TOK), ALU.mult)\
                        .then_inc(sw_ready, 1)
                for k in range(ahead, (ahead // RAW + 1) * RAW):
                    lo(n, k)
                with pool.Fori(ahead // RAW + 1, L_UNITS // RAW) as i:
                    lo_round(i * RAW + n)
        @block.scalar
        def _(act):
            def hi(n, k):
                if isinstance(n, int):
                    landed = (ring_round((n + k) // RAW) + 1) * 16
                else:
                    landed = n * (16 // RAW) + (k // RAW + N_ADA + 1) * 16
                act.wait_ge(raw_landed[k % RAW // PIECE], landed)
                act.wait_ge(unit_used, n + k + 1)
                act.activation(w_hi[:, k % SLOTS, :], w_raw[:, k % RAW, :], ACT.Copy).then_inc(hi_ready, 1)

            def his(a, b, n=0):
                for k in range(a, b):
                    hi(n, k)

            def turn_hi(n, dst, c0, nch, free=None):
                for t in range(TOK):
                    act.wait_ge(t_ready, n + t + 1)
                    if free is not None and t == 0:
                        act.wait_ge(unit_used, free)
                    act.activation(dst[:, c0:c0 + nch, t * P:(t + 1) * P],
                                   T[:, t, 0:nch * P].rearrange("p (c n) -> p c n", n=P), ACT.Copy).then_inc(t_hi, 1)

            def down_his(n, k, t, pairs, after=None):
                for q in range(pairs + 1):
                    if q < pairs:
                        turn_hi(t + 2 * q, yT_hi, 2 * (q % 2), 2, done(n + (k + 2 * q - 2)) if q >= 2 else None)
                    if after:
                        after(q)
                    if q >= 1:
                        his(k + 2 * (q - 1) + SLOTS, k + 2 * q + SLOTS, n)

            def root(n, ap):
                act.wait_ge(var_ready, n + 1)
                act.activation(ap, ap, ACT.Sqrt).then_inc(std_ready, 1)

            def turn_hi_x(n, t):
                for b in range(2):
                    act.wait_ge(t_ready, n + b + 1)
                    act.activation(xT_hi[:, 4 * b:4 * b + 4, t * P:(t + 1) * P],
                                   T[:, b, :].rearrange("p (c n) -> p c n", n=P), ACT.Copy).then_inc(t_hi, 1)

            def activate(kind, n_done):
                act.wait_ge(unit_used, n_done)
                if kind == "mlp":
                    act.activation(tile(0), G[:, :, :], ACT.Relu).then_inc(act_out, 1)
                else:
                    act.activation(ffn_a, G[:, :, 0:DE], ACT.Silu).then_inc(act_out, 1)

            def ffn_step(kind, e, last, n, k, t, ndown):
                turn_hi(t, yT_hi, 0, ndown)
                if e == last:
                    return
                ahead = ndown + UP if e < last - 1 else 2 * ndown
                for j in range(ahead):
                    if j == UP:
                        activate(kind, done(n + k))
                    hi(n, k + j)
                if ahead <= UP:
                    activate(kind, done(n + k))

            def mod_rows(i):
                act.wait_ge(mod_sum, i + 1)
                v = ADA_ORDER[i]
                act.activation(mod[:, v * D:(v + 1) * D].rearrange("p (b n) -> p b n", b=2), G[:, :, :], ACT.Copy).then_inc(mod_out, 1)

            act.dma_start(onehot, A["onehot"]).then_inc(bias_in_loaded, 16)
            act.dma_start(tab[0:BUCKETS, :], A["rel_bias"]).then_inc(bias_in_loaded, 16)
            act.wait_ge(mod_cleared_b, 1)
            act.dma_start(mod[0:1, 2 * D:], A["b_ada"][:, 2 * D:]).then_inc(ada_b2_loaded, 16)
            act.wait_ge(c_loaded, 16)
            act.activation(csil, ccol, ACT.Silu).then_inc(c_ready, 1)
            for h in range(N_AH):
                act.wait_ge(bias_row, h + 1)
                act.activation(bias_vec[:, h, :], row_banks[h % len(row_banks)], ACT.Copy).then_inc(bias_rows_out, 1)
                if h == N_AH // 2 - 1:
                    mod_rows(0)
                if h == N_AH // 2 + 1:
                    act.wait_ge(x_loaded, 16)
                    for t in range(TOK):
                        i = act.activation(h_sb[:, t, :], x_sb[:, t, :], ACT.Square, accum_out=sm[:, 16 + t:17 + t])
                    i.then_inc(sumsq_ready, 1)
                if h == N_AH - 2:
                    root(0, sm[:, 16:18])
            his(U_RET_IN, U_RET_IN + SLOTS)
            mod_rows(1)
            act.wait_ge(bias_rows_out, N_AH)
            act.dma_start(A["rel_scratch"][:, 0:P, :].rearrange("h p n -> p h n"), bias_vec).then_inc(bias_stored, 16)
            for t in range(TOK):
                turn_hi_x(T_H1 + 2 * t, t)
            act.wait_ge(h_ready, TOK)
            act.dma_start(mod[:, 0:2048], A["gn_g"].partition_broadcast(P)).then_inc(gn_g_loaded, 16)
            act.dma_start(W, A["gn_b"].partition_broadcast(P)).then_inc(gn_b_loaded, 16)
            for j in range(N_RET_IN + 1):
                his(U_RET_IN + UP * (j + 1), U_RET_IN + UP * (j + 2))
                if 1 <= j <= 4:
                    for tk in range(TOK):
                        act.wait_ge(rqk_ready, 2 * (j - 1) + tk + 1)
                        act.activation(qkT[:, 4 * (j - 1):4 * j, tk * P:(tk + 1) * P],
                                       T[:, tk, :].rearrange("p (c n) -> p c n", n=P), ACT.Copy).then_inc(rqk_out, 1)
                if 6 <= j < 6 + RH:
                    h = j - 6
                    act.wait_ge(ro_ready, h + 1)
                    act.activation(tile(h), AC[:, 2:4, :], ACT.Copy).then_inc(ro_out, 1)
                    root(R_GN + h, sm[:, 32 + 2 * h:34 + 2 * h])
                if 8 <= j < N_RET_IN:
                    act.wait_ge(unit_used, done(U_RET_IN + UP * (j + 1)))
                    act.activation(tile(j), (G, AC)[j % 2][:, 0:2, :], ACT.Silu).then_inc(rg_gated, 1)
            act.wait_ge(y_ready, RH)
            act.wait_ge(bias_stored, 16)

            def mod_and_bias(q):
                if 2 * RH - (N_ADA - 2) <= q < 2 * RH:
                    mod_rows(q - 2 * RH + N_ADA)
                load_bias(q)

            def load_bias(q):
                g = q // 2
                if q % 2 or g >= len(GROUPS):
                    return
                flat = A["rel_scratch"].rearrange("h p n -> h (p n)")[g * AH:(g + 1) * AH, :]
                for t, (c0, n) in enumerate(((0, P), (P, S))):
                    a = S - 1 - t * P
                    src = flat[:, a:a + P * (2 * S - 1)].rearrange("h (p n) -> p h n", n=2 * S - 1)[:, :, 0:n]
                    act.dma_start(rel[g][:, :, c0:c0 + n], src).then_inc(rel_loaded[g], 16)

            down_his(0, U_RET_OUT, T_RET, 2 * RH, mod_and_bias)
            his(U_ATT_IN + SLOTS, POS0 - UP + SLOTS)
            n_turned = 0
            for p in range(-UP, N_POS):
                if p < N_POS - 1:
                    his(POS0 + p + SLOTS, POS0 + p + SLOTS + 1)
                if turn_at(p):
                    g, n = turn_at(p)
                    tk, qk = n // 2, n % 2
                    act.wait_ge(aqk_ready, n_turned + 1)
                    act.activation(aqkT[g % 2][:, 4 * qk:4 * qk + 4, tk * P:(tk + 1) * P],
                                   T[:, n % 2, :].rearrange("p (c n) -> p c n", n=P), ACT.Copy).then_inc(aqk_out, 1)
                    n_turned += 1
                k = head_at(p, 1)
                if k is not None:
                    act.wait_ge(as_out, k + 1)
                    if k >= 2:
                        act.wait_ge(aeT_ready, k - 1)
                    act.activation(a_e[:, k % 2, 0:P], scr[:, k % 2, 0:P], ACT.Exp, bias=anm[:, 2 * k:2 * k + 1],
                                   accum_out=aden[:, 2 * k:2 * k + 1])
                    act.activation(a_e[:, k % 2, P:384], scr[:, k % 2, P:384], ACT.Exp, bias=anm[:, 2 * k + 1:2 * k + 2],
                                   accum_out=aden[:, 2 * k + 1:2 * k + 2]).then_inc(ae_ready, 1)
                k = head_at(p, 5)
                if k is not None:
                    g, h = k // AH, k % AH
                    act.wait_ge(ao_ready, k + 1)
                    act.activation(tile(3 * g)[:, :, h * ADH:(h + 1) * ADH],
                                   AC[:, 3, 0:256].rearrange("p (t n) -> p t n", t=TOK), ACT.Copy).then_inc(ao_out, 1)
                    if k == N_AH - 1:
                        act.wait_ge(lse_diff, 1)
                        act.activation(afac, adiff, ACT.Exp).then_inc(lse_exp, 1)
                j = (p - (U_GATE - POS0)) // UP
                if j >= 0 and p % UP == UP - 1:
                    act.wait_ge(unit_used, done(U_GATE + UP * (j + 1)))
                    act.activation(tile((1, 2, 4, 5)[j]), (G, AC)[j % 2][:, 0:2, :], ACT.Sigmoid).then_inc(gate_read, 1)
            his(U_ATT_OUT - 1 + SLOTS, U_ATT_OUT + SLOTS)
            act.wait_ge(ao_ready, N_AH)
            act.dma_start(norm2_row, A["norm2_g"].partition_broadcast(P)).then_inc(norm2_loaded, 16)
            down_his(0, U_ATT_OUT, T_ATT, 2)
            down_his(0, U_WO, T_MERGE, 4)
            act.dma_start(arena[:, 17024:18432], A["const2"]).then_inc(cst2_loaded, 16)
            act.dma_start(sel, A["row_select"]).then_inc(cst2_loaded, 16)
            for t in range(TOK):
                root(R_NORM2 + t, var[t])
                turn_hi_x(T_H2 + 2 * t, t)
            act.wait_ge(h_ready, 2 * TOK)
            act.dma_start(row2["ln2_g"], A["norm_f_g"].partition_broadcast(P)).then_inc(normf_loaded, 16)
            his(U_MLP + 4, U_MLP + 7)
            activate("mlp", done(U_MLP + UP))
            his(U_MLP + 7, U_MLP + 8)
            act.wait_ge(ang_ready, 1)
            act.activation(sinM, sm[:, 64:96].rearrange("p (t n) -> p t n", t=TOK), ACT.Sin)
            act.activation(cosM, sm[:, 96:128].rearrange("p (t n) -> p t n", t=TOK), ACT.Sin).then_inc(trig_ready, 1)
            act.wait_ge(cst2_loaded, 32)
            with act.Fori(0, FF_TILES - 2) as e:
                ffn_step("mlp", 0, FF_TILES - 1, e * 8 + U_MLP, 8, e * 2 + T_MLP, 4)
            for e in (FF_TILES - 2, FF_TILES - 1):
                ffn_step("mlp", e, FF_TILES - 1, U_MLP, 8 + 8 * e, T_MLP + 2 * e, 4)
            root(R_FINAL, var[0])
            with act.Fori(0, LAYERS) as l:
                n = l * L_UNITS + U_LAYERS
                t = l * LT + T_LAYERS
                r = l * LR + R_LAYERS
                his(0, SLOTS - 1, n)
                turn_hi_x(t + LT_X, 0)
                his(SLOTS - 1, SLOTS, n)
                root(r, var[1])
                turn_hi_x(t + (LT_X + 2), 1)
                act.wait_ge(x_ready, l * TOK + TOK)
                act.dma_start(mod[:, 0:ROWS2], A["rows2"][bass.ds(l, 1), :].rearrange("o n -> (o n)").partition_broadcast(P))\
                   .then_inc(rows_loaded, 16)
                act.dma_start(cvw, A["conv_col"][bass.ds(l, 1), :, :].rearrange("o p n -> p (o n)")).then_inc(rows_loaded, 16)
                his(SLOTS, 2 * SLOTS, n)
                act.wait_ge(g_free, l * LM + (G_CREDIT + M_LAYERS + 1))
                for tk in range(TOK):
                    act.activation(HB[:, tk, 0:256], P2[:, tk, 0:256], ACT.Square, accum_out=sm[:, 200 + tk:201 + tk])
                    i = act.activation(HB[:, tk, 256:384], P2[:, tk, 256:384], ACT.Square, accum_out=sm[:, 202 + tk:203 + tk])
                i.then_inc(mla_sumsq, 1)
                root(r + 1, sm[:, 200:204])
                act.wait_ge(sp_in, l + 1)
                act.wait_ge(rows_loaded, l * 32 + 32)
                act.activation(sp_e, sp_e, ACT.Exp)
                act.activation(ea, row2["a_log"], ACT.Exp).then_inc(sp_exp, 1)
                his(L_UKV, L_REST, n)
                turn_hi(t + LT_MLA, yT_hi, 0, 3)
                his(L_REST, L_REST + 2, n)
                for tk in range(TOK):
                    act.wait_ge(unit_used, done(n + L_UQ))
                    kv = (G if tk == 0 else T)[:, :, :].rearrange("p c (h d) -> p (c h) d", d=NOPE + MV)
                    act.activation(KF[:, tk, :].rearrange("p (h d) -> p h d", d=QD)[:, :, 0:NOPE], kv[:, :, 0:NOPE], ACT.Copy)
                    act.activation(V2[:, tk, :].rearrange("p (h d) -> p h d", d=MV), kv[:, :, NOPE:], ACT.Copy).then_inc(kv_out, 1)

                his(L_REST + 2, L_REST + SLOTS, n)

                def turned(m):
                    qk, tk, hg = m // 4, m // 2 % 2, m % 2
                    act.wait_ge(mqkT_ready, l * 8 + m + 1)
                    act.activation((mqT, mkT)[qk][0:QD, 4 * hg:4 * hg + 4, tk * P:(tk + 1) * P],
                                   T[0:QD, m % 2, :].rearrange("p (c n) -> p c n", n=P), ACT.Copy).then_inc(mqkT_out, 1)

                def to_xpad(m):
                    act.wait_ge(sx_T, l * 3 + m + 1)
                    if m < 2:
                        dst, src = xpad[:, 0:4, 2 + m * P:2 + (m + 1) * P], T[:, m, :].rearrange("p (c n) -> p c n", n=P)
                    else:
                        dst, src = xpad[:, 4:6, 2:2 + S], T[:, 0, :].rearrange("p (c n) -> p c n", n=S)
                    act.activation(dst, src, ACT.Copy).then_inc(sx_out, 1)

                for p in range(N_POS2 + 1):
                    if p >= 1 and p != N_POS2 - 1:
                        ahead = L_REST + SLOTS + min(p - 1, N_POS2 - 2)
                        his(ahead, ahead + 1, n)
                    if p in (1, 2):
                        turned(2 * p - 2)
                        turned(2 * p - 1)
                    if p == 3:
                        for m in range(4, 8):
                            turned(m)
                    if p == 4:
                        to_xpad(0)
                        to_xpad(1)
                        act.activation(yT_lo[:, :, :].rearrange("p c n -> p (c n)"), masks, ACT.Copy)
                        act.activation(sel_r, sel, ACT.Copy)
                        act.activation(ident_r, ident[:, :], ACT.Copy)
                    if p == 5:
                        to_xpad(2)
                        act.wait_ge(rows_T, l + 1)
                        act.activation(rowT, T[0:32, 1, 0:S], ACT.Copy).then_inc(rows_out, 1)
                    h = p - 5
                    if 0 <= h < MH:
                        act.wait_ge(mmax_ready, l * MH + h + 1)
                        if h >= 2:
                            act.wait_ge(meT_ready, l * MH + h - 1)
                        for tk in range(TOK):
                            i = act.activation(me[:, h % 2, tk, :], AC[:, 2, tk * S:(tk + 1) * S], ACT.Exp, scale=QD ** -0.5,
                                               bias=mnm[:, 2 * h + tk:2 * h + tk + 1], accum_out=mden[:, 2 * h + tk:2 * h + tk + 1])
                        i.then_inc(me_ready, 1)
                    if p == 9:
                        for tk in range(TOK):
                            act.wait_ge(lqk_T, l * TOK + tk + 1)
                            for c in range(4):
                                i = act.activation(lqkT[c][:, tk * P:(tk + 1) * P], AC[:, tk, c * P:(c + 1) * P], ACT.Copy)
                            i.then_inc(lqk_out, 1)
                act.wait_ge(conv_done, l + 1)
                for c in range(XBC_CH):
                    act.activation(xc[:, c, :], xc[:, c, :], ACT.Silu, bias=cv_b[:, c:c + 1])
                act.activation(P2[:, :, IN2["z"]:IN2["z"] + 256], P2[:, :, IN2["z"]:IN2["z"] + 256], ACT.Silu).then_inc(conv_act, 1)
                def lstm_weights(h):
                    for j in (2 * h, 2 * h + 1):
                        c = j % 2 * LH + h
                        act.wait_ge(lmax_ready, l * 8 + j + 1)
                        if h >= 2 and j % 2 == 0:
                            act.wait_ge(lpT_ready, l * LH + h - 1)
                        for tk in range(TOK):
                            i = act.activation(lw[:, j % 4, tk, :], AC[:, j % 2, tk * S:(tk + 1) * S], ACT.Exp,
                                               bias=lnm[:, tk * 8 + c:tk * 8 + c + 1])
                        i.then_inc(lexp_ready, 1)
                    act.wait_ge(lfl_in, l * LH + h + 1)
                    fl = lfloor[:, 4 * h:4 * h + 4]
                    act.activation(fl, fl, ACT.Exp, scale=-1.0).then_inc(lfl_out, 1)

                lstm_weights(0)
                act.wait_ge(sxt_T, l + 1)
                act.activation(XT, T[:, 0, :].rearrange("p (t n) -> p t n", t=TOK), ACT.Copy).then_inc(sxt_out, 1)
                for g in range(SG):
                    act.wait_ge(scb_ready, l * SG + g + 1)
                    act.activation(cbs[g], T[:, 1 - g, :], ACT.Copy).then_inc(scb_out, 1)

                his(L_OUT + SLOTS - 1, L_OUT + SLOTS, n)

                def lstm_turned(h):
                    act.wait_ge(lpT_ready, l * LH + h + 1)
                    if h >= 2:
                        act.wait_ge(lnum_ready, l * LH + h - 1)
                    act.activation(lpT[:, h % 2, :], T[:, 0, :], ACT.Copy).then_inc(lpT_out, 1)

                for h in range(LH):
                    if h >= 1:
                        lstm_weights(h)
                    for j in (2 * h, 2 * h + 1):
                        c = j % 2 * SH + h
                        act.wait_ge(srow_ready, l * 8 + j + 1)
                        if h >= 2 and j % 2 == 0:
                            act.wait_ge(sy_ready, l * SH + h - 1)
                        for st in range(TOK):
                            i = act.activation(sw[:, j % 4, st, :], (AC[:, 2, :], T[:, 1, :])[j % 2][:, st * S:(st + 1) * S], ACT.Exp,
                                               bias=ncs[:, st * 8 + c:st * 8 + c + 1])
                        i.then_inc(sexp_ready, 1)
                    if h >= 1:
                        lstm_turned(h - 1)
                lstm_turned(LH - 1)
                def gate_and_roots(q):
                    if q == 0:
                        act.wait_ge(g_free, l * LM + (G_CREDIT + M_LAYERS + N_IN2))
                        act.activation(P2[:, :, IN2["mo"]:IN2["mo"] + 256], P2[:, :, IN2["mo"]:IN2["mo"] + 256], ACT.Sigmoid).then_inc(lgate, 1)
                    if q == 1:
                        root(r + 2, sm[:, 64:72])
                        root(r + 3, sm[:, 72:76])
                    if q == 4:
                        root(r + 4, var[0])

                down_his(n, L_OUT, t + LT_OUT, 4, gate_and_roots)
                for tk in range(TOK):
                    if tk:
                        root(r + 4 + tk, var[tk])
                    turn_hi_x(t + (LT_X2 + 2 * tk), tk)
                his(L_MOE + 3, L_MOE + 6, n)
                act.wait_ge(gexp_in, l + 1)
                act.activation(rt_e, rt_e, ACT.Exp).then_inc(gexp_out, 1)
                activate("moe", done(n + L_MOE + UP))
                his(L_MOE + 6, L_MOE + 8, n)
                with act.Fori(0, 3) as e4:
                    for q in range(4):
                        ffn_step("moe", 0, EXPERTS - 1, e4 * 24 + n, L_MOE + 8 + 6 * q, t + LT_MOE + e4 * 8 + 2 * q, 2)
                for e in range(12, EXPERTS):
                    ffn_step("moe", e, EXPERTS - 1, n, L_MOE + 8 + 6 * e, t + LT_MOE + 2 * e, 2)
                root(r + 6, var[0])
            root(R_LAYERS + LAYERS * LR, var[1])
        @block.tensor
        def _(pe):
            def mm3(out, xh, xl, wh, wl, start, stop):
                pe.matmul(out, xh, wh, start=start, stop=False)
                pe.matmul(out, xh, wl, start=False, stop=False)
                return pe.matmul(out, xl, wh, start=False, stop=stop)

            def up_unit(n, k, u, banks):
                pe.wait_ge(lo_ready, n + (k + u + 1))
                s = (k + u) % SLOTS
                for t in range(TOK):
                    for j in range(2):
                        c, w = 2 * u + j, slice(j * NT, (j + 1) * NT)
                        i = mm3(banks[:, t, :], xT_hi[:, c, t * P:(t + 1) * P], xT_lo[:, c, t * P:(t + 1) * P],
                                w_hi[:, s, w], w_lo[:, s, w], c == 0, c == KC - 1)
                i.then_inc(unit_used, 1)

            def up(n, k, banks):
                for u in range(UP):
                    up_unit(n, k, u, banks)

            def up_tile(n, k, u, t, banks, amid=None):
                if t == 0:
                    pe.wait_ge(lo_ready, n + (k + u + 1))
                s = (k + u) % SLOTS
                for j in range(2):
                    if j == 1 and amid:
                        amid()
                    c, w = 2 * u + j, slice(j * NT, (j + 1) * NT)
                    i = mm3(banks[:, t, :], xT_hi[:, c, t * P:(t + 1) * P], xT_lo[:, c, t * P:(t + 1) * P],
                            w_hi[:, s, w], w_lo[:, s, w], c == 0, c == KC - 1)
                if t == TOK - 1:
                    i.then_inc(unit_used, 1)

            def turn_x(n, t, src):
                for b in range(2):
                    if not (isinstance(n, int) and n + b < 2):
                        pe.wait_ge(t_lo, n + b - 1)
                    for c in range(4):
                        i = pe.transpose(T[:, b, c * P:(c + 1) * P], src[:, t, b * NT + c * P:b * NT + (c + 1) * P], ident[:, :])
                    i.then_inc(t_ready, 1)

            def up_normed(n, k, banks, tn, src, ready, at):
                pe.wait_ge(ready, at + 1)
                turn_x(tn, 0, src)
                pe.wait_ge(t_lo, tn + 2)
                for u in range(UP):
                    if u == UP - 1:
                        pe.wait_ge(ready, at + 2)
                        turn_x(tn + 2, 1, src)
                    up_tile(n, k, u, 0, banks)
                pe.wait_ge(t_lo, tn + 4)
                for u in range(UP):
                    up_tile(n, k, u, 1, banks)

            def down(n, k, nch, first, last, c0=0):
                def step(c, t):
                    s = (k + c) % SLOTS
                    for j in range(2):
                        w = slice(j * NT, (j + 1) * NT)
                        i = mm3(AC[:, 2 * t + j, :], yT_hi[:, c0 + c, t * P:(t + 1) * P], yT_lo[:, c0 + c, t * P:(t + 1) * P],
                                w_hi[:, s, w], w_lo[:, s, w], first and c == 0, last and c == nch - 1)
                    if t == TOK - 1:
                        i.then_inc(unit_used, 1)
                    elif last and c == nch - 1:
                        i.then_inc(acc_ready, 1)

                tiles = range(TOK)
                for t, c in [(t, c) for t in tiles for c in range(nch)] if last else [(t, c) for c in range(nch) for t in tiles]:
                    if t == 0:
                        pe.wait_ge(lo_ready, n + (k + c + 1))
                    step(c, t)

            def turn(n, src, nch):
                for t in range(TOK):
                    if not (isinstance(n, int) and n < TOK):
                        pe.wait_ge(t_lo, n + t - 1)
                    for c in range(nch):
                        i = pe.transpose(T[:, t, c * P:(c + 1) * P], src[:, t, c * P:(c + 1) * P], ident[:, :])
                    i.then_inc(t_ready, 1)

            def down_pairs(n, k, t, src, pairs, before=None):
                for q in range(pairs + 1):
                    if q < pairs:
                        if before:
                            before(q)
                        turn(t + 2 * q, src(q), 2)
                    if q >= 1:
                        pe.wait_ge(t_lo, t + 2 * q)
                        down(n, k + 2 * (q - 1), 2, q == 1, q == pairs, 2 * ((q - 1) % 2))

            def clear_acc():
                for b in range(4):
                    pe.matmul(AC[:, b, :], zero_r[0:1, :], xT_hi[0:1, 0:2, :].rearrange("p c n -> p (c n)"),
                              start=True, stop=False)

            def ffn_step(e, last, n, k, t, h, h_src, ndown):
                pe.wait_ge(ffn_h, h + 1)
                turn(t, h_src, ndown)
                if e < last:
                    up(n, k, G)
                pe.wait_ge(t_lo, t + TOK)
                down(n, k + UP if e < last else k, ndown, False, e == last)

            pe.wait_ge(tab_wide, 1)
            pe.wait_ge(bias_in_loaded, 32)
            def bias_row_of(h):
                if h >= len(row_banks):
                    pe.wait_ge(bias_rows_out, h - len(row_banks) + 1)
                pe.matmul(row_banks[h % len(row_banks)], tab_bc[:, h, :], onehot[:, h // AH, :], start=True, stop=True).then_inc(bias_row, 1)
            def mod_sums(i):
                v = ADA_ORDER[i]
                pe.wait_ge(ada_summed, i + 1)
                if i:
                    pe.wait_ge(mod_out, i)
                for b in range(2):
                    k = pe.matmul(G[:, b, :], ones_col.to_broadcast([P, P]), mod[:, v * D + b * NT:v * D + (b + 1) * NT], start=True, stop=True)
                k.then_inc(mod_sum, 1)

            for h in range(N_AH // 2):
                bias_row_of(h)
            mod_sums(0)
            for h in range(N_AH // 2, N_AH):
                bias_row_of(h)
            mod_sums(1)
            def ret_turn(j):
                for tk in range(TOK):
                    n = 2 * j + tk
                    pe.wait_ge(rope_done, j + 1)
                    if n >= 2:
                        pe.wait_ge(rqk_out, n - 1)
                    for c in range(4):
                        i = pe.transpose(T[:, tk, c * P:(c + 1) * P], tile(j)[:, tk, c * P:(c + 1) * P], ident[:, :])
                    i.then_inc(rqk_ready, 1)

            def ret_scores(h):
                if h >= 2:
                    pe.wait_ge(rs_out, h - 1)
                b = h % 2
                for c in range(2):
                    pe.matmul(T[:, b, 0:S], qkT[:, 8 + 2 * h + c, 0:P], qkT[:, 2 * h + c, :], start=c == 0, stop=c == 1)
                for c in range(2):
                    i = pe.matmul(T[:, b, S:S + P], qkT[:, 8 + 2 * h + c, P:S], qkT[:, 2 * h + c, P:S], start=c == 0, stop=c == 1)
                i.then_inc(rs_ready, 1)

            def ret_out(h):
                b, v = h % 2, tile(4 + h)
                pe.wait_ge(rs_out, h + 1)
                if h >= 1:
                    pe.wait_ge(ro_out, h)
                pe.matmul(AC[:, 2, :], scr[:, b, 0:P], v[:, 0, :], start=True, stop=True)
                pe.matmul(AC[:, 3, :], scr[:, b, P:S], v[:, 0, :], start=True, stop=False)
                pe.matmul(AC[:, 3, :], scr[:, b, S:S + P], v[:, 1, :], start=False, stop=True).then_inc(ro_ready, 1)

            pe.wait_ge(ident_loaded, 16)
            pe.wait_ge(bias_rows_out, N_AH)
            for j in range(N_RET_IN):
                if j == 0:
                    up_normed(0, U_RET_IN, G, T_H1, h_sb, h_ready, 0)
                else:
                    if j < 10:
                        pe.wait_ge(g_free, G_CREDIT + j - 1)
                    else:
                        pe.wait_ge(rg_gated, j - 9)
                    up(0, U_RET_IN + j * UP, (G, AC)[j % 2])
                if 1 <= j <= 4:
                    ret_turn(j - 1)
                if j == 5:
                    pe.wait_ge(rqk_out, 8)
                    ret_scores(0)
                    ret_scores(1)
                if 6 <= j < 6 + RH:
                    ret_out(j - 6)
                    if j < 4 + RH:
                        ret_scores(j - 4)
            pe.wait_ge(rg_gated, 3)
            up(0, U_ATT_FIRST, G)
            pe.wait_ge(rg_gated, RH)

            def ret_head(q):
                pe.wait_ge(y_ready, q // 2 + 1)
                if q >= 2 * RH - (N_ADA - 2):
                    pe.wait_ge(g_free, G_CREDIT + M_ATT_IN + 1)
                    mod_sums(q - 2 * RH + N_ADA)

            down_pairs(0, U_RET_OUT, T_RET, lambda q: tile(8 + q // 2)[:, :, q % 2 * 256:(q % 2 + 1) * 256], 2 * RH, ret_head)
            pe.wait_ge(mod_out, N_ADA)
            up(0, U_ATT_IN, G)
            pe.wait_ge(acc_free, 1)

            def att_qk_turn(g, n, n_turned, n_eT):
                tk, qk = n // 2, n % 2
                pe.wait_ge(g_free, G_CREDIT + M_ATT_IN + 3 * g + 2)
                if n_turned >= 2:
                    pe.wait_ge(aqk_out, n_turned - 1)
                if n_eT:
                    pe.wait_ge(aeT_out, n_eT)
                for c in range(AH):
                    i = pe.transpose(T[:, n % 2, c * P:(c + 1) * P], tile(3 * g + qk)[:, tk, c * P:(c + 1) * P], ident[:, :])
                i.then_inc(aqk_ready, 1)

            def att_scores(k, n_turned):
                h, qk = k % AH, aqkT[k // AH % 2]
                pe.wait_ge(aqk_out, n_turned)
                if k >= 1:
                    pe.wait_ge(as_out, k)
                pe.matmul(AC[:, 2, 0:P], qk[:, h, 0:P], qk[:, AH + h, 0:P], start=True, stop=True)
                pe.matmul(AC[:, 2, P:384], qk[:, h, P:S], qk[:, AH + h, :], start=True, stop=True).then_inc(as_ready, 1)

            def att_turn(k, n_turned):
                b = k % 2
                pe.wait_ge(ae_ready, k + 1)
                pe.wait_ge(aqk_out, n_turned)
                if k >= 2:
                    pe.wait_ge(aeT_out, k - 1)
                for c in range(3):
                    i = pe.transpose(T[:, b, c * P:(c + 1) * P], a_e[:, b, c * P:(c + 1) * P], ident[:, :])
                i.then_inc(aeT_ready, 1)

            def att_values(k):
                b, v = k % 2, tile(3 * (k // AH) + 2)[:, :, k % AH * ADH:(k % AH + 1) * ADH]
                pe.wait_ge(g_free, G_CREDIT + M_ATT_IN + 3 * (k // AH) + 3)
                pe.wait_ge(aeT_out, k + 1)
                if k >= 1:
                    pe.wait_ge(ao_out, k)
                pe.matmul(AC[:, 3, 0:P], a_eT[b][:, 0:P], v[:, 0, :], start=True, stop=True)
                pe.matmul(AC[:, 3, P:S], a_eT[b][:, P:S], v[:, 0, :], start=True, stop=False)
                pe.matmul(AC[:, 3, P:S], a_eT[b][:, S:384], v[:, 1, :], start=False, stop=True).then_inc(ao_ready, 1)

            n_turned, n_eT = 0, 0
            for p in range(-UP, N_POS):
                j = p // UP + 3
                if p % UP == 0 and p >= 0:
                    if j < N_ATT_IN + 2:
                        pe.wait_ge(g_free, G_CREDIT + M_ATT_IN + j - 1)
                    else:
                        pe.wait_ge(gate_read, j - N_ATT_IN - 1)
                up_unit(0, POS0 + p // UP * UP, p % UP, (AC, G)[j % 2])
                if head_at(p, 3) is not None:
                    att_turn(head_at(p, 3), n_turned)
                    n_eT += 1
                if turn_at(p):
                    att_qk_turn(*turn_at(p), n_turned, n_eT)
                    n_turned += 1
                if head_at(p, 0) is not None:
                    att_scores(head_at(p, 0), n_turned)
                if head_at(p, 4) is not None:
                    att_values(head_at(p, 4))
            pe.wait_ge(att_ready, 1)
            pe.wait_ge(ao_out, N_AH)
            down_pairs(0, U_ATT_OUT, T_ATT, lambda q: tile(0)[:, :, q * 256:(q + 1) * 256], 2,
                       lambda q: pe.wait_ge(gate_read, N_GATE - 1 + q))
            pe.wait_ge(acc_free, 2)
            down_pairs(0, U_WO, T_MERGE, lambda q: tile(10 + q // 2)[:, :, q % 2 * 256:(q % 2 + 1) * 256], 4,
                       lambda q: pe.wait_ge(merged_ready, q // 2 + 1))
            up_normed(0, U_MLP, G, T_H2, h_sb, h_ready, 2)
            pe.wait_ge(zero_ready, 1)
            clear_acc()
            with pe.Fori(0, FF_TILES - 2) as e:
                ffn_step(0, FF_TILES - 1, e * 8 + U_MLP, UP, e * 2 + T_MLP, e, tile(1), 4)
            for e in (FF_TILES - 2, FF_TILES - 1):
                ffn_step(e, FF_TILES - 1, U_MLP, UP + 8 * e, T_MLP + 2 * e, e, tile(1), 4)

            pe.wait_ge(cst2_loaded, 32)
            with pe.Fori(0, LAYERS) as l:
                n = l * L_UNITS + U_LAYERS
                tb = l * LT + T_LAYERS
                m = l * LM + (M_LAYERS + G_CREDIT)
                up_normed(n, L_IN, G, tb + LT_X, x_sb, x_ready, l * TOK)
                for u in range(UP):
                    if u == UP - 1:
                        pe.wait_ge(cq_ready, l + 1)
                        turn(tb + LT_MLA, P2, 3)
                    up_unit(n, L_IN + UP, u, AC)
                pe.wait_ge(t_lo, tb + (LT_MLA + TOK))
                pe.wait_ge(g_free, m + 1)
                pe.wait_ge(lo_ready, n + (L_UKV + 1))
                s = L_UKV % SLOTS
                for t in range(TOK):
                    for b in range(2):
                        w = slice(b * NT, (b + 1) * NT)
                        i = mm3((G, T)[t][:, b, :], yT_hi[:, 2, t * P:(t + 1) * P], yT_lo[:, 2, t * P:(t + 1) * P],
                                w_hi[:, s, w], w_lo[:, s, w], True, True)
                i.then_inc(unit_used, 1)
                pe.wait_ge(g_free, m + 2)
                for c in range(2):
                    pe.wait_ge(lo_ready, n + (L_UQ + c + 1))
                    s = (L_UQ + c) % SLOTS
                    for t in range(TOK):
                        for b, (w0, w1) in enumerate(((0, NT), (NT, MH * QD))):
                            i = mm3(AC[:, 2 * t + b, 0:w1 - w0], yT_hi[:, c, t * P:(t + 1) * P], yT_lo[:, c, t * P:(t + 1) * P],
                                    w_hi[:, s, w0:w1], w_lo[:, s, w0:w1], c == 0, c == 1)
                    i.then_inc(unit_used, 1)

                def running_sums():
                    pe.wait_ge(cum_in, l + 1)
                    cum = AC[:, 3, 0:64].rearrange("p (k n) -> p k n", n=16)
                    pe.matmul(cum[:, 0, :], tri_f, cu[:, 0, :], start=True, stop=True)
                    pe.matmul(cum[:, 1, :], ones, cu[:, 0, :], start=True, stop=False)
                    pe.matmul(cum[:, 1, :], tri_f, cu[:, 1, :], start=False, stop=True)
                    pe.matmul(cum[:, 2, :], tri_b, cu[:, 0, :], start=True, stop=False)
                    pe.matmul(cum[:, 2, :], ones, cu[:, 1, :], start=False, stop=True)
                    pe.matmul(cum[:, 3, :], tri_b, cu[:, 1, :], start=True, stop=True).then_inc(cum_ready, 1)

                def mla_qk_turn(k):
                    qk, tk, hg = k // 4, k // 2 % 2, k % 2
                    pe.wait_ge((q_ready, kv_ready)[qk], l + 1)
                    if k >= 2:
                        pe.wait_ge(mqkT_out, l * 8 + (k - 1))
                    else:
                        pe.wait_ge(kv_out, l * TOK + TOK)
                    for c in range(4):
                        h = 4 * hg + c
                        i = pe.transpose(T[0:QD, k % 2, c * P:(c + 1) * P], (Q, KF)[qk][:, tk, h * QD:(h + 1) * QD], ident[:, :])
                    i.then_inc(mqkT_ready, 1)

                def conv_turn(k):
                    if k == 0:
                        pe.wait_ge(mqkT_out, l * 8 + 8)
                        pe.wait_ge(g_free, m + 3)
                    if k == 2:
                        pe.wait_ge(sx_out, l * 3 + 1)
                    for c in range(4):
                        t, ch = (k, c) if k < 2 else (c % 2, 4 + c // 2)
                        a = IN2["xbc"] + ch * P
                        i = pe.transpose(T[:, k % 2, c * P:(c + 1) * P], P2[:, t, a:a + P], ident[:, :])
                    i.then_inc(sx_T, 1)

                def mla_scores(h):
                    if h >= 1:
                        pe.wait_ge(me_ready, l * MH + h)
                    for t in range(TOK):
                        i = pe.matmul(AC[:, 2, t * S:(t + 1) * S], mqT[0:QD, h, t * P:(t + 1) * P], mkT[0:QD, h, :], start=True, stop=True)
                    i.then_inc(ms_ready, 1)

                def mla_turn(h):
                    pe.wait_ge(me_ready, l * MH + (h + 1))
                    if h >= 2:
                        pe.wait_ge(meT_out, l * MH + (h - 1))
                    for kt in range(TOK):
                        for t in range(TOK):
                            c = kt * TOK + t
                            i = pe.transpose(T[:, h % 2, c * P:(c + 1) * P], me[:, h % 2, t, kt * P:(kt + 1) * P], ident[:, :])
                    i.then_inc(meT_ready, 1)

                def mla_values(h):
                    pe.wait_ge(meT_out, l * MH + (h + 1))
                    if h >= 1:
                        pe.wait_ge(mo_out, l * MH + h)
                    for t in range(TOK):
                        for kt in range(TOK):
                            c = kt * TOK + t
                            i = pe.matmul(AC[:, 3, t * MV:(t + 1) * MV], meT[:, h % 2, c * P:(c + 1) * P],
                                          V2[:, kt, h * MV:(h + 1) * MV], start=kt == 0, stop=kt == TOK - 1)
                    i.then_inc(mo_ready, 1)

                def mlstm_rows(h):
                    for j in (2 * h, 2 * h + 1):
                        if j >= 2:
                            pe.wait_ge(lexp_ready, l * 8 + (j - 1))
                        row(AC[:, j % 2, :], j % 2 * LH + h, (mask_f, mask_b)[j % 2]).then_inc(lrow_ready, 1)

                def row(out, c, mask):
                    pe.matmul(out, sel_r[:, c:c + 1].to_broadcast([32, P]), rowT.unsqueeze(1).to_broadcast([32, TOK, S]), start=True, stop=False)
                    return pe.matmul(out, ident_r, mask, start=False, stop=True)

                def ssd_inputs():
                    pe.wait_ge(conv_act, l + 1)
                    pe.wait_ge(meT_out, l * MH + MH)
                    for t in range(TOK):
                        for c in range(2):
                            a = (t * 2 + c) * P
                            i = pe.transpose(T[:, 0, a:a + P], xc[:, c, t * P:(t + 1) * P], ident[:, :])
                    i.then_inc(sxt_T, 1)
                    for g in range(SG):
                        if g == 1:
                            pe.wait_ge(sxt_out, l + 1)
                        for st in range(TOK):
                            i = pe.matmul(T[:, 1 - g, st * S:(st + 1) * S], xc[:, 2 + g, st * P:(st + 1) * P], xc[:, 4 + g, :],
                                          start=True, stop=True)
                        i.then_inc(scb_ready, 1)

                for p in range(N_POS2 + 3):
                    if p == 0:
                        pe.wait_ge(kv_out, l * TOK + TOK)
                    if p == 2 * UP:
                        pe.wait_ge(g_free, m + 3)
                    if p < N_POS2 - 2:
                        up_unit(n, L_REST + p // UP * UP, p % UP, (G, AC, G)[p // UP])
                    elif p < N_POS2 + 2:
                        half = p - (N_POS2 - 2)
                        up_tile(n, L_REST + N_POS2 - UP, UP - 2 + half // TOK, half % TOK, G)
                    if p == 0:
                        pe.wait_ge(q_out, l + 1)
                        running_sums()
                    if p in (1, 2):
                        mla_qk_turn(2 * p - 2)
                        mla_qk_turn(2 * p - 1)
                    if p == 3:
                        for k in range(4, 8):
                            mla_qk_turn(k)
                    if p == 4:
                        conv_turn(0)
                        conv_turn(1)
                    if p == 5:
                        conv_turn(2)
                        pe.wait_ge(sx_out, l * 3 + 2)
                        pe.wait_ge(rows_w, l + 1)
                        for t in range(TOK):
                            i = pe.transpose(T[0:32, 1, t * P:(t + 1) * P], rw[:, t, :], ident[:, :])
                        i.then_inc(rows_T, 1)
                    if 4 <= p < 4 + MH:
                        mla_scores(p - 4)
                    if 6 <= p < 6 + MH:
                        if p == 6:
                            pe.wait_ge(sx_out, l * 3 + 3)
                            pe.wait_ge(rows_out, l + 1)
                        mla_turn(p - 6)
                    if p == N_POS2 + 2:
                        ssd_inputs()
                    if 7 <= p < 7 + MH:
                        mla_values(p - 7)
                    if p == N_POS2 - 1:
                        pe.wait_ge(lqk_out, l * TOK + TOK)
                        mlstm_rows(0)
                    if p == 8:
                        pe.wait_ge(g_free, m + 4)
                        for t in range(TOK):
                            for c in range(4):
                                a = IN2["mq"] + c * P
                                i = pe.transpose(AC[:, t, c * P:(c + 1) * P], P2[:, t, a:a + P], ident[:, :])
                            i.then_inc(lqk_T, 1)

                def lstm_turn(h):
                    pe.wait_ge(lp_ready, l * LH + (h + 1))
                    if h >= 1:
                        pe.wait_ge(lpT_out, l * LH + h)
                    for st in range(TOK):
                        for t in range(TOK):
                            c = st * TOK + t
                            i = pe.transpose(T[:, 0, c * P:(c + 1) * P], lw[:, 2 * h % 4, t, st * P:(st + 1) * P], ident[:, :])
                    i.then_inc(lpT_ready, 1)

                def lstm_values(h):
                    pe.wait_ge(lpT_out, l * LH + (h + 1))
                    a = IN2["mv"] + h * LDH
                    for t in range(TOK):
                        for st in range(TOK):
                            c = st * TOK + t
                            i = pe.matmul(G[:, 0, t * S + h * LDH:t * S + (h + 1) * LDH], lpT[:, h % 2, c * P:(c + 1) * P],
                                          P2[:, st, a:a + LDH], start=st == 0, stop=st == TOK - 1)
                    i.then_inc(lnum_ready, 1)

                def ssd_values(h):
                    pe.wait_ge(sw_ready, l * 8 + (2 * h + 2))
                    for t, pairs in enumerate((((0, 0), (1, 0), (1, 1)), ((0, 0), (0, 1), (1, 1)))):
                        for k, (d, st) in enumerate(pairs):
                            i = pe.matmul(G[:, 1, t * S + h * SP_:t * S + (h + 1) * SP_], sw[:, (2 * h + d) % 4, st, t * P:(t + 1) * P],
                                          xdt[:, st, d, h * SP_:(h + 1) * SP_], start=k == 0, stop=k == 2)
                    i.then_inc(sy_ready, 1)

                def lstm_products(h):
                    if h >= 1:
                        pe.wait_ge(lmul_ready, l * LH + h)
                    else:
                        pe.wait_ge(mo_out, l * MH + MH)
                    a = h % 2 * LDH
                    for t in range(TOK):
                        i = pe.matmul(AC[:, 3, t * S:(t + 1) * S], lqkT[h // 2][a:a + LDH, t * P:(t + 1) * P],
                                      lqkT[2 + h // 2][a:a + LDH, :], start=True, stop=True)
                    i.then_inc(lqk_ready, 1)

                pe.wait_ge(g_free, m + N_IN2)
                for h in range(LH + 1):
                    if h < LH:
                        if h == 0:
                            pe.wait_ge(me_ready, l * MH + MH)
                        for j in (2 * h, 2 * h + 1):
                            if j >= 2:
                                pe.wait_ge(sexp_ready, l * 8 + (j - 1))
                            elif j == 1:
                                pe.wait_ge(scb_out, l * SG + 1)
                            row((AC[:, 2, :], T[:, 1, :])[j % 2], 8 + j % 2 * SH + h, (mask_b, mask_f)[j % 2]).then_inc(srow_ready, 1)
                        if h == 0:
                            lstm_products(0)
                        if h + 1 < LH:
                            mlstm_rows(h + 1)
                    if h >= 1:
                        if h == 1:
                            pe.wait_ge(scb_out, l * SG + SG)
                        ssd_values(h - 1)
                        lstm_turn(h - 1)
                    if h + 1 < LH:
                        lstm_products(h + 1)
                    if h >= 1:
                        lstm_values(h - 1)
                pe.wait_ge(lpT_out, l * LH + LH)

                def heads_wait(q):
                    if q >= 2:
                        pe.wait_ge((lstm_ready, heads_ready)[q - 2], l + 1)

                down_pairs(n, L_OUT, tb + LT_OUT, lambda q: HB[:, :, q * 256:(q + 1) * 256], 4, heads_wait)
                nr = EGROUPS + EXPERTS

                def router():
                    pe.wait_ge(lo_ready, n + (L_ROUTER + 1))
                    s = L_ROUTER % SLOTS
                    for c in range(KC):
                        w = slice(c * nr, (c + 1) * nr)
                        i = mm3(AC[0:nr, 0, 0:S], w_hi[:, s, w], w_lo[:, s, w], xT_hi[:, c, :], xT_lo[:, c, :], c == 0, c == KC - 1)
                    i.then_inc(unit_used, 1)

                for t in range(TOK):
                    pe.wait_ge(x2_ready, l * TOK + (t + 1))
                    turn_x(tb + (LT_X2 + 2 * t), t, x_sb)
                    pe.wait_ge(t_lo, tb + (LT_X2 + 2 * t + 2))
                    if t == TOK - 1:
                        router()
                    for u in range(UP - 1):
                        turn_logits = t == TOK - 1 and u == 0
                        up_tile(n, L_MOE, u, t, G, (lambda: pe.wait_ge(logits_out, l + 1)) if turn_logits else None)
                        if turn_logits:
                            for k in range(TOK):
                                i = pe.transpose(AC[:, 1, k * 32:k * 32 + nr], logitsT[:, k * P:(k + 1) * P], ident[0:nr, 0:nr])
                            i.then_inc(logits_ready, 1)
                for t in range(TOK):
                    up_tile(n, L_MOE, UP - 1, t, G)
                pe.wait_ge(g_free, m + LM)
                clear_acc()
                with pe.Fori(0, 3) as e4:
                    for q in range(4):
                        ffn_step(0, EXPERTS - 1, e4 * 24 + n, L_MOE + UP + 6 * q, e4 * 8 + (tb + (LT_MOE + 2 * q)),
                                 l * EXPERTS + e4 * 4 + (FF_TILES + q), moe_h, 2)
                for e in range(12, EXPERTS):
                    ffn_step(e, EXPERTS - 1, n, L_MOE + UP + 6 * e, tb + (LT_MOE + 2 * e), l * EXPERTS + (FF_TILES + e), moe_h, 2)
        @block.vector
        def _(dve):
            dep = dve.drain

            def lo(n, dst_hi, dst_lo, c0, nch):
                for t in range(TOK):
                    dve.wait_ge(t_hi, n + t + 1)
                    s = slice(t * P, (t + 1) * P)
                    dve.tensor_tensor(dst_lo[:, c0:c0 + nch, s], T[:, t, 0:nch * P].rearrange("p (c n) -> p c n", n=P),
                                      dst_hi[:, c0:c0 + nch, s].bitcast(F32), ALU.subtract).then_inc(t_lo, 1)

            def lo_x(n, t):
                for b in range(2):
                    dve.wait_ge(t_hi, n + b + 1)
                    chunks, s = slice(4 * b, 4 * b + 4), slice(t * P, (t + 1) * P)
                    dve.tensor_tensor(xT_lo[:, chunks, s], T[:, b, :].rearrange("p (c n) -> p c n", n=P),
                                      xT_hi[:, chunks, s].bitcast(F32), ALU.subtract).then_inc(t_lo, 1)

            def down_los(n, q0, q1):
                for q in range(q0, q1):
                    lo(n + 2 * q, yT_hi, yT_lo, 2 * (q % 2), 2)

            def rstd(n, ap, scale, eps, meanwhile=None):
                dep()
                dve.tensor_scalar(ap, ap, scale, eps, ALU.mult, ALU.add).then_inc(var_ready, 1)
                if meanwhile:
                    meanwhile()
                dve.wait_ge(std_ready, n + 1)
                dve.reciprocal(ap, ap)
                dep()

            def stats(t):
                dep()
                for c in range(2):
                    dve.bn_stats(bst[:, 2 * t + c, :], x_sb[:, t, c * NT:(c + 1) * NT])
                dep()
                dve.bn_aggr(mv[:, t, :], bst[:, 2 * t:2 * t + 2, :])
                dep()

            def rms_stats(t):
                stats(t)
                dve.scalar_tensor_tensor(var[t], mv[:, t, 0:1], mv[:, t, 0:1], mv[:, t, 1:2], ALU.mult, ALU.add)
                dep()
                dve.tensor_scalar(var[t], var[t], 1.0, 1e-6, ALU.mult, ALU.add).then_inc(var_ready, 1)
                dve.memset(mv[:, t, 0:1], 0.0)
                dep()

            def inverse_root(n, t):
                dve.wait_ge(std_ready, n + 1)
                dve.reciprocal(var[t], var[t])
                dep()

            def wide(row, t=TOK):
                return row.unsqueeze(1).to_broadcast([P, t, row.shape[1]])

            def read_tile(dst, banks, n_done):
                dve.wait_ge(unit_used, n_done)
                dve.tensor_copy(dst, banks[:, 0:2, :]).then_inc(g_free, 1)

            def norm_scale(sc, A1, g_loaded):
                dve.wait_ge(g_loaded, 16)
                dve.scalar_tensor_tensor(A1, mod[:, sc * D:(sc + 1) * D], 1.0, A1, ALU.add, ALU.mult)
                dep()

            def scaled(t, A1):
                dve.scalar_tensor_tensor(h_sb[:, t, :], x_sb[:, t, :], var[t], A1, ALU.mult, ALU.mult)

            def shifted(t, sh):
                dve.tensor_tensor(h_sb[:, t, :], h_sb[:, t, :], mod[:, sh * D:(sh + 1) * D], ALU.add).then_inc(h_ready, 1)

            def ada(i, s0, s1):
                v = ADA_ORDER[i]
                m = mod[:, v * D:(v + 1) * D]
                for s in range(s0, s1):
                    dve.wait_ge(raw_landed[s // PIECE], 16 * (ada_round(i) + 1))
                    dve.scalar_tensor_tensor(m, w_raw[:, s, :], csil[:, s:s + 1], m, ALU.mult, ALU.add).then_inc(ada_used, 1)
                    dep()
                if s1 == KC:
                    dve.memset(sm[:, 892:893], 0.0).then_inc(ada_summed, 1)

            dve.memset(mod[:, 0:2 * D], 0.0).then_inc(mod_cleared_a, 1)
            dve.memset(sm[:, 892:893], 0.0).then_inc(unit_used, SLOTS)
            dve.memset(sm[:, 893:894], 0.0).then_inc(g_free, G_CREDIT)
            dve.memset(zero_r[:, :].bitcast(F32), 0.0).then_inc(zero_ready, 1)
            dve.memset(ones_col, 1.0)
            for k in range(4):
                dve.memset(wt4[:, k:k + 1], 4.0 - k)
            dve.memset(tab[BUCKETS:BUCKETS + 1, :], NEG)
            dep()
            dve.wait_ge(bias_in_loaded, 32)
            dve.tensor_copy(tab_bc, tab.unsqueeze(2).to_broadcast([BUCKETS + 1, N_AH, P])).then_inc(tab_wide, 1)
            dve.wait_ge(c_ready, 1)
            dve.wait_ge(ada_b_loaded, 16)
            ada(0, 0, KC)
            ada(1, 0, 4)
            dve.wait_ge(mod_out, 1)
            norm_scale(1, W[:, 0:D], norm1_loaded)
            ada(1, 4, 6)
            dve.wait_ge(sumsq_ready, 1)
            rstd(0, sm[:, 16:18], 1.0 / D, 1e-6, lambda: ada(1, 6, KC))
            for t in range(TOK):
                scaled(t, W[:, 0:D])
            dep()
            dve.wait_ge(mod_out, 2)
            for t in range(TOK):
                shifted(t, 0)
            for t in range(TOK):
                lo_x(T_H1 + 2 * t, t)
            dve.wait_ge(bias_stored, 16)
            dve.wait_ge(cst_loaded, 16)

            def rotate(j):
                x = tile(j).rearrange("p t (h x n) -> p t h x n", h=2, x=2)
                x1, x2 = x[:, :, :, 0, :], x[:, :, :, 1, :]
                t1, t2 = [tile(8)[:, a, :].rearrange("p (t h n) -> p t h n", t=TOK, h=2) for a in range(2)]
                c, s = [r.unsqueeze(2).to_broadcast([P, TOK, 2, P]) for r in (cosR, sinR)]
                dep()
                dve.tensor_tensor(t1, x1, s, ALU.mult)
                dve.tensor_tensor(t2, x2, s, ALU.mult)
                dep()
                dve.tensor_tensor(x1, x1, c, ALU.mult)
                dve.tensor_tensor(x2, x2, c, ALU.mult)
                dep()
                dve.tensor_tensor(x1, x1, t2, ALU.subtract)
                dve.tensor_tensor(x2, x2, t1, ALU.add).then_inc(rope_done, 1)
                dep()

            def ret_in_tile(j):
                read_tile(tile(j), (G, AC)[j % 2], done(U_RET_IN + (j + 1) * UP))

            def decayed(h):
                dve.wait_ge(rs_ready, h + 1)
                if h >= 2:
                    dve.wait_ge(ro_ready, h - 1)
                dve.tensor_tensor(scr[:, h % 2, :], T[:, h % 2, 0:384], decay[:, h, :], ALU.mult).then_inc(rs_out, 1)

            def group_norm(h):
                o, cols = tile(h), slice(h * RDV, (h + 1) * RDV)
                ks = range(2 * h, 2 * h + TOK)
                dve.wait_ge(ro_out, h + 1)
                for k in ks:
                    dve.bn_stats(bst[:, k, :], o[:, k % 2, :])
                dep()
                for k in ks:
                    dve.bn_aggr(mv[:, k, :], bst[:, k, :])
                dep()
                sd = sm[:, 32 + 2 * h:34 + 2 * h]
                dve.tensor_copy(sd, mv[:, 2 * h:2 * h + 2, 1])
                rstd(R_GN + h, sd, 1.0, 1e-5)
                for k in ks:
                    dve.tensor_scalar(o[:, k % 2, :], o[:, k % 2, :], mv[:, k, 0:1], sd[:, k % 2:k % 2 + 1], ALU.subtract, ALU.mult)
                dve.wait_ge(gn_g_loaded, 16)
                dve.wait_ge(gn_b_loaded, 16)
                dep()
                dve.tensor_tensor(o, o, wide(mod[:, cols]), ALU.mult)
                dep()
                dve.tensor_tensor(o, o, wide(W[:, cols]), ALU.add)
                dep()

            def gated(h):
                dve.wait_ge(rg_gated, h + 1)
                dve.tensor_tensor(tile(8 + h), tile(8 + h), tile(h), ALU.mult).then_inc(y_ready, 1)

            dve.wait_ge(ada_b2_loaded, 16)
            for j in range(4):
                ret_in_tile(j)
                rotate(j)
                if j in (1, 2):
                    ada(2, 4 * j - 4, 4 * j)
            ret_in_tile(4)
            ret_in_tile(5)
            decayed(0)
            decayed(1)
            ret_in_tile(6)
            ada(3, 0, 4)
            group_norm(0)
            decayed(2)
            ret_in_tile(7)
            ada(3, 4, KC)
            group_norm(1)
            decayed(3)
            ada(4, 0, 4)
            group_norm(2)
            gated(0)
            ada(4, 4, KC)
            group_norm(3)
            gated(1)
            gated(2)
            gated(3)
            read_tile(tile(0), G, done(U_ATT_FIRST + UP))
            for q in range(2 * RH):
                down_los(T_RET, q, q + 1)
                if 2 <= q < 6:
                    ada(5, 2 * (q - 2), 2 * (q - 1))
            acc_ct = AC[:, :, :].rearrange("p (t c) n -> p t c n", t=TOK)
            dve.wait_ge(unit_used, done(U_RET_OUT + 4 * RH))
            dve.tensor_copy(tile(10), acc_ct[:, :, 0, :])
            dve.tensor_copy(tile(11), acc_ct[:, :, 1, :]).then_inc(acc_free, 1)
            read_tile(tile(1), G, done(U_ATT_IN + UP))
            for p in range(-UP, N_POS):
                k = head_at(p, 3)
                if k is not None:
                    dve.wait_ge(aeT_ready, k + 1)
                    if k >= 2:
                        dve.wait_ge(ao_ready, k - 1)
                    dve.tensor_copy(a_eT[k % 2], T[:, k % 2, 0:384]).then_inc(aeT_out, 1)
                k = head_at(p, 0)
                if k is not None:
                    g, h = k // AH, k % AH
                    s = scr[:, k % 2, :]
                    if h == 0:
                        dve.wait_ge(rel_loaded[g], 32)
                    dve.wait_ge(as_ready, k + 1)
                    if k >= 2:
                        dve.wait_ge(ae_ready, k - 1)
                    dve.scalar_tensor_tensor(s, AC[:, 2, 0:384], ADH ** -0.5, rel[g][:, h, :], ALU.mult, ALU.add)
                    dep()
                    dve.tensor_reduce(amx[:, 2 * k:2 * k + 1], s[:, 0:P], AX.X, ALU.max)
                    dve.tensor_reduce(amx[:, 2 * k + 1:2 * k + 2], s[:, P:384], AX.X, ALU.max)
                    dep()
                    dve.tensor_scalar(anm[:, 2 * k:2 * k + 2], amx[:, 2 * k:2 * k + 2], -1.0, None, ALU.mult).then_inc(as_out, 1)
                if p % UP == UP - 1 and p < U_GATE - POS0:
                    j = p // UP + 3
                    read_tile(tile(j), (AC, G)[j % 2], done(POS0 + p + 1))
            dve.tensor_tensor(aM, amx[:, 0:8], amx[:, 8:16], ALU.max)
            dep()
            dve.tensor_tensor(aM, aM, amx[:, 16:24], ALU.max)
            dep()
            dve.tensor_tensor(adiff.rearrange("p (g n) -> p g n", g=3), amx.rearrange("p (g n) -> p g n", g=3),
                              aM.unsqueeze(1).to_broadcast([P, 3, 8]), ALU.subtract).then_inc(lse_diff, 1)
            dve.wait_ge(lse_exp, 1)
            dve.tensor_tensor(aden, aden, afac, ALU.mult)
            dep()
            dve.tensor_reduce(aD, aden.rearrange("p (g n) -> p n g", g=3), AX.X, ALU.add)
            dep()
            dve.reciprocal(aD, aD)
            dep()
            dve.tensor_tensor(afac.rearrange("p (g n) -> p g n", g=3), afac.rearrange("p (g n) -> p g n", g=3),
                              aD.unsqueeze(1).to_broadcast([P, 3, 8]), ALU.mult)
            dep()
            dve.wait_ge(ao_out, N_AH)
            for g in range(3):
                for h in range(AH):
                    for t in range(TOK):
                        k = (g * AH + h) * 2 + t
                        o, a = tile(3 * g)[:, t, h * ADH:(h + 1) * ADH], tile(0)[:, t, h * ADH:(h + 1) * ADH]
                        if g == 0:
                            dve.tensor_scalar(o, o, afac[:, k:k + 1], None, ALU.mult)
                        else:
                            i = dve.scalar_tensor_tensor(a, o, afac[:, k:k + 1], a, ALU.mult, ALU.add)
                if g < 2:
                    dep()
            i.then_inc(att_ready, 1)
            down_los(T_ATT, 0, 2)
            def acc_wait(n, n_done, t):
                if t == 0:
                    dve.wait_ge(acc_ready, n)
                else:
                    dve.wait_ge(unit_used, n_done)

            dve.wait_ge(gate_read, N_GATE)
            for n in range(2):
                dve.tensor_tensor(tile(10 + n), tile(10 + n), tile(1 + n), ALU.mult)
            for t in range(TOK):
                acc_wait(ACC_ATT, done(U_WO), t)
                for n in range(2):
                    i = dve.tensor_tensor(tile(4 + n)[:, t, :], tile(4 + n)[:, t, :], acc_ct[:, t, n, :], ALU.mult)
                if t == TOK - 1:
                    i.then_inc(acc_free, 1)
                dep()
                for n in range(2):
                    i = dve.tensor_tensor(tile(10 + n)[:, t, :], tile(10 + n)[:, t, :], tile(4 + n)[:, t, :], ALU.add)
                    if t == TOK - 1:
                        i.then_inc(merged_ready, 1)
            down_los(T_MERGE, 0, 4)
            def gated_residual(g, t):
                tmp = arena[:, 10240:11264]
                dve.tensor_tensor(tmp, AC_tok[:, t, :], mod[:, g * D:(g + 1) * D], ALU.mult)
                dep()
                dve.tensor_tensor(x_sb[:, t, :], x_sb[:, t, :], tmp, ALU.add)

            dve.wait_ge(mod_out, N_ADA)
            norm_scale(4, norm2_row, norm2_loaded)
            for t in range(TOK):
                acc_wait(ACC_WO, done(U_MLP), t)
                gated_residual(2, t)
                if t == 1:
                    lo_x(T_H2, 0)
                rms_stats(t)
                inverse_root(R_NORM2 + t, t)
                scaled(t, norm2_row)
                dep()
                shifted(t, 3)
            lo_x(T_H2 + 2, 1)
            dve.wait_ge(pos_loaded, 32)
            pos, ang, turns = sm[:, 18:20], sm[:, 128:160], sm[:, 160:192]
            dve.tensor_copy(pos, pos_i[:, :])
            dep()
            for t in range(TOK):
                dve.tensor_scalar(ang[:, t * 16:(t + 1) * 16], inv_row, pos[:, t:t + 1], None, ALU.mult)
            dep()
            big = 1.5 * 2.0 ** 23
            c2 = float(np.float32(2 * np.pi - 6.28125))
            c3 = 2 * np.pi - 6.28125 - c2
            for quarter, dst in ((0.0, sm[:, 64:96]), (0.25, sm[:, 96:128])):
                dve.tensor_scalar(turns, ang, 1 / (2 * np.pi), quarter, ALU.mult, ALU.add)
                dep()
                dve.tensor_scalar(turns, turns, big, None, ALU.add)
                dep()
                dve.tensor_scalar(turns, turns, big, None, ALU.subtract)
                dep()
                dve.scalar_tensor_tensor(dst, turns, -6.28125, ang, ALU.mult, ALU.add)
                dep()
                dve.scalar_tensor_tensor(dst, turns, -c2, dst, ALU.mult, ALU.add)
                dep()
                dve.scalar_tensor_tensor(dst, turns, -c3, dst, ALU.mult, ALU.add)
                dep()
                dve.tensor_scalar(dst, dst, quarter * 2 * np.pi, 3.1415925, ALU.add, ALU.min)
                dep()
                i = dve.tensor_scalar(dst, dst, -3.1415925, None, ALU.max)
                if quarter == 0.0:
                    dep()
            i.then_inc(ang_ready, 1)
            def mlp_hidden(e):
                dve.wait_ge(act_out, e + 1)
                dve.tensor_tensor(tile(1), tile(0), tile(0), ALU.mult).then_inc(ffn_h, 1)

            mlp_hidden(0)
            with dve.Fori(0, FF_TILES - 1) as e:
                lo(e * 2 + T_MLP, yT_hi, yT_lo, 0, 4)
                mlp_hidden(e + 1)
            lo(T_MLP + 2 * (FF_TILES - 1), yT_hi, yT_lo, 0, 4)
            def normed(n, t, g, b, out_sem):
                dve.scalar_tensor_tensor(x_sb[:, t, :], x_sb[:, t, :], mv[:, t, 0:1], row2[g], ALU.subtract, ALU.mult)
                inverse_root(n, t)
                dve.scalar_tensor_tensor(x_sb[:, t, :], x_sb[:, t, :], var[t], row2[b], ALU.mult, ALU.add).then_inc(out_sem, 1)

            dve.memset(row2["ln2_b"], 0.0)
            dve.wait_ge(normf_loaded, 16)
            dve.wait_ge(trig_ready, 1)
            for flag, value in ((about_zero, 1.0), (about_mean, 0.0), (norm_eps, 1e-6)):
                dve.memset(flag, value)
            for t in range(TOK):
                acc_wait(ACC_MLP, done(U_LAYERS), t)
                gated_residual(5, t)
                if t == 0:
                    rms_stats(0)
                    normed(R_FINAL, 0, "ln2_g", "ln2_b", x_ready)

            def residual(t):
                dve.scalar_tensor_tensor(x_sb[:, t, :], x_sb[:, t, :], ALPHA, AC_tok[:, t, :], ALU.mult, ALU.add)

            def last_stats():
                t = TOK - 1
                stats(t)
                dve.scalar_tensor_tensor(var[t], mv[:, t, 0:1], about_zero, mv[:, t, 0:1], ALU.mult, ALU.mult)
                dep()
                dve.scalar_tensor_tensor(var[t], var[t], norm_eps, mv[:, t, 1:2], ALU.add, ALU.add).then_inc(var_ready, 1)
                dve.tensor_scalar(mv[:, t, 0:1], mv[:, t, 0:1], about_mean, None, ALU.mult)
                dep()

            def residual_stats(t, meanwhile=None):
                residual(t)
                if meanwhile:
                    meanwhile()
                stats(t)
                dve.tensor_scalar(var[t], mv[:, t, 1:2], 1.0, 1e-5, ALU.mult, ALU.add).then_inc(var_ready, 1)

            def rope(x1, x2, t1, t2, c, s):
                dve.tensor_tensor(t1, x1, s, ALU.mult)
                dve.tensor_tensor(t2, x2, s, ALU.mult)
                dep()
                dve.tensor_tensor(x1, x1, c, ALU.mult)
                dve.tensor_tensor(x2, x2, c, ALU.mult)
                dep()
                dve.tensor_tensor(x1, x1, t2, ALU.subtract)
                return dve.tensor_tensor(x2, x2, t1, ALU.add)

            def first_max(v, m, hot):
                dve.tensor_reduce(m, v, AX.X, ALU.max)
                dep()
                dve.tensor_tensor(hot, v, m.to_broadcast([P, TOK, 4]), ALU.is_ge)
                dep()
                dve.tensor_tensor(hot, hot, wide(wt4), ALU.mult)
                dep()
                dve.tensor_reduce(r_w[:, :, 0:1], hot, AX.X, ALU.max)
                dep()
                dve.tensor_tensor(hot, hot, r_w[:, :, 0:1].to_broadcast([P, TOK, 4]), ALU.is_equal)
                dep()

            with dve.Fori(0, LAYERS) as l:
                n = l * L_UNITS + U_LAYERS
                tb = l * LT + T_LAYERS
                r = l * LR + R_LAYERS
                lo_x(tb + LT_X, 0)
                last_stats()
                normed(r, 1, "ln2_g", "ln2_b", x_ready)
                lo_x(tb + (LT_X + 2), 1)
                for flag, value in ((about_zero, 0.0), (about_mean, 1.0), (norm_eps, 1e-5)):
                    dve.memset(flag, value)

                def in_tile(j):
                    k = L_IN + (j + 1) * UP if j < 2 else L_REST + (j - 1) * UP
                    read_tile(P2[:, :, j * NT:(j + 1) * NT], (G, AC, G, AC, G)[j], n + done(k))

                in_tile(0)
                dep()
                dve.wait_ge(rows_loaded, l * 32 + 32)
                dve.tensor_tensor(GT, P2[:, :, IN2["mg"]:IN2["mg"] + 24], wide(row2["gate_bias"]), ALU.add)
                dep()
                dve.tensor_scalar(SI[:, :, 0:4], GT[:, :, 4:8], -1.0, None, ALU.mult)
                dve.tensor_scalar(SI[:, :, 4:8], GT[:, :, 12:16], -1.0, None, ALU.mult)
                dve.tensor_copy(SI[:, :, 8:16], GT[:, :, 16:24])
                dep()
                dve.scalar_tensor_tensor(sp_e, SI, -1.0, SI, ALU.mult, ALU.min).then_inc(sp_in, 1)
                dve.wait_ge(mla_sumsq, l + 1)
                dve.tensor_scalar(sm[:, 200:202], sm[:, 200:202], 1.0 / 256, 1e-6, ALU.mult, ALU.add)
                rstd(r + 1, sm[:, 202:204], 1.0 / 128, 1e-6)
                dve.reciprocal(sm[:, 200:202], sm[:, 200:202])
                dep()
                for t in range(TOK):
                    dve.scalar_tensor_tensor(P2[:, t, 0:256], P2[:, t, 0:256], sm[:, 200 + t:201 + t], row2["q_norm"], ALU.mult, ALU.mult)
                    i = dve.scalar_tensor_tensor(P2[:, t, 256:384], P2[:, t, 256:384], sm[:, 202 + t:203 + t], row2["kv_norm"], ALU.mult, ALU.mult)
                i.then_inc(cq_ready, 1)
                lo(tb + LT_MLA, yT_hi, yT_lo, 0, 3)
                in_tile(1)
                dve.wait_ge(sp_exp, l + 1)
                dve.tensor_scalar(w_sp, sp_e, 2.0, None, ALU.add)
                dep()
                dve.reciprocal(w_sp, w_sp)
                dep()
                dve.tensor_tensor(z_sp, sp_e, w_sp, ALU.mult)
                dep()
                dve.tensor_tensor(w_sp, z_sp, z_sp, ALU.mult)
                dep()
                dve.tensor_scalar(q_sp, w_sp, 1.0 / 17, 1.0 / 15, ALU.mult, ALU.add)
                dep()
                for k in (13, 11, 9, 7, 5, 3, 1):
                    dve.tensor_tensor(q_sp, q_sp, w_sp, ALU.mult)
                    dep()
                    dve.tensor_scalar(q_sp, q_sp, 1.0 / k, None, ALU.add)
                    dep()
                dve.scalar_tensor_tensor(q_sp, q_sp, 2.0, z_sp, ALU.mult, ALU.mult)
                dep()
                dve.scalar_tensor_tensor(SP, SI, 0.0, q_sp, ALU.max, ALU.add)
                dep()
                dve.tensor_scalar(cu[:, :, 0:8], SP[:, :, 0:8], -1.0, None, ALU.mult)
                dve.scalar_tensor_tensor(cu[:, :, 8:16], SP[:, :, 8:16], -1.0, wide(ea), ALU.mult, ALU.mult).then_inc(cum_in, 1)
                dve.wait_ge(unit_used, n + done(L_REST))
                for t in range(TOK):
                    i = dve.tensor_copy(Q[:, t, :], AC_tok[:, t, 0:MH * QD])
                i.then_inc(q_out, 1)
                dep()
                qh = Q.rearrange("p t (h d) -> p t h d", d=QD)
                t1, t2 = [scr[:, b, 0:256].rearrange("p (t h n) -> p t h n", t=TOK, h=MH) for b in range(2)]
                hr = ROPE // 2
                rope(qh[:, :, :, NOPE:NOPE + hr], qh[:, :, :, NOPE + hr:QD], t1, t2,
                     *[v.unsqueeze(2).to_broadcast([P, TOK, MH, hr]) for v in (cosM, sinM)]).then_inc(q_ready, 1)
                dep()
                kr = P2[:, :, IN2["kr"]:IN2["kr"] + ROPE]
                rope(kr[:, :, 0:hr], kr[:, :, hr:ROPE], scr[:, 0, 0:32].rearrange("p (t n) -> p t n", t=TOK),
                     scr[:, 1, 0:32].rearrange("p (t n) -> p t n", t=TOK), cosM, sinM)
                dep()
                dve.wait_ge(kv_out, l * TOK + TOK)
                dve.tensor_copy(KF.rearrange("p t (h d) -> p t h d", d=QD)[:, :, :, NOPE:QD],
                                kr.unsqueeze(2).to_broadcast([P, TOK, MH, ROPE])).then_inc(kv_ready, 1)
                dve.wait_ge(cum_ready, l + 1)
                for d in range(2):
                    dve.tensor_copy(cs.rearrange("p t (k d h) -> p t k d h", k=2, d=2)[:, :, :, d, :],
                                    AC[:, 3, 32 * d:32 * d + 32].rearrange("p (t k d h) -> p t k d h", t=TOK, k=2, d=2)[:, :, :, d, :])
                dep()
                for d in range(2):
                    dve.tensor_tensor(rows16[:, :, 4 * d:4 * d + 4], GT[:, :, 8 * d:8 * d + 4], cs[:, :, 4 * d:4 * d + 4], ALU.subtract)
                dve.tensor_copy(rows16[:, :, 8:16], cs[:, :, 8:16])
                dve.tensor_scalar(ncs.rearrange("p (t c) -> p t c", t=TOK), cs[:, :, 8:16], -1.0, None, ALU.mult)
                dep()
                dve.tensor_copy(rw[:, :, 0:16].bitcast(F32R), rows16)
                dep()
                dve.tensor_tensor(rw[:, :, 16:32], rows16, rw[:, :, 0:16], ALU.subtract).then_inc(rows_w, 1)
                in_tile(2)

                def mla_max(h):
                    dve.wait_ge(ms_ready, l * MH + (h + 1))
                    dve.tensor_reduce(mmax[:, 2 * h:2 * h + 2], AC[:, 2, :].rearrange("p (t n) -> p t n", t=TOK), AX.X, ALU.max)
                    dep()
                    dve.tensor_scalar(mnm[:, 2 * h:2 * h + 2], mmax[:, 2 * h:2 * h + 2], -QD ** -0.5, None, ALU.mult).then_inc(mmax_ready, 1)

                def mla_eT(h):
                    dve.wait_ge(meT_ready, l * MH + (h + 1))
                    if h >= 2:
                        dve.wait_ge(mo_ready, l * MH + (h - 1))
                    dve.tensor_copy(meT[:, h % 2, :], T[:, h % 2, :]).then_inc(meT_out, 1)

                def mla_out(h):
                    dve.reciprocal(mrden[:, 2 * h:2 * h + 2], mden[:, 2 * h:2 * h + 2])
                    dep()
                    dve.wait_ge(mo_ready, l * MH + (h + 1))
                    dve.tensor_tensor(HB[:, :, h * MV:(h + 1) * MV], AC[:, 3, 0:2 * MV].rearrange("p (t n) -> p t n", t=TOK),
                                      mrden[:, 2 * h:2 * h + 2].unsqueeze(2).to_broadcast([P, TOK, MV]), ALU.mult).then_inc(mo_out, 1)

                def conv_tap(k):
                    if k == 0:
                        dve.wait_ge(sx_out, l * 3 + 3)
                    for c in range(XBC_CH):
                        src = xpad[:, c, k:k + S]
                        if k == 0:
                            i = dve.tensor_scalar(xc[:, c, :], src, cv_w[:, c, 0:1], None, ALU.mult)
                        else:
                            i = dve.scalar_tensor_tensor(xc[:, c, :], src, cv_w[:, c, k:k + 1], xc[:, c, :], ALU.mult, ALU.add)
                    return i

                by_c = lMx.rearrange("p (t c) -> p t c", t=TOK)
                nm_c = lnm.rearrange("p (t c) -> p t c", t=TOK)

                def lstm_max(h):
                    for j in (2 * h, 2 * h + 1):
                        c = j % 2 * LH + h
                        dve.wait_ge(lrow_ready, l * 8 + (j + 1))
                        dve.tensor_reduce(by_c[:, :, c:c + 1], AC[:, j % 2, :].rearrange("p (t n) -> p t n", t=TOK), AX.X, ALU.max)
                        dep()
                        dve.tensor_scalar(nm_c[:, :, c:c + 1], by_c[:, :, c:c + 1], -1.0, None, ALU.mult).then_inc(lmax_ready, 1)
                    fl = lfloor[:, 4 * h:4 * h + 4]
                    both = [v.rearrange("p t (d h) -> p t d h", d=2)[:, :, :, h] for v in (by_c, cs[:, :, 0:8])]
                    dve.tensor_tensor(fl.rearrange("p (t d) -> p t d", t=TOK), both[0], both[1], ALU.add).then_inc(lfl_in, 1)

                for p in range(4, N_POS2 + 4):
                    if p == N_POS2:
                        lstm_max(0)
                    if p == 4:
                        dve.wait_ge(mqkT_out, l * 8 + 8)
                        dve.memset(xpad[:, :, 0:2], 0.0)
                        dve.memset(xpad[:, :, S + 2:S + 4], 0.0)
                    if 8 <= p < 8 + MH:
                        mla_out(p - 8)
                    if 4 <= p < 4 + MH:
                        mla_max(p - 4)
                    if 6 <= p < 6 + MH:
                        mla_eT(p - 6)
                    if p in (7, N_POS2 + 1):
                        in_tile(3 if p == 7 else 4)
                    if 6 <= p < 6 + CONV:
                        i = conv_tap(p - 6)
                        if p == 5 + CONV:
                            i.then_inc(conv_done, 1)
                        dep()

                xh = XT.rearrange("p t (h n) -> p t h n", h=SH)
                dve.wait_ge(sxt_out, l + 1)
                for d in range(2):
                    dve.tensor_tensor(xdt[:, :, d, :].rearrange("p t (h n) -> p t h n", h=SH), xh,
                                      SP[:, :, 8 + 4 * d:12 + 4 * d].unsqueeze(3).to_broadcast([P, TOK, SH, SP_]), ALU.mult)

                for h in range(LH):
                    den = lden[:, 4 * h:4 * h + 4]
                    dve.wait_ge(lqk_ready, l * LH + (h + 1))
                    for j in (2 * h, 2 * h + 1):
                        dve.wait_ge(lexp_ready, l * 8 + (j + 1))
                        for t in range(TOK):
                            k = t * 2 + j % 2
                            i = dve.scalar_tensor_tensor(lw[:, j % 4, t, :], AC[:, 3, t * S:(t + 1) * S], LDH ** -0.5, lw[:, j % 4, t, :],
                                                         ALU.mult, ALU.mult, accum_out=den[:, k:k + 1])
                    i.then_inc(lmul_ready, 1)
                    if h + 1 < LH:
                        lstm_max(h + 1)
                    dep()
                    dve.scalar_tensor_tensor(den, den, -1.0, den, ALU.mult, ALU.max)
                    dep()
                    dve.wait_ge(lfl_out, l * LH + (h + 1))
                    dve.tensor_tensor(den, den, lfloor[:, 4 * h:4 * h + 4], ALU.max)
                    dep()
                    dve.reciprocal(den, den)
                    dep()
                    b0, b1 = 2 * h % 4, (2 * h + 1) % 4
                    for t in range(TOK):
                        dve.tensor_scalar(lw[:, b1, t, :], lw[:, b1, t, :], den[:, 2 * t + 1:2 * t + 2], None, ALU.mult)
                    dep()
                    for t in range(TOK):
                        i = dve.scalar_tensor_tensor(lw[:, b0, t, :], lw[:, b0, t, :], den[:, 2 * t:2 * t + 1], lw[:, b1, t, :], ALU.mult, ALU.add)
                    i.then_inc(lp_ready, 1)
                down_los(tb + LT_OUT, 0, 2)
                dve.wait_ge(lnum_ready, l * LH + LH)
                num = G[:, 0, :].rearrange("p (k n) -> p k n", n=LDH)
                cen8, csq8 = [v.rearrange("p (k n) -> p k n", n=LDH) for v in (cen, csq)]
                dve.tensor_reduce(lsum, num, AX.X, ALU.add)
                dep()
                dve.tensor_scalar(lsum, lsum, -1.0 / LDH, None, ALU.mult)
                dep()
                dve.tensor_tensor(cen8, num, lsum.unsqueeze(2).to_broadcast([P, 8, LDH]), ALU.add)
                dep()
                dve.tensor_tensor(csq, cen, cen, ALU.mult)
                dep()
                dve.tensor_reduce(sm[:, 64:72], csq8, AX.X, ALU.add)
                rstd(r + 2, sm[:, 64:72], 1.0 / LDH, 1e-5)
                dve.tensor_tensor(cen8, cen8, sm[:, 64:72].unsqueeze(2).to_broadcast([P, 8, LDH]), ALU.mult)
                dep()
                cen2 = cen.rearrange("p (t n) -> p t n", t=TOK)
                dve.tensor_tensor(cen2, cen2, wide(row2["mlstm_norm"]), ALU.mult)
                dep()
                dve.wait_ge(lgate, l + 1)
                dve.tensor_tensor(HB[:, :, 512:768], cen2, P2[:, :, IN2["mo"]:IN2["mo"] + 256], ALU.mult).then_inc(lstm_ready, 1)
                dve.wait_ge(sy_ready, l * SH + SH)
                ysh = ys.rearrange("p t (h n) -> p t h n", h=SH)
                dve.tensor_tensor(ysh, xh, row2["d_skip"].unsqueeze(1).unsqueeze(3).to_broadcast([P, TOK, SH, SP_]), ALU.mult)
                dep()
                dve.tensor_tensor(ys, ys, G[:, 1, :].rearrange("p (t n) -> p t n", t=TOK), ALU.add)
                dep()
                dve.tensor_tensor(ys, ys, P2[:, :, IN2["z"]:IN2["z"] + 256], ALU.mult)
                dep()
                dve.tensor_tensor(ysq, ys, ys, ALU.mult)
                dep()
                dve.tensor_reduce(sm[:, 72:76], ysq.rearrange("p t (g n) -> p (t g) n", g=SG), AX.X, ALU.add)
                rstd(r + 3, sm[:, 72:76], 1.0 / P, 1e-6)
                ysg = ys.rearrange("p t (g n) -> p (t g) n", g=SG)
                dve.tensor_tensor(ysg, ysg, sm[:, 72:76].unsqueeze(2).to_broadcast([P, 4, P]), ALU.mult)
                dep()
                dve.tensor_tensor(HB[:, :, 768:1024], ys, wide(row2["ssd_norm"]), ALU.mult).then_inc(heads_ready, 1)
                down_los(tb + LT_OUT, 2, 4)
                for t in range(TOK):
                    acc_wait(l * LACC + (ACC_LAYERS + 1), n + done(L_ROUTER), t)
                    residual_stats(t, (lambda: lo_x(tb + LT_X2, 0)) if t == 1 else None)
                    normed(r + 4 + t, t, "ln1_g", "ln1_b", x2_ready)
                lo_x(tb + (LT_X2 + 2), 1)
                dve.wait_ge(unit_used, n + done(L_MOE))
                dve.tensor_copy(logitsT, AC[0:EGROUPS + EXPERTS, 0, 0:S]).then_inc(logits_out, 1)
                dve.wait_ge(logits_ready, l + 1)
                logits = AC[:, 1, 0:TOK * 32].rearrange("p (t n) -> p t n", t=TOK)[:, :, 0:EGROUPS + EXPERTS]
                dve.tensor_tensor(rlog, logits, wide(row2["router_b"]), ALU.add).then_inc(g_free, 1)
                dep()
                first_max(rlog[:, :, 0:4], r_m[:, :, 0:1], r_g)
                dve.tensor_tensor(rt_e[:, :, 0:4], rlog[:, :, 0:4], r_m[:, :, 0:1].to_broadcast([P, TOK, 4]), ALU.subtract)
                dve.tensor_tensor(r_pr, rlog[:, :, 4:20].rearrange("p t (g e) -> p t g e", g=EGROUPS),
                                  r_g.unsqueeze(3).to_broadcast([P, TOK, EGROUPS, EPG]), ALU.mult)
                dep()
                dve.tensor_reduce(r_el, r_pr.rearrange("p t g e -> p t e g"), AX.X, ALU.add)
                dep()
                first_max(r_el, r_m[:, :, 0:1], r_1)
                dve.scalar_tensor_tensor(r_el2, r_1, NEG, r_el, ALU.mult, ALU.add)
                dep()
                first_max(r_el2, r_m[:, :, 1:2], r_2)
                dve.tensor_tensor(rt_e[:, :, 4:5], r_m[:, :, 1:2], r_m[:, :, 0:1], ALU.subtract).then_inc(gexp_in, 1)
                dve.wait_ge(gexp_out, l + 1)
                dve.tensor_reduce(r_w[:, :, 0:1], rt_e[:, :, 0:4], AX.X, ALU.add)
                dve.tensor_scalar(r_w[:, :, 1:2], rt_e[:, :, 4:5], 1.0, None, ALU.add)
                dep()
                dve.tensor_tensor(r_w[:, :, 2:3], r_w[:, :, 0:1], r_w[:, :, 1:2], ALU.mult)
                dep()
                dve.reciprocal(r_w[:, :, 2:3], r_w[:, :, 2:3])
                dve.tensor_tensor(r_2, r_2, rt_e[:, :, 4:5].to_broadcast([P, TOK, 4]), ALU.mult)
                dep()
                dve.tensor_tensor(r_1, r_1, r_2, ALU.add)
                dep()
                dve.tensor_tensor(r_1, r_1, r_w[:, :, 2:3].to_broadcast([P, TOK, 4]), ALU.mult)
                dep()
                dve.tensor_tensor(comb.rearrange("p (t g e) -> p t g e", t=TOK, g=EGROUPS),
                                  r_g.unsqueeze(3).to_broadcast([P, TOK, EGROUPS, EPG]),
                                  r_1.unsqueeze(2).to_broadcast([P, TOK, EGROUPS, EPG]), ALU.mult)
                dep()

                def moe_hidden(e0, e):
                    dve.wait_ge(act_out, l * EXPERTS + e0 + (FF_TILES + e + 1))
                    for t in range(TOK):
                        i = dve.scalar_tensor_tensor(moe_h[:, t, :], ffn_a[:, t, :], comb[:, bass.ds(e0 + (t * EXPERTS + e), 1)],
                                                     G[:, t, DE:2 * DE], ALU.mult, ALU.mult)
                    i.then_inc(ffn_h, 1)

                moe_hidden(0, 0)
                with dve.Fori(0, 3) as e4:
                    for q in range(4):
                        lo(e4 * 8 + (tb + (LT_MOE + 2 * q)), yT_hi, yT_lo, 0, 2)
                        moe_hidden(e4 * 4, q + 1)
                for e in range(12, EXPERTS):
                    lo(tb + (LT_MOE + 2 * e), yT_hi, yT_lo, 0, 2)
                    if e + 1 < EXPERTS:
                        moe_hidden(0, e + 1)
                for t in range(TOK):
                    acc_wait(l * LACC + (ACC_LAYERS + 2), n + done(L_UNITS), t)
                    if t == 0:
                        residual_stats(0)
                        normed(r + 6, 0, "ln2_g", "ln2_b", x_ready)
                    else:
                        residual(t)
            last_stats()
            normed(R_LAYERS + LAYERS * LR, 1, "ln2_g", "ln2_b", x_ready)


def up_units(w):
    n = w.shape[1] // NT
    return w.reshape(UP, 2, P, n, NT).transpose(3, 0, 2, 1, 4).reshape(n * UP, P, UNIT)


def down_units(w):
    return w.reshape(-1, P, UNIT)


def padded(w, cols):
    return np.concatenate([w, np.zeros(w.shape[:-1] + (cols - w.shape[-1],), np.float32)], axis=-1)


def ffn_units(ups, downs):
    parts = [ups[0]]
    for e in range(len(ups)):
        if e + 1 < len(ups):
            parts.append(ups[e + 1])
        parts.append(downs[e])
    return parts


def weight_stream(a):
    w_in = up_units(a["w_in"][0])
    parts = [w_in[:U_RET_OUT], down_units(a["w_ret_out"][0]), w_in[U_RET_OUT:], down_units(a["w_att_out"][0]), down_units(a["w_o"][0])]
    ff1 = up_units(a["w_ff1"][0]).reshape(FF_TILES, UP, P, UNIT)
    ff2 = down_units(a["w_ff2"][0]).reshape(FF_TILES, 4, P, UNIT)
    parts += ffn_units(ff1, ff2)
    for l in range(LAYERS):
        w = a["w_in_2"][l]
        at, sizes = {}, (("cq", 256), ("ckv", 128), ("kr", 32), ("mq", 256), ("mk", 256), ("mv", 256), ("mo", 256),
                         ("mg", 16), ("z", 256), ("xbc", XBC), ("dt", 8))
        c = 0
        for name, n in sizes:
            at[name] = w[:, c:c + n]
            c += n
        first = padded(np.concatenate([at[k] for k in ("cq", "ckv", "kr", "mg", "dt")], axis=1), NT)
        rest = np.concatenate([at[k] for k in ("xbc", "z", "mq", "mk", "mv", "mo")], axis=1)
        tiles = up_units(np.concatenate([first, rest], axis=1))
        parts.append(tiles[:2 * UP])
        parts.append(a["mla_w_ukv_2"][l].reshape(1, P, UNIT))
        parts.append(padded(a["mla_w_uq_2"][l].reshape(2, P, MH * QD), UNIT))
        parts.append(tiles[2 * UP:])
        parts.append(down_units(a["w_out_2"][l]))
        we = a["router_expert_w_2"][l].transpose(1, 0, 2).reshape(D, EXPERTS)
        router = np.concatenate([a["router_group_w_2"][l], we], axis=1)
        parts.append(padded(router.reshape(KC, P, -1).transpose(1, 0, 2).reshape(1, P, -1), UNIT))
        both = np.concatenate([a["expert_w_gate_2"][l], a["expert_w_up_2"][l]], axis=2)
        parts += ffn_units([up_units(w) for w in both], [down_units(w) for w in a["expert_w_down_2"][l]])
    units = np.concatenate(parts, axis=0).reshape(UNITS // RAW, RAW, P, UNIT)
    ada = a["w_ada"][0].reshape(KC, P, N_ADA, D).transpose(2, 0, 1, 3)
    units = np.insert(units, ADA_BEFORE, ada[list(ADA_ORDER)], axis=0)
    return np.ascontiguousarray(units.reshape(-1, PIECE, P, UNIT).transpose(0, 2, 1, 3)).reshape(-1, P, PIECE * UNIT)


def bucket_of(dist):
    exact = BUCKETS // 2
    d = np.maximum(dist, 1).astype(np.float32)
    scale = np.float32(np.log(MAX_DIST / exact))
    large = exact + (np.log(d / np.float32(exact)) / scale * np.float32(BUCKETS - exact)).astype(np.int32)
    return np.where(dist < exact, dist, np.minimum(large, BUCKETS - 1))


def shape_constants():
    f = np.float32
    idx = np.arange(P, dtype=f)
    log_g = np.log1p(-(2.0 ** (-5.0 - np.arange(RH))))
    s, t = np.arange(P)[:, None], np.arange(S)[None, :]
    dec = np.where(t >= s, np.exp(log_g[:, None, None] * np.maximum(t - s, 0)), 0.0) * RDK ** -0.5
    decay = np.concatenate([dec, dec[:, :, 0:P]], axis=2).transpose(1, 0, 2).reshape(P, -1).astype(f)
    half = RDK // 2
    inv = f(10000.0) ** (-np.arange(half, dtype=f) / f(half))
    ang = np.arange(S, dtype=f)[:, None] * inv[None, :]
    by_p = lambda v: v.reshape(TOK, P, half).transpose(1, 0, 2).reshape(P, -1).astype(f)
    const1 = np.concatenate([decay, by_p(np.cos(ang)), by_p(np.sin(ang))], axis=1)
    onehot = np.zeros((BUCKETS + 1, len(GROUPS), NT), f)
    for g, (win, dil) in enumerate(GROUPS):
        for c in range(NT):
            d = S - 1 - c
            ok = 0 <= d <= win and d % dil == 0
            onehot[bucket_of(np.array([d]))[0] if ok else BUCKETS, g, c] = 1.0
    u, v = np.arange(P)[:, None], np.arange(P)[None, :]
    tri_f, tri_b = (u <= v).astype(f), (u >= v).astype(f)
    first, second = np.arange(S)[:, None], np.arange(S)[None, :]
    tiles = lambda m: m.reshape(TOK, P, S).transpose(1, 0, 2).reshape(P, -1)
    mask_f = tiles(np.where(second <= first, 0.0, NEG).astype(f))
    mask_b = tiles(np.where(second >= first, 0.0, NEG).astype(f))
    const2 = np.concatenate([tri_f, tri_b, np.ones((P, P), f), mask_f, mask_b], axis=1)
    select = np.zeros((32, 16), f)
    for c in range(16):
        select[[c, 16 + c], c] = 1.0
    hr = ROPE // 2
    inv_freq = f(10000.0) ** (-np.arange(0, ROPE, 2, dtype=f) / f(ROPE))
    return {"identity": np.eye(P, dtype=f), "const1": const1, "onehot": onehot.reshape(BUCKETS + 1, -1), "const2": const2,
            "row_select": select, "inv_freq": inv_freq.astype(f).reshape(hr)}


def kernel(**inputs):
    import concourse.bacc as bacc
    from concourse.bass_utils import run_bass_kernel_spmd

    a = {k: np.asarray(v) for k, v in inputs.items()}
    arrays = shape_constants()
    arrays["w_stream"] = weight_stream(a)
    arrays["c_col"] = a["c"].reshape(KC, P).T
    arrays["x"] = a["x"]
    arrays["rel_bias"] = a["rel_bias"]
    arrays["b_ada"] = a["b_ada"]
    for name, src in (("norm1_g", "norm1_g"), ("norm2_g", "norm2_g"), ("norm_f_g", "norm_f_g"), ("gn_g", "ret_gn_g"), ("gn_b", "ret_gn_b")):
        arrays[name] = a[src].reshape(-1)
    arrays["pos_col"] = a["positions_2"].reshape(TOK, P).T
    rows = [np.concatenate([a[n][l].reshape(-1) for n in
                            ("ln1_g_2", "ln1_b_2", "ln2_g_2", "ln2_b_2", "mla_q_norm_2", "mla_kv_norm_2", "mlstm_gate_bias_2",
                             "ssd_dt_bias_2", "ssd_a_log_2", "ssd_d_2", "ssd_norm_2", "mlstm_norm_2", "router_group_b_2",
                             "router_expert_b_2")]) for l in range(LAYERS)]
    arrays["rows2"] = np.stack(rows)
    conv = [np.concatenate([a["ssd_conv_w_2"][l].T.reshape(XBC_CH, P, CONV).transpose(1, 0, 2).reshape(P, -1),
                            a["ssd_conv_b_2"][l].reshape(XBC_CH, P).T], axis=1) for l in range(LAYERS)]
    arrays["conv_col"] = np.stack(conv)
    arrays = {n: np.ascontiguousarray(v) for n, v in arrays.items()}

    nc = bacc.Bacc("TRN2", target_bir_lowering=False, num_devices=1)
    A = {n: nc.dram_tensor(n, v.shape, mybir.dt.from_np(v.dtype), kind="ExternalInput").ap() for n, v in arrays.items()}
    A["rel_scratch"] = nc.dram_tensor("rel_scratch", (N_AH, P + 1, NT), F32, kind="Internal").ap()
    A["out"] = nc.dram_tensor("out", a["x"].shape, F32, kind="ExternalOutput").ap()
    program(nc, A)
    r = run_bass_kernel_spmd(nc, [arrays], core_ids=[0])
    return r.results[0]["out"]
```
